# Optimizing a Trainium2 kernel written in Bass

```python
import math
import jax, jax.numpy as jnp
from jax import lax
import numpy as np

D_MODEL = 1024
BATCH = 1
SEQ = 256
DEPTH = 1
DEC_BATCH = 8
DEC_SEQ = 4
PAST_LEN = 1024
PAGE_SIZE = 128

HEAD_DIM = 64
GDN_HEADS = 8
SB_HEADS = 8
GDN_WIDTH = GDN_HEADS * HEAD_DIM
SB_WIDTH = SB_HEADS * HEAD_DIM
MIX_WIDTH = GDN_WIDTH + SB_WIDTH
CONV_WIDTH = 4
CONV_DIM = 3 * GDN_WIDTH
GDN_CHUNK = 64
SB_BLOCK = 128
SB_BIAS_INIT = -8.0
IN_DIM = CONV_DIM + GDN_WIDTH + 2 * GDN_HEADS + 3 * SB_WIDTH
N_EXPERTS = 32
TOP_K = 4
D_FF = D_MODEL
MOE_BLOCK = 128
SWIGLU_LIMIT = 7.0
SWIGLU_ALPHA = 1.702
RMS_EPS = 1e-6
L2_EPS = 1e-6

kernel_name = 'hymba_gdn_stickbreaking_moe_step'

def rms_norm(x, w):
    xf = x.astype(jnp.float32)
    y = xf * lax.rsqrt(jnp.mean(xf * xf, axis=-1, keepdims=True) + RMS_EPS)
    return (y * w.astype(jnp.float32)).astype(x.dtype)

def l2_normalize(x):
    return x * lax.rsqrt(jnp.sum(x * x, axis=-1, keepdims=True) + L2_EPS)

def causal_short_conv(u, buf, conv_w):
    length = u.shape[1]
    full = jnp.concatenate([buf.astype(u.dtype), u], axis=1)
    out = sum(full[:, i:i + length] * conv_w[i] for i in range(CONV_WIDTH))
    return jax.nn.silu(out), full[:, -(CONV_WIDTH - 1):]

def gated_delta_chunked(q, k, v, g, beta, s0, chunk):
    b, l, h, _ = q.shape
    n = l // chunk

    def blocks(t):
        t = t.reshape((b, n, chunk, h) + t.shape[3:])
        return jnp.moveaxis(t, 1, 0).swapaxes(2, 3)

    qc, kc, vc, gc, bc = (blocks(t) for t in (q, k, v, g, beta))
    G = jnp.cumsum(gc, axis=-1)
    incl = jnp.tril(jnp.ones((chunk, chunk), bool))
    strict = jnp.tril(jnp.ones((chunk, chunk), bool), -1)
    diff = G[..., :, None] - G[..., None, :]
    decay = jnp.where(incl, jnp.exp(jnp.where(incl, diff, 0.0)), 0.0)
    kb = kc * bc[..., None]
    low = jnp.where(strict, jnp.einsum('nbhid,nbhjd->nbhij', kb, kc) * decay, 0.0)
    eye = jnp.eye(chunk, dtype=low.dtype)
    t_inv = lax.linalg.triangular_solve(eye + low, jnp.broadcast_to(eye, low.shape),
                                        left_side=True, lower=True)
    u = jnp.einsum('nbhij,nbhjd->nbhid', t_inv, vc * bc[..., None])
    w = jnp.einsum('nbhij,nbhjd->nbhid', t_inv, kb * jnp.exp(G)[..., None])
    qk = jnp.where(incl, jnp.einsum('nbhid,nbhjd->nbhij', qc, kc) * decay, 0.0)
    g_last = G[..., -1]
    k_tail = kc * jnp.exp(g_last[..., None] - G)[..., None]
    q_head = qc * jnp.exp(G)[..., None]

    def step(state, xs):
        u_c, w_c, qk_c, qh_c, kt_c, gl_c = xs
        v_new = u_c - jnp.einsum('bhcd,bhde->bhce', w_c, state)
        o = jnp.einsum('bhcd,bhde->bhce', qh_c, state) + jnp.einsum('bhij,bhje->bhie', qk_c, v_new)
        state = state * jnp.exp(gl_c)[..., None, None] + jnp.einsum('bhcd,bhce->bhde', kt_c, v_new)
        return state, o

    s_final, o = lax.scan(step, s0.astype(jnp.float32), (u, w, qk, q_head, k_tail, g_last))
    o = jnp.moveaxis(o.swapaxes(2, 3), 0, 1).reshape(b, l, h, -1)
    return o, s_final

def stick_breaking(q, k, v, past_len, bias):
    b, l, h, d = q.shape
    key_pos = jnp.arange(k.shape[1])
    blk = SB_BLOCK if l % SB_BLOCK == 0 else l
    nb = l // blk
    q_blocks = jnp.moveaxis(q.reshape(b, nb, blk, h, d), 1, 0)
    q_pos = past_len + jnp.arange(l).reshape(nb, blk)
    scale = 1.0 / math.sqrt(d)
    bias_f = bias.astype(jnp.float32)[None, :, None, None]

    def one_block(args):
        q_blk, pos = args
        z = jnp.einsum('bqhd,bkhd->bhqk', q_blk, k, preferred_element_type=jnp.float32) * scale + bias_f
        mask = key_pos[None, :] < pos[:, None]
        log_rem = jnp.where(mask, jax.nn.log_sigmoid(-z), 0.0)
        after = lax.cumsum(log_rem, axis=3, reverse=True) - log_rem
        a = jnp.where(mask, jnp.exp(jax.nn.log_sigmoid(z) + after), 0.0)
        return jnp.einsum('bhqk,bkhd->bqhd', a.astype(v.dtype), v)

    o = lax.map(one_block, (q_blocks, q_pos))
    return jnp.moveaxis(o, 0, 1).reshape(b, l, h, d)

def mixer_layer(h, conv_buf, s0, past_k, past_v, w_in, conv_w, a_log, dt_bias, gdn_norm, sb_bias, w_out):
    b, l, _ = h.shape
    proj = h @ w_in
    c1 = CONV_DIM
    c2 = c1 + GDN_WIDTH
    c3 = c2 + GDN_HEADS
    c4 = c3 + GDN_HEADS
    qkv_g, z_g, beta_in, a_in, qkv_s = jnp.split(proj, [c1, c2, c3, c4], axis=-1)
    conv_out, conv_new = causal_short_conv(qkv_g, conv_buf, conv_w)
    qg, kg, vg = (t.reshape(b, l, GDN_HEADS, HEAD_DIM).astype(jnp.float32)
                  for t in jnp.split(conv_out, 3, axis=-1))
    qg = l2_normalize(qg) * (HEAD_DIM ** -0.5)
    kg = l2_normalize(kg)
    beta = jax.nn.sigmoid(beta_in.astype(jnp.float32))
    g = -jnp.exp(a_log.astype(jnp.float32)) * jax.nn.softplus(a_in.astype(jnp.float32) + dt_bias.astype(jnp.float32))
    chunk = GDN_CHUNK if l % GDN_CHUNK == 0 else l
    o_g, s_new = gated_delta_chunked(qg, kg, vg, g, beta, s0, chunk)
    gate = jax.nn.silu(z_g.astype(jnp.float32)).reshape(b, l, GDN_HEADS, HEAD_DIM)
    o_g = (rms_norm(o_g, gdn_norm) * gate).reshape(b, l, GDN_WIDTH)
    qs, ks, vs = (t.reshape(b, l, SB_HEADS, HEAD_DIM) for t in jnp.split(qkv_s, 3, axis=-1))
    k_all = jnp.concatenate([past_k.astype(ks.dtype), ks], axis=1)
    v_all = jnp.concatenate([past_v.astype(vs.dtype), vs], axis=1)
    o_s = stick_breaking(qs, k_all, v_all, past_k.shape[1], sb_bias).reshape(b, l, SB_WIDTH)
    out = jnp.concatenate([o_g.astype(h.dtype), o_s.astype(h.dtype)], axis=-1) @ w_out
    return out, ks, vs, conv_new, s_new

def moe_ffn(h, router_w, router_b, w_up, b_up, w_down, b_down):
    shp = h.shape
    t = h.reshape(-1, shp[-1])
    n_tok = t.shape[0]
    logits = jnp.dot(t, router_w, preferred_element_type=jnp.float32) + router_b.astype(jnp.float32)
    top_v, top_i = lax.top_k(logits, TOP_K)
    gates = jax.nn.softmax(top_v, axis=-1)
    n_pairs = n_tok * TOP_K
    pair_e = top_i.reshape(-1)
    pair_tok = jnp.arange(n_pairs, dtype=jnp.int32) // TOP_K
    pair_w = gates.reshape(-1)
    order = jnp.argsort(pair_e)
    e_sorted = pair_e[order]
    counts = jnp.bincount(pair_e, length=N_EXPERTS)
    padded = (counts + MOE_BLOCK - 1) // MOE_BLOCK * MOE_BLOCK
    start = jnp.cumsum(counts) - counts
    ends_pad = jnp.cumsum(padded)
    start_pad = ends_pad - padded
    dest = start_pad[e_sorted] + jnp.arange(n_pairs) - start[e_sorted]
    n_slots = (-(-n_pairs // MOE_BLOCK) + N_EXPERTS) * MOE_BLOCK
    n_blocks = n_slots // MOE_BLOCK
    slot_tok = jnp.zeros((n_slots,), jnp.int32).at[dest].set(pair_tok[order])
    slot_w = jnp.zeros((n_slots,), jnp.float32).at[dest].set(pair_w[order])
    block_e = jnp.minimum(jnp.searchsorted(ends_pad, jnp.arange(n_blocks) * MOE_BLOCK, side='right'),
                          N_EXPERTS - 1)

    def expert_block(args):
        tok, e = args
        hu = t[tok] @ w_up[e] + b_up[e]
        gate = jnp.minimum(hu[:, ::2], SWIGLU_LIMIT)
        up = jnp.clip(hu[:, 1::2], -SWIGLU_LIMIT, SWIGLU_LIMIT)
        act = (up + 1.0) * gate * jax.nn.sigmoid(SWIGLU_ALPHA * gate)
        return act @ w_down[e] + b_down[e]

    out = lax.map(expert_block, (slot_tok.reshape(n_blocks, MOE_BLOCK), block_e))
    out = out.reshape(n_slots, -1).astype(jnp.float32) * slot_w[:, None]
    y = jax.ops.segment_sum(out, slot_tok, num_segments=n_tok)
    return y.reshape(shp).astype(h.dtype)

def setup_inputs(seed: int = 0) -> dict:
    key = jax.random.key(seed)
    ks = jax.random.split(key, 24)
    f32 = jnp.float32
    n_pages = PAST_LEN // PAGE_SIZE
    used = DEC_BATCH * n_pages
    n_pool = used + used // 4

    def nrm(k, shape, scale):
        return jax.random.normal(k, shape, f32) * scale

    x_prompt = nrm(ks[0], (BATCH, SEQ, D_MODEL), 1.0)
    x_sample = nrm(ks[1], (DEC_BATCH, DEC_SEQ, D_MODEL), 1.0)
    cache_k = nrm(ks[2], (DEPTH, n_pool, PAGE_SIZE, SB_HEADS, HEAD_DIM), 1.0)
    cache_v = nrm(ks[3], (DEPTH, n_pool, PAGE_SIZE, SB_HEADS, HEAD_DIM), 1.0)
    page_table = jax.random.permutation(ks[4], n_pool)[:used].reshape(DEC_BATCH, n_pages).astype(jnp.int32)
    state_conv = nrm(ks[5], (DEPTH, DEC_BATCH, CONV_WIDTH - 1, CONV_DIM), 1.0)
    state_ssm = nrm(ks[6], (DEPTH, DEC_BATCH, GDN_HEADS, HEAD_DIM, HEAD_DIM), 0.1)
    norm_mix = 1.0 + nrm(ks[7], (DEPTH, D_MODEL), 0.02)
    w_in = nrm(ks[8], (DEPTH, D_MODEL, IN_DIM), D_MODEL ** -0.5)
    conv_w = nrm(ks[9], (DEPTH, CONV_WIDTH, CONV_DIM), CONV_WIDTH ** -0.5)
    a_log = jnp.log(jax.random.uniform(ks[10], (DEPTH, GDN_HEADS), f32, 1.0, 16.0))
    dt_bias = jnp.log(jnp.expm1(jax.random.uniform(ks[11], (DEPTH, GDN_HEADS), f32, 0.001, 0.1)))
    gdn_norm = 1.0 + nrm(ks[12], (DEPTH, HEAD_DIM), 0.02)
    sb_bias = SB_BIAS_INIT + nrm(ks[22], (DEPTH, SB_HEADS), 0.1)
    w_out = nrm(ks[13], (DEPTH, MIX_WIDTH, D_MODEL), MIX_WIDTH ** -0.5)
    norm_ffn = 1.0 + nrm(ks[14], (DEPTH, D_MODEL), 0.02)
    router_w = nrm(ks[15], (DEPTH, D_MODEL, N_EXPERTS), D_MODEL ** -0.5)
    router_b = nrm(ks[16], (DEPTH, N_EXPERTS), 0.01)
    w_up = nrm(ks[17], (DEPTH, N_EXPERTS, D_MODEL, 2 * D_FF), D_MODEL ** -0.5)
    b_up = nrm(ks[18], (DEPTH, N_EXPERTS, 2 * D_FF), 0.01)
    w_down = nrm(ks[19], (DEPTH, N_EXPERTS, D_FF, D_MODEL), D_FF ** -0.5)
    b_down = nrm(ks[20], (DEPTH, N_EXPERTS, D_MODEL), 0.01)
    norm_final = 1.0 + nrm(ks[21], (D_MODEL,), 0.02)
    return {'x_prompt': x_prompt, 'x_sample': x_sample, 'cache_k': cache_k, 'cache_v': cache_v,
            'page_table': page_table, 'state_conv': state_conv, 'state_ssm': state_ssm,
            'norm_mix': norm_mix, 'w_in': w_in, 'conv_w': conv_w, 'a_log': a_log, 'dt_bias': dt_bias,
            'gdn_norm': gdn_norm, 'sb_bias': sb_bias, 'w_out': w_out, 'norm_ffn': norm_ffn,
            'router_w': router_w, 'router_b': router_b, 'w_up': w_up, 'b_up': b_up, 'w_down': w_down,
            'b_down': b_down, 'norm_final': norm_final}

def reference(x_prompt, x_sample, cache_k, cache_v, page_table, state_conv, state_ssm,
              norm_mix, w_in, conv_w, a_log, dt_bias, gdn_norm, sb_bias, w_out,
              norm_ffn, router_w, router_b, w_up, b_up, w_down, b_down, norm_final):
    xp, xs = x_prompt, x_sample
    bp, bs = xp.shape[0], xs.shape[0]
    k_p, v_p, c_p, s_p, k_s, v_s, c_s, s_s = ([] for _ in range(8))
    for l in range(DEPTH):
        mix = (w_in[l], conv_w[l], a_log[l], dt_bias[l], gdn_norm[l], sb_bias[l], w_out[l])
        ffn = (router_w[l], router_b[l], w_up[l], b_up[l], w_down[l], b_down[l])
        zero_conv = jnp.zeros((bp, CONV_WIDTH - 1, CONV_DIM), xp.dtype)
        zero_ssm = jnp.zeros((bp, GDN_HEADS, HEAD_DIM, HEAD_DIM), jnp.float32)
        no_past = jnp.zeros((bp, 0, SB_HEADS, HEAD_DIM), xp.dtype)
        out_p, kp, vp, cp, sp = mixer_layer(rms_norm(xp, norm_mix[l]), zero_conv, zero_ssm,
                                            no_past, no_past, *mix)
        xp = xp + out_p
        xp = xp + moe_ffn(rms_norm(xp, norm_ffn[l]), *ffn)
        past_k = cache_k[l][page_table].reshape(bs, -1, SB_HEADS, HEAD_DIM)
        past_v = cache_v[l][page_table].reshape(bs, -1, SB_HEADS, HEAD_DIM)
        out_s, ksn, vsn, csn, ssn = mixer_layer(rms_norm(xs, norm_mix[l]), state_conv[l], state_ssm[l],
                                                past_k, past_v, *mix)
        xs = xs + out_s
        xs = xs + moe_ffn(rms_norm(xs, norm_ffn[l]), *ffn)
        k_p.append(kp); v_p.append(vp); c_p.append(cp); s_p.append(sp)
        k_s.append(ksn); v_s.append(vsn); c_s.append(csn); s_s.append(ssn)
    y_prompt = rms_norm(xp, norm_final)
    y_sample = rms_norm(xs, norm_final)
    return (y_prompt, y_sample,
            jnp.stack(k_p), jnp.stack(v_p), jnp.stack(c_p), jnp.stack(s_p),
            jnp.stack(k_s), jnp.stack(v_s), jnp.stack(c_s), jnp.stack(s_s))


_drawn_inputs = setup_inputs


def setup_inputs(seed=0):
    import zlib

    import numpy as np

    out = dict(_drawn_inputs(seed))
    spreads = {}
    factors = {'sb_bias': 8.0, 'b_up': 8.0, 'b_down': 8.0, 'norm_final': 2.747}
    for name, (base, spread) in spreads.items():
        noise = np.random.default_rng([zlib.crc32(name.encode()), seed]).standard_normal(out[name].shape)
        drawn = base * np.exp(spread * noise) if base else spread * noise
        out[name] = __import__('jax').numpy.asarray(drawn.astype(out[name].dtype))
    for name, factor in factors.items():
        out[name] = (out[name] * factor).astype(out[name].dtype)
    return out
```

```python
from contextlib import ExitStack

import numpy as np
import concourse.bass as bass
from concourse import mybir

F32 = mybir.dt.float32
I32 = mybir.dt.int32
ALU = mybir.AluOpType
ACT = mybir.ActivationFunctionType
AX = mybir.AxisListType

P = 128
D = 1024
KD = D // P
HD = 64
NH = 8
HP = NH // 2
GW = NH * HD
CONV = 4
NSEQ, NDEC = 8, 4
ND = NSEQ * NDEC
SEQ = 256
T = SEQ + ND
ROWS = [P, P, ND]
TOK0 = [0, P, 2 * P]
PAGE, NPG = 128, 8
PAST = PAGE * NPG
POOL = 80
NE, TOPK, FF = 32, 4, 1024
CAP = 64
RBUF = 4096
RSLOT = 2048
NRB, NSLOT = 6, 12
BIG = 1.0e30
EPS = 1e-6
SCALE = HD ** -0.5
CONVD = 3 * GW
WORK = 15900
C_Z, C_BA, C_S = CONVD, CONVD + GW, CONVD + GW + 2 * NH


class Chain:

    def __init__(self, eng, sem):
        self.eng, self.sem, self.n, self.base = eng, sem, 0, 0

    def __call__(self, ins):
        self.n += 1
        ins.then_inc(self.sem, 1)
        self.eng.wait_ge(self.sem, self.base + self.n)


def build(nc, x_prompt, x_sample, cache_k, cache_v, page_table, state_conv, state_ssm, norm_mix, w_in, conv_w,
          a_log, dt_bias, gdn_norm, sb_bias, w_out, norm_ffn, router_w, router_b, w_up, b_up, w_down, b_down,
          norm_final, y_prompt, y_sample, k_prompt, v_prompt, conv_prompt, ssm_prompt, k_sample, v_sample,
          conv_sample, ssm_sample):
    ctx = ExitStack()
    with ctx:
        def sb(name, shape, dt=F32):
            return ctx.enter_context(nc.sbuf_tensor(name, shape, dt))

        def sem(name):
            return ctx.enter_context(nc.semaphore(name))

        bank = ctx.enter_context(nc.psum_tensor("bank", [P, 8, 512], F32))

        ring = sb("ring", [P, NSLOT * RSLOT])
        X = sb("X", [P, 3, D])
        wb = sb("wb", [P, D])
        hT = sb("hT", [P, KD, T])
        oT = sb("oT", [P, KD, T])
        ident = sb("ident", [P, P])
        ones = sb("ones", [P, P])
        stat = sb("stat", [P, 3, 4])
        epst = sb("epst", [P, 2])
        work = sb("work", [P, WORK])

        def at(off, shape, parts=P):
            n = int(np.prod(shape))
            v = work[0:parts, off:off + n]
            if len(shape) == 2:
                v = v.rearrange("p (a b) -> p a b", a=shape[0])
            elif len(shape) == 3:
                v = v.rearrange("p (a b c) -> p a b c", a=shape[0], b=shape[1])
            return v

        def rb(i):
            return ring[:, i * RBUF:(i + 1) * RBUF]

        def rows(t):
            return slice(0, ROWS[t])

        def toks(t):
            return slice(TOK0[t], TOK0[t] + ROWS[t])

        c0 = WORK
        def const(*shape):
            nonlocal c0
            c0 -= int(np.prod(shape))
            return at(c0, shape) if len(shape) > 1 else work[:, c0:c0 + shape[0]]

        Lst, Linc, Uinc = const(P), const(P), const(P)
        negS = const(P)
        LVL = const(7, P)
        blk64 = const(P)
        SM = const(ND)
        dLst, dLinc, dUinc, dneg = const(ND), const(ND), const(ND), const(ND)
        E = const(2, P)
        Sel = const(2, 16)
        headmask = const(512)
        sel8, hch = const(P), const(512)
        sbcol, sbb, sbrow, nsbrow, nsbb = const(1), const(NH), const(1), const(1), const(NH)
        alog, dtb = const(NH), const(NH)
        gnorm = const(HD)
        convw = const(12, CONV)
        scT = const(12, 24)
        pt = work[0:1, c0 - 64:c0].bitcast(I32)
        c0 -= 64
        CONST_END = c0

        qsT, ksT = at(0, (HP, T)), at(HP * T, (HP, T))
        A1 = 2 * HP * T
        vs_tok, z_tok = at(A1, (3, GW)), at(A1 + 3 * GW, (3, GW))
        A2 = A1 + 6 * GW
        ba = at(A2, (3, 2 * NH))
        A2 += 48

        s_x = sem("x_loaded")
        s_small = sem("small_loaded")
        s_wb = sem("norm_weight_loaded")
        s_pool = sem("pool_chain")
        s_act = sem("act_chain")
        s_dve = sem("dve_chain")
        s_pe = sem("pe_chain")
        s_ring = [sem(f"ring_loaded{i}") for i in range(NRB)]
        s_ringfree = sem("ring_used")
        s_ba_w = sem("ba_weights_loaded")
        wba = sb("wba", [P, KD, 2 * NH])
        scrow = work[0:24, 0:CONVD]
        cwrow = work[0:CONV, CONVD:2 * CONVD]

        w_in_v = w_in[0].rearrange("(k p) n -> p k n", p=P)
        w_out_v = w_out[0].rearrange("(k p) n -> p k n", p=P)
        GROUP_COL = [0, GW, 2 * GW, C_Z, C_S, C_S + GW, C_S + 2 * GW]
        ring_n = [0]

        def ring_buf(n):
            return (n + 5) % NRB

        def ring_wait(eng, n):
            return eng.wait_ge(s_ring[ring_buf(n)], 16 * NPG_OF(n))

        def NPG_OF(n):
            total = 0
            for m in range(n % NRB, n + 1, NRB):
                total += NPG if L_K0 <= m < L_WO else 1
            return total

        L_K0, L_WO = 7, 23

        def load_begin(eng, n):
            if n >= NRB:
                eng.wait_ge(s_ringfree, n - NRB + 1)

        act_n, dve_n, pool_n, pe_n = [0], [0], [0], [0]
        with nc.Block() as block:
            @block.sync
            def _(sp):
                sp.dma_start(X[:, 0:2, :], x_prompt[0].rearrange("(t p) d -> p t d", p=P)).then_inc(s_x, 16)
                sp.dma_start(X[0:ND, 2, :], x_sample.rearrange("s i d -> (s i) d")).then_inc(s_x, 16)
                sp.dma_start(wb[:], norm_mix[0].partition_broadcast(P)).then_inc(s_wb, 16)
                sp.dma_start(scrow, state_conv[0].rearrange("s w c -> (s w) c")).then_inc(s_small, 16)
                sp.dma_start(cwrow, conv_w[0]).then_inc(s_small, 16)
                sp.dma_start(sbcol[0:NH, :], sb_bias.rearrange("o h -> h o")).then_inc(s_small, 16)
                sp.dma_start(sbb, sb_bias[0].partition_broadcast(P)).then_inc(s_small, 16)
                sp.dma_start(alog, a_log[0].partition_broadcast(P)).then_inc(s_small, 16)
                sp.dma_start(dtb, dt_bias[0].partition_broadcast(P)).then_inc(s_small, 16)
                sp.dma_start(gnorm, gdn_norm[0].partition_broadcast(P)).then_inc(s_small, 16)
                sp.dma_start(pt, page_table.rearrange("(o s) n -> o (s n)", o=1)).then_inc(s_small, 16)
                sp.dma_start(wba[:], w_in_v[:, :, C_BA:C_BA + 2 * NH]).then_inc(s_ba_w, 16)
                for n in range(6):
                    g = GROUP_COL[n]
                    sp.dma_start(rb(ring_buf(n)).rearrange("p (k n) -> p k n", k=KD), w_in_v[:, :, g:g + GW])\
                      .then_inc(s_ring[ring_buf(n)], 16)
                sp.wait_ge(s_small, 128)
                sp.wait_ge(s_x, 32)

            @block.gpsimd
            def _(pool):
                c = Chain(pool, s_pool)

                def keep(v, pattern, cmp, base, cm, fill=0.0):
                    c(pool.affine_select(out=v, in_=v, pattern=pattern, compare_op=cmp, fill=fill, base=base,
                                         channel_multiplier=cm))

                c(pool.memset(ones[:], 1.0))
                c(pool.memset(ident[:], 0.0))
                keep(ident[:], [[-1, P]], ALU.not_equal, 0, 1, 1.0)
                c(pool.memset(epst[:, 0:1], EPS))
                c(pool.memset(epst[:, 1:2], HD * EPS))
                for m, v in ((Lst, 1.0), (Linc, 1.0), (Uinc, 1.0), (negS, 0.0)):
                    c(pool.memset(m, v))
                keep(Lst, [[-1, P]], ALU.is_gt, 0, 1)
                keep(Linc, [[-1, P]], ALU.is_ge, 0, 1)
                keep(Uinc, [[1, P]], ALU.is_ge, 0, -1)
                keep(negS, [[-1, P]], ALU.is_gt, 0, 1, -BIG)
                c(pool.memset(LVL, 0.0))
                for l in range(7):
                    b = 1 << l
                    nb = P // (2 * b)
                    v = LVL[:, l, :].rearrange("p (n h b) -> p n h b", h=2, b=b)[:, :, 0, :]
                    c(pool.memset(v, 1.0))
                    keep(v, [[-2 * b, nb], [0, b]], ALU.is_ge, -b, 1)
                    keep(v, [[2 * b, nb], [0, b]], ALU.is_ge, 2 * b - 1, -1)
                c(pool.memset(blk64, 0.0))
                c(pool.memset(blk64[0:HD, 0:HD], 1.0))
                c(pool.memset(blk64[HD:P, HD:P], 1.0))
                d = slice(0, ND)
                for m in (SM, dLst, dLinc, dUinc):
                    c(pool.memset(m[d, :], 1.0))
                    v = m[d, :].rearrange("p (s j) -> p s j", j=NDEC)
                    keep(v, [[-NDEC, NSEQ], [0, NDEC]], ALU.is_ge, 0, 1)
                    keep(v, [[NDEC, NSEQ], [0, NDEC]], ALU.is_ge, NDEC - 1, -1)
                keep(dLst[d, :], [[-1, ND]], ALU.is_gt, 0, 1)
                keep(dLinc[d, :], [[-1, ND]], ALU.is_ge, 0, 1)
                keep(dUinc[d, :], [[1, ND]], ALU.is_ge, 0, -1)
                c(pool.tensor_scalar(dneg[d, :], dLst[d, :], 1.0, BIG, ALU.subtract, ALU.mult))
                for g in range(2):
                    v = E[d, g, :].rearrange("p (s h i) -> p s h i", s=4, h=NH)
                    c(pool.memset(v, 0.0))
                    keep(v, [[NDEC, 4], [0, NH], [1, NDEC]], ALU.not_equal, 16 * g, -1, 1.0)
                c(pool.memset(sel8[0:NH, :], 0.0))
                keep(sel8[0:NH, :].rearrange("p (s h i) -> p s h i", s=4, h=NH), [[0, 4], [1, NH], [0, NDEC]],
                     ALU.not_equal, 0, -1, 1.0)
                c(pool.memset(hch[0:NH, :], 0.0))
                keep(hch[0:NH, :].rearrange("p (h c) -> p h c", c=HD), [[1, NH], [0, HD]], ALU.not_equal, 0, -1, 1.0)
                c(pool.memset(hT[:], 0.0))
                c(pool.memset(z_tok, 0.0))
                c(pool.memset(ba, 0.0))
                pool.wait_ge(s_small, 128)
                c(pool.tensor_scalar(nsbb, sbb, -1.0, None, ALU.mult))
                pool_n[0] = c.n

        with nc.Block() as block:
            s_t = sem("turned")

            @block.tensor
            def _(pe):
                for t in range(12):
                    pe.transpose(bank[:, 0, 24 * t:24 * t + 24], scrow[:, t * P:(t + 1) * P], ident[0:24, 0:24])
                    pe.transpose(bank[:, 1, CONV * t:CONV * (t + 1)], cwrow[:, t * P:(t + 1) * P], ident[0:CONV, 0:CONV])
                for g in range(2):
                    pe.transpose(bank[:, 2, 32 * g:32 * g + 32], E[0:ND, g, :], ident[0:ND, 0:ND])
                pe.matmul(bank[:, 3, :], sel8[0:NH, :], hch[0:NH, :], start=True, stop=True)
                pe.matmul(bank[:, 4, 0:1], sel8[0:NH, :], sbcol[0:NH, :], start=True, stop=True).then_inc(s_t, 1)

            @block.vector
            def _(dve):
                dve.wait_ge(s_t, 1)
                dve.tensor_copy(scT, bank[:, 0, 0:288].rearrange("p (a b) -> p a b", a=12))
                dve.tensor_copy(convw, bank[:, 1, 0:48].rearrange("p (a b) -> p a b", a=12))
                dve.tensor_copy(Sel[:, 0, :], bank[:, 2, 0:16])
                dve.tensor_copy(Sel[:, 1, :], bank[:, 2, 48:64])
                dve.tensor_copy(headmask, bank[:, 3, :])
                dve.tensor_copy(sbrow, bank[:, 4, 0:1])
                dve.tensor_scalar(nsbrow, bank[:, 4, 0:1], -1.0, None, ALU.mult)

        def norm(tag, rowbuf, weight_wait, turned):
            s_std, s_row, s_tp, s_ev = (sem(f"{tag}_{n}") for n in ("std", "rows", "turned", "copied"))
            with nc.Block() as block:
                @block.scalar
                def _(act):
                    c = Chain(act, s_act)
                    c.n = act_n[0]
                    for t in range(3):
                        r = rows(t)
                        c(act.activation(rowbuf(t), X[r, t, :], ACT.Square, accum_out=stat[r, t, 0:1]))
                        act.activation(stat[r, t, 1:2], stat[r, t, 0:1], ACT.Sqrt, scale=1.0 / D,
                                       bias=epst[r, 0:1]).then_inc(s_std, 1)
                    if turned:
                        for t in range(3):
                            act.wait_ge(s_tp, t + 1)
                            b = 2 * (t % 2)
                            n = ROWS[t]
                            act.activation(hT[:, :, toks(t)],
                                           bank[:, b:b + 2, :].rearrange("p b n -> p (b n)")[:, 0:KD * n]
                                           .rearrange("p (k n) -> p k n", k=KD), ACT.Copy).then_inc(s_ev, 1)
                    act_n[0] = c.n

                @block.vector
                def _(dve):
                    c = Chain(dve, s_dve)
                    c.n = dve_n[0]
                    weight_wait(dve)
                    for t in range(3):
                        r = rows(t)
                        dve.wait_ge(s_std, t + 1)
                        c(dve.reciprocal(stat[r, t, 2:3], stat[r, t, 1:2]))
                        dve.scalar_tensor_tensor(out=rowbuf(t), in0=X[r, t, :], scalar=stat[r, t, 2:3], in1=wb[r, :],
                                                 op0=ALU.mult, op1=ALU.mult).then_inc(s_row, 1)
                    dve_n[0] = c.n

                if turned:
                    @block.tensor
                    def _(pe):
                        for t in range(3):
                            pe.wait_ge(s_row, t + 1)
                            if t == 2:
                                pe.wait_ge(s_ev, 1)
                            b, n = 2 * (t % 2), ROWS[t]
                            dst = bank[:, b:b + 2, :].rearrange("p b n -> p (b n)")
                            for k in range(KD):
                                ins = pe.transpose(dst[:, k * n:(k + 1) * n], rowbuf(t)[:, k * P:(k + 1) * P],
                                                   ident[0:n, 0:n])
                            ins.then_inc(s_tp, 1)

        hrow = lambda t: work[rows(t), A2 + D * t:A2 + D * (t + 1)]
        norm("mixnorm", hrow, lambda e: e.wait_ge(s_wb, 16), True)

        B0 = A2
        pad = [work[:, B0 + 316 * i:B0 + 316 * i + 315] for i in range(2)]
        B1 = B0 + 632
        turnT = [work[:, B1 + T * i:B1 + T * (i + 1)] for i in range(2)]
        B2 = B1 + 2 * T
        csig = work[:, B2:B2 + 2 * T].rearrange("p (b n) -> p b n", b=2)
        B3 = B2 + 2 * T
        cdec, cpro = work[0:NSEQ * 7, B3:B3 + 512], work[0:3, B3 + 512:B3 + 1024]
        kst = at(B3 + 1024, (3, GW))
        gq = sb("gq", [P, 12, T])
        tiles = [("conv", j) for j in range(12)] + [("z", j) for j in range(4)] + \
                [("q", j) for j in range(4)] + [("k", j) for j in range(4)] + [("v", j) for j in range(4)] + [("ba", 0)]
        turned_tiles = [i for i, (kind, _) in enumerate(tiles) if kind in ("z", "k", "v", "ba")]
        s_pj, s_pje = sem("projected"), sem("projection_copied")
        s_tt, s_tte = sem("proj_turned"), sem("proj_turned_copied")
        s_cu, s_cue = sem("convstate_turned"), sem("convstate_copied")
        s_cv, s_sg, s_pb = sem("conv_summed"), sem("conv_sigmoid"), sem("conv_state_placed")
        s_cs = sem("conv_state_stored")
        s_kvout = sem("kv_stored")
        s_silu = sem("conv_silu")

        def padx(i):
            return pad[i % 2][:, 3:259], pad[i % 2][:, 259:315].rearrange("p (s w) -> p s w", w=7)

        with nc.Block() as block:
            @block.sync
            def _(sp):
                n = 6
                load_begin(sp, n)
                g = GROUP_COL[n]
                sp.dma_start(rb(ring_buf(n)).rearrange("p (k n) -> p k n", k=KD), w_in_v[:, :, g:g + GW])\
                  .then_inc(s_ring[ring_buf(n)], 16)
                for g in range(3):
                    sp.wait_ge(s_cue, 2 * g + 2)
                    cs = conv_sample[0].rearrange("s w c -> s w c")
                    for s in range(NSEQ):
                        sp.dma_start(cs[s, :, g * 512:(g + 1) * 512], cdec[7 * s + 4:7 * s + 7, :]).then_inc(s_cs, 16)
                    sp.dma_start(conv_prompt[0, 0][:, g * 512:(g + 1) * 512], cpro).then_inc(s_cs, 16)
                    sp.wait_ge(s_cs, 16 * 9 * (g + 1))
                i_k = [turned_tiles.index(tiles.index(("k", 3))), turned_tiles.index(tiles.index(("v", 3)))]
                for i, (src, dp, ds_) in zip(i_k, ((kst, k_prompt, k_sample), (vs_tok, v_prompt, v_sample))):
                    sp.wait_ge(s_tte, i + 1)
                    sp.dma_start(dp[0, 0].rearrange("(t p) h d -> p t (h d)", p=P), src[:, 0:2, :]).then_inc(s_kvout, 16)
                    sp.dma_start(ds_[0].rearrange("s i h d -> (s i) (h d)"), src[0:ND, 2, :]).then_inc(s_kvout, 16)
                sp.wait_ge(s_kvout, 64)

            @block.tensor
            def _(pe):
                done_turn = [0]

                def turn(i):
                    kind, j = tiles[i]
                    if kind == "conv":
                        pe.wait_ge(s_pje, i + 1)
                        if j % 4 == 0 and j:
                            pe.wait_ge(s_cue, 2 * (j // 4))
                        px, pd = padx(i)
                        pe.transpose(bank[0:3, 4, (j % 4) * P:(j % 4 + 1) * P], px[:, SEQ - 3:SEQ], ident[:])
                        pe.wait_ge(s_pb, max(1, i))
                        pe.transpose(bank[0:NSEQ * 7, 5, (j % 4) * P:(j % 4 + 1) * P], pad[i % 2][:, 259:315],
                                     ident[:]).then_inc(s_cu, 1)
                    elif i in turned_tiles:
                        pe.wait_ge(s_pje, i + 1)
                        m = done_turn[0]
                        done_turn[0] += 1
                        if m >= 2:
                            pe.wait_ge(s_tte, m - 1)
                        n = 2 * NH if kind == "ba" else P
                        src = ksT[:, j, :] if kind == "k" else turnT[m % 2]
                        for t in range(3):
                            ins = pe.transpose(bank[rows(t), 2 + m % 2, t * P:t * P + n], src[0:n, toks(t)],
                                               ident[0:n, 0:n])
                        ins.then_inc(s_tt, 1)

                for i, (kind, j) in enumerate(tiles):
                    if i >= 2:
                        pe.wait_ge(s_pje, i - 1)
                    n = i // 4
                    if kind == "ba":
                        pe.wait_ge(s_ba_w, 16)
                    elif i % 4 == 0:
                        ring_wait(pe, n)
                    m = 2 * NH if kind == "ba" else P
                    w = wba[:] if kind == "ba" else rb(ring_buf(n)).rearrange("p (k n) -> p k n", k=KD)[:, :, j % 4 * P:(j % 4 + 1) * P]
                    for k in range(KD):
                        ins = pe.matmul(bank[0:m, i % 2, 0:T], w[:, k, :], hT[:, k, :], start=k == 0, stop=k == KD - 1)
                    ins.then_inc(s_pj, 1)
                    if i % 4 == 3:
                        pe.wait_ge(s_pj, i + 1)
                        pe.sem_inc(s_ringfree, 1)
                    if i >= 1:
                        turn(i - 1)
                turn(len(tiles) - 1)

            @block.scalar
            def _(act):
                m = 0
                for i, (kind, j) in enumerate(tiles):
                    act.wait_ge(s_pj, i + 1)
                    src = bank[:, i % 2, 0:T]
                    if kind == "conv":
                        if i == 0:
                            act.wait_ge(s_pb, 1)
                        if i >= 2:
                            act.wait_ge(s_cv, i - 1)
                            act.wait_ge(s_cu, i - 1)
                        px, pd = padx(i)
                        act.activation(px, src[:, 0:SEQ], ACT.Copy)
                        act.activation(pd[:, :, 3:7], src[:, SEQ:T].rearrange("p (s i) -> p s i", i=NDEC),
                                       ACT.Copy).then_inc(s_pje, 1)
                        if j >= 1:
                            act.wait_ge(s_cv, i)
                            if i >= 3:
                                act.wait_ge(s_silu, i - 2)
                            act.activation(csig[:, (i - 1) % 2, :], gq[:, i - 1, :], ACT.Sigmoid).then_inc(s_sg, 1)
                        continue
                    if i == 12:
                        act.wait_ge(s_cv, 12)
                        act.wait_ge(s_silu, 10)
                        act.activation(csig[:, 1, :], gq[:, 11, :], ACT.Sigmoid).then_inc(s_sg, 1)
                    if kind == "q":
                        dst = qsT[:, j, :]
                    elif kind == "k":
                        dst = ksT[:, j, :]
                        m += 1
                    else:
                        if m >= 2:
                            act.wait_ge(s_tt, m - 1)
                        dst = turnT[m % 2]
                        m += 1
                    n = 2 * NH if kind == "ba" else P
                    act.activation(dst[0:n, :], src[0:n, :], ACT.Copy).then_inc(s_pje, 1)

            @block.gpsimd
            def _(pool):
                c = Chain(pool, s_pool)
                c.n = pool_n[0]
                for i in range(2):
                    c(pool.memset(pad[i][:, 0:3], 0.0))
                    c(pool.tensor_copy(padx(i)[1][:, :, 0:3], scT[:, i, :].rearrange("p (s w) -> p s w", w=3)))
                pool.memset(pad[0][:, 0:3], 0.0).then_inc(s_pb, 1)
                pool_n[0] = c.n
                for i in range(12):
                    if i >= 2:
                        pool.wait_ge(s_cv, i - 1)
                        pool.wait_ge(s_cu, i - 1)
                        pool.tensor_copy(padx(i)[1][:, :, 0:3], scT[:, i, :].rearrange("p (s w) -> p s w", w=3))\
                            .then_inc(s_pb, 1)
                    pool.wait_ge(s_sg, i + 1)
                    pool.tensor_tensor(gq[:, i, :], gq[:, i, :], csig[:, i % 2, :], ALU.mult).then_inc(s_silu, 1)

            @block.vector
            def _(dve):
                c = Chain(dve, s_dve)
                c.n = dve_n[0]
                state = {"m": 0}

                def conv(i):
                    dve.wait_ge(s_pje, i + 1)
                    dve.wait_ge(s_pb, max(1, i))
                    px, pd = pad[i % 2], padx(i)[1]
                    op, od = gq[:, i, 0:SEQ], gq[:, i, SEQ:T].rearrange("p (s i) -> p s i", i=NDEC)
                    for w in range(CONV):
                        sp_, sd = px[:, w:w + SEQ], pd[:, :, w:w + NDEC]
                        sc = convw[:, i, w:w + 1]
                        if w == 0:
                            dve.tensor_scalar(op, sp_, sc, None, ALU.mult)
                            c(dve.tensor_scalar(od, sd, sc, None, ALU.mult))
                        else:
                            dve.scalar_tensor_tensor(out=op, in0=sp_, scalar=sc, in1=op, op0=ALU.mult, op1=ALU.add)
                            ins = dve.scalar_tensor_tensor(out=od, in0=sd, scalar=sc, in1=od, op0=ALU.mult, op1=ALU.add)
                            if w < CONV - 1:
                                c(ins)
                            else:
                                ins.then_inc(s_cv, 1)

                def turned(i):
                    kind, j = tiles[i]
                    m = state["m"]
                    state["m"] += 1
                    dve.wait_ge(s_tt, m + 1)
                    n = 2 * NH if kind == "ba" else P
                    dst = {"z": z_tok, "k": kst, "v": vs_tok, "ba": ba}[kind]
                    src = bank[:, 2 + m % 2, 0:3 * P].rearrange("p (t n) -> p t n", t=3)
                    dve.tensor_copy(dst[:, 0:2, j * P:j * P + n], src[:, 0:2, 0:n])
                    dve.tensor_copy(dst[0:ND, 2, j * P:j * P + n], src[0:ND, 2, 0:n]).then_inc(s_tte, 1)

                for i, (kind, j) in enumerate(tiles):
                    if kind == "conv":
                        conv(i)
                        if j % 4 == 3:
                            dve.wait_ge(s_cu, j + 1)
                            if j > 3:
                                dve.wait_ge(s_cs, 16 * 9 * (j // 4))
                            dve.tensor_copy(cpro, bank[0:3, 4, :]).then_inc(s_cue, 1)
                            dve.tensor_copy(cdec, bank[0:NSEQ * 7, 5, :]).then_inc(s_cue, 1)
                    elif i in turned_tiles:
                        turned(i)
                dve_n[0] = c.n


        NPAIR, CH = NE // 2, 24
        s_w = [sem(f"expert_weights{i}") for i in range(NSLOT)]
        s_wused = sem("expert_chunk_used")

        def load_chunk(sp, j, ch):
            kp, e = (ch % 8) // 2, ch % 2
            src, col = (w_up, D * (ch // 8)) if ch < 16 else (w_down, 0)
            sp.dma_start(ring[:, (ch % NSLOT) * RSLOT:(ch % NSLOT + 1) * RSLOT].rearrange("p (k n) -> p k n", k=2),
                         src[0, bass.ds(2 * j + e, 1), 256 * kp:256 * kp + 256, col:col + D]
                         .rearrange("o (k p) n -> p (o k) n", p=P)).then_inc(s_w[ch % NSLOT], 16)


        G = 4
        NK = PAST + ND
        KT = [hT[:].rearrange("p k t -> p (k t)")[:, 0:RSLOT].rearrange("p (s h k) -> p s h k", s=G, h=HP),
              work[:, A2:A2 + RSLOT].rearrange("p (s h k) -> p s h k", s=G, h=HP)]
        AT = work[:, A2:A2 + PAST].rearrange("p (g r) -> p g r", g=NPG)
        D1 = A2 + RSLOT
        beta, incl, rem = work[:, D1:D1 + NK], work[:, D1 + NK:D1 + 2 * NK + 1], work[:, D1 + 2 * NK + 1:D1 + 3 * NK + 1]
        D2 = D1 + 3 * NK + 1
        ATn, qbd = work[0:ND, D2:D2 + P], at(D2 + P, (HP, NSEQ, 32))
        om = rem[:, 0:GW]
        assert D2 + P + HP * NSEQ * 32 <= CONST_END
        s_qbd, s_kt, s_kta, s_ktd, s_sc, s_new = (sem(n) for n in (
            "query_blocks", "keys_turned", "keys_copied_act", "keys_copied_dve", "scores_done", "new_scores"))
        s_beta, s_A, s_AT, s_ATe, s_av, s_om, s_oT, s_oTe = (sem(n) for n in (
            "betas", "weights_A", "A_turned", "A_copied", "values_summed", "own_heads", "heads_turned", "heads_copied"))

        with nc.Block() as block:
            @block.sync
            def _(sp):
                n = L_K0
                for g in range(2):
                    for cache in (cache_k, cache_v):
                        for s in range(G * g, G * g + G):
                            load_begin(sp, n)
                            for pg in range(NPG):
                                page = sp.value_load(pt[0:1, NPG * s + pg:NPG * s + pg + 1], min_val=0, max_val=POOL - 1)
                                sp.dma_start(rb(ring_buf(n))[:, pg * GW:(pg + 1) * GW],
                                             cache[0, bass.ds(page, 1)].rearrange("o p h d -> (o p) (h d)"))\
                                  .then_inc(s_ring[ring_buf(n)], 16)
                            n += 1
                for m in range(2):
                    load_begin(sp, n)
                    sp.dma_start(rb(ring_buf(n)).rearrange("p (k n) -> p k n", k=KD), w_out_v[:, :, m * 512:(m + 1) * 512])\
                      .then_inc(s_ring[ring_buf(n)], 16)
                    n += 1
                sp.wait_ge(s_ringfree, L_WO)
                for ch in range(8):
                    load_chunk(sp, 0, ch)

            @block.tensor
            def _(pe):
                def turn_keys(g, pg):
                    q = NPG * g + pg
                    if q >= 1:
                        pe.wait_ge(s_kta, q)
                        pe.wait_ge(s_ktd, q)
                    if g == 1 and pg == 0:
                        pe.wait_ge(s_ATe, 1)
                    for s in range(G):
                        n = L_K0 + 2 * G * g + s
                        if pg == 0:
                            ring_wait(pe, n)
                        for p in range(HP):
                            ins = pe.transpose(bank[:, 1 + s, p * P:(p + 1) * P],
                                               rb(ring_buf(n))[:, pg * GW + p * P:pg * GW + (p + 1) * P], ident[:])
                    ins.then_inc(s_kt, 1)

                def scores(g, pg):
                    q = NPG * g + pg
                    pe.wait_ge(s_kta, q + 1)
                    pe.wait_ge(s_ktd, q + 1)
                    if g == 1 and pg == 0:
                        pe.wait_ge(s_beta, 1)
                    c = (pg % 4) * PAGE
                    for p in range(HP):
                        for s in range(G):
                            ins = pe.matmul(bank[32 * s:32 * s + 32, 6 + pg // 4, c:c + PAGE], qbd[:, p, G * g + s, :],
                                            KT[q % 2][:, s, p, :], start=p == 0, stop=p == HP - 1)
                    ins.then_inc(s_sc, 1)

                pe.wait_ge(s_qbd, 1)
                for g in range(2):
                    if g == 1:
                        pe.wait_ge(s_oTe, 1)
                    for p in range(HP):
                        for s in range(G):
                            pe.matmul(bank[32 * s:32 * s + 32, 0, 0:ND], qbd[:, p, G * g + s, :], ksT[:, p, SEQ:T],
                                      start=p == 0, stop=False, skip_group_check=True)
                    pe.matmul(bank[:, 0, 0:ND], E[0:ND, g, :], dneg[0:ND, :], start=False, stop=True,
                              skip_group_check=True).then_inc(s_new, 1)
                    for pg in range(NPG):
                        turn_keys(g, pg)
                        if pg:
                            scores(g, pg - 1)
                    pe.wait_ge(s_kt, NPG * (g + 1))
                    pe.sem_inc(s_ringfree, G)
                    scores(g, NPG - 1)
                    pe.wait_ge(s_A, g + 1)
                    for pg in range(NPG):
                        pe.transpose(bank[:, 1 + pg // 4, (pg % 4) * P:(pg % 4 + 1) * P], beta[:, pg * PAGE:(pg + 1) * PAGE],
                                     ident[:])
                    pe.transpose(bank[0:ND, 3, 0:P], beta[:, PAST:NK], ident[:]).then_inc(s_AT, 1)
                    pe.wait_ge(s_ATe, g + 1)
                    if g == 1:
                        pe.wait_ge(s_om, 1)
                    for s in range(G):
                        ring_wait(pe, L_K0 + 2 * G * g + G + s)
                    for pg in range(NPG):
                        for s in range(G):
                            n = L_K0 + 2 * G * g + G + s
                            pe.matmul(bank[32 * s:32 * s + 32, 5, :], AT[:, pg, 32 * s:32 * s + 32],
                                      rb(ring_buf(n))[:, pg * GW:(pg + 1) * GW], start=pg == 0, stop=False)
                    for s in range(G):
                        ins = pe.matmul(bank[32 * s:32 * s + 32, 5, :], ATn[:, 32 * s:32 * s + 32], vs_tok[0:ND, 2, :],
                                        start=False, stop=True)
                    ins.then_inc(s_av, 1)
                    pe.wait_ge(s_av, g + 1)
                    pe.sem_inc(s_ringfree, G)
                    pe.wait_ge(s_om, g + 1)
                    for p in range(HP):
                        ins = pe.matmul(bank[:, 0, 64 + 16 * p:80 + 16 * p], om[:, p * P:(p + 1) * P], Sel[:, g, :],
                                        start=True, stop=True)
                    ins.then_inc(s_oT, 1)

            @block.scalar
            def _(act):
                for g in range(2):
                    for pg in range(NPG):
                        q = NPG * g + pg
                        act.wait_ge(s_kt, q + 1)
                        if q >= 2:
                            act.wait_ge(s_sc, q - 1)
                        if q == 9:
                            act.wait_ge(s_av, 1)
                        act.activation(KT[q % 2][:, 0:2, :, :].rearrange("p s h k -> p (s h k)"),
                                       bank[:, 1:3, :].rearrange("p b n -> p (b n)"), ACT.Copy).then_inc(s_kta, 1)
                    act.wait_ge(s_sc, NPG * (g + 1))
                    act.wait_ge(s_new, g + 1)
                    if g == 1:
                        act.wait_ge(s_AT, 1)
                        act.wait_ge(s_oT, 1)
                    z = bank[:, 6:8, :].rearrange("p b n -> p (b n)")
                    act.activation(rem[:, 0:PAST], z, ACT.Sigmoid, scale=-SCALE, bias=nsbrow)
                    act.activation(rem[:, PAST:NK], bank[:, 0, 0:ND], ACT.Sigmoid, scale=-SCALE, bias=nsbrow)
                    act.activation(beta[:, 0:PAST], z, ACT.Sigmoid, scale=SCALE, bias=sbrow)
                    act.activation(beta[:, PAST:NK], bank[:, 0, 0:ND], ACT.Sigmoid, scale=SCALE, bias=sbrow)\
                       .then_inc(s_beta, 1)
                    act.wait_ge(s_oT, g + 1)
                    act.activation(oT[:, HP:KD, SEQ + 16 * g:SEQ + 16 * g + 16],
                                   bank[:, 0, 64:128].rearrange("p (h c) -> p h c", h=HP), ACT.Copy).then_inc(s_oTe, 1)

            @block.vector
            def _(dve):
                c = Chain(dve, s_dve)
                c.n = dve_n[0]
                c(dve.memset(qbd, 0.0))
                dve.memset(incl[:, NK:NK + 1], 1.0)
                for p in range(HP):
                    for half in range(2):
                        r, col = slice(HD * half, HD * half + HD), NDEC * (2 * p + half)
                        ins = dve.tensor_copy(qbd[r, p, :, col:col + NDEC],
                                              qsT[r, p, SEQ:T].rearrange("p (s i) -> p s i", i=NDEC))
                c(ins)
                dve.memset(incl[:, NK:NK + 1], 1.0).then_inc(s_qbd, 1)
                for g in range(2):
                    for pg in range(NPG):
                        q = NPG * g + pg
                        dve.wait_ge(s_kt, q + 1)
                        if q >= 2:
                            dve.wait_ge(s_sc, q - 1)
                        if q == 9:
                            dve.wait_ge(s_av, 1)
                        dve.tensor_copy(KT[q % 2][:, 2:4, :, :].rearrange("p s h k -> p (s h k)"),
                                        bank[:, 3:5, :].rearrange("p b n -> p (b n)")).then_inc(s_ktd, 1)
                    dve.wait_ge(s_beta, g + 1)
                    c(dve.tensor_tensor_scan(incl[:, 0:NK][:, ::-1], rem[:, ::-1], rem[:, ::-1], 1.0, ALU.mult, ALU.bypass))
                    dve.tensor_tensor(beta, beta, incl[:, 1:NK + 1], ALU.mult).then_inc(s_A, 1)
                    dve.wait_ge(s_AT, g + 1)
                    dve.wait_ge(s_sc, NPG * (g + 1))
                    dve.tensor_copy(AT.rearrange("p g r -> p (g r)"), bank[:, 1:3, :].rearrange("p b n -> p (b n)"))
                    dve.tensor_copy(ATn, bank[0:ND, 3, 0:P]).then_inc(s_ATe, 1)
                    dve.wait_ge(s_av, g + 1)
                    dve.tensor_tensor(om, bank[:, 5, :], headmask, ALU.mult).then_inc(s_om, 1)
                dve_n[0] = c.n

        W3 = 3 * P
        pbeta = [work[:, A2 + W3 * i:A2 + W3 * (i + 1)] for i in range(2)]
        prem = [work[:, A2 + W3 * (2 + i):A2 + W3 * (3 + i)] for i in range(2)]
        D3 = A2 + 4 * W3
        pincl = [work[:, D3 + 386 * i:D3 + 386 * (i + 1)] for i in range(2)]
        D4 = D3 + 772
        pAT = [work[:, D4 + W3 * i:D4 + W3 * (i + 1)] for i in range(2)]
        assert D4 + 2 * W3 <= CONST_END
        s_pz, s_pbeta, s_pA, s_pAT, s_pATe, s_po, s_poe = (sem(n) for n in (
            "prompt_scores", "prompt_betas", "prompt_A", "prompt_A_turned", "prompt_A_copied", "prompt_heads",
            "prompt_heads_copied"))
        with nc.Block() as block:
            @block.tensor
            def _(pe):
                def scores(h):
                    p, r = h // 2, slice(HD * (h % 2), HD * (h % 2) + HD)
                    if h >= 2:
                        pe.wait_ge(s_pbeta, h - 1)
                    z = bank[:, h % 2, :]
                    pe.matmul(z[:, 0:P], qsT[r, p, 0:P], ksT[r, p, 0:P], start=True, stop=False, skip_group_check=True)
                    pe.matmul(z[:, 0:P], ident[:], negS, start=False, stop=True, skip_group_check=True)
                    pe.matmul(z[:, P:W3], qsT[r, p, P:SEQ], ksT[r, p, 0:SEQ], start=True, stop=False, skip_group_check=True)
                    pe.matmul(z[:, 2 * P:W3], ident[:], negS, start=False, stop=True, skip_group_check=True)\
                      .then_inc(s_pz, 1)

                def turn(h):
                    pe.wait_ge(s_pA, h + 1)
                    if h >= 2:
                        pe.wait_ge(s_pATe, h - 1)
                    for b in range(3):
                        ins = pe.transpose(bank[:, 2 + h % 2, b * P:(b + 1) * P], pbeta[h % 2][:, b * P:(b + 1) * P], ident[:])
                    ins.then_inc(s_pAT, 1)

                def values(h):
                    pe.wait_ge(s_pATe, h + 1)
                    if h >= 4 and h % 2 == 0:
                        pe.wait_ge(s_poe, h // 2 - 1)
                    r = slice(HD * (h % 2), HD * (h % 2) + HD)
                    o = bank[r, 4 + (h // 2) % 2, :]
                    a = pAT[h % 2]
                    hc = slice(HD * h, HD * h + HD)
                    pe.matmul(o[:, 0:P], vs_tok[:, 0, hc], a[:, 0:P], start=True, stop=True)
                    pe.matmul(o[:, P:SEQ], vs_tok[:, 0, hc], a[:, P:2 * P], start=True, stop=False)
                    pe.matmul(o[:, P:SEQ], vs_tok[:, 1, hc], a[:, 2 * P:W3], start=False, stop=True).then_inc(s_po, 1)

                scores(0)
                for h in range(NH):
                    if h + 1 < NH:
                        scores(h + 1)
                    turn(h)
                    if h:
                        values(h - 1)
                values(NH - 1)

            @block.scalar
            def _(act):
                for h in range(NH):
                    act.wait_ge(s_pz, h + 1)
                    if h >= 2:
                        act.wait_ge(s_pAT, h - 1)
                    act.activation(prem[h % 2], bank[:, h % 2, 0:W3], ACT.Sigmoid, scale=-SCALE, bias=nsbb[:, h:h + 1])
                    act.activation(pbeta[h % 2], bank[:, h % 2, 0:W3], ACT.Sigmoid, scale=SCALE, bias=sbb[:, h:h + 1])\
                       .then_inc(s_pbeta, 1)
                    if h >= 1:
                        act.wait_ge(s_pAT, h)
                        if h >= 3:
                            act.wait_ge(s_po, h - 2)
                        act.activation(pAT[(h - 1) % 2], bank[:, 2 + (h - 1) % 2, 0:W3], ACT.Copy).then_inc(s_pATe, 1)
                act.wait_ge(s_pAT, NH)
                act.wait_ge(s_po, NH - 2)
                act.activation(pAT[(NH - 1) % 2], bank[:, 2 + (NH - 1) % 2, 0:W3], ACT.Copy).then_inc(s_pATe, 1)

            def copy_heads(dve, p):
                dve.wait_ge(s_po, 2 * p + 2)
                dve.tensor_copy(oT[:, HP + p, 0:SEQ], bank[:, 4 + p % 2, 0:SEQ]).then_inc(s_poe, 1)

            @block.vector
            def _(dve):
                c = Chain(dve, s_dve)
                c.n = dve_n[0]
                for i in range(2):
                    for col in (P, 385):
                        ins = dve.memset(pincl[i][:, col:col + 1], 1.0)
                c(ins)
                for h in range(NH):
                    dve.wait_ge(s_pbeta, h + 1)
                    b, m, i = pbeta[h % 2], prem[h % 2], pincl[h % 2]
                    dve.tensor_tensor_scan(i[:, 0:P][:, ::-1], m[:, 0:P][:, ::-1], m[:, 0:P][:, ::-1], 1.0, ALU.mult, ALU.bypass)
                    c(dve.tensor_tensor_scan(i[:, 129:385][:, ::-1], m[:, P:W3][:, ::-1], m[:, P:W3][:, ::-1], 1.0, ALU.mult,
                                             ALU.bypass))
                    dve.tensor_tensor(b[:, 0:P], b[:, 0:P], i[:, 1:P + 1], ALU.mult)
                    dve.tensor_tensor(b[:, P:W3], b[:, P:W3], i[:, 130:386], ALU.mult).then_inc(s_pA, 1)
                    if h % 2 == 1:
                        if h >= 3:
                            copy_heads(dve, h // 2 - 1)
                copy_heads(dve, HP - 1)
                dve_n[0] = c.n

        sq = work[:, A2:A2 + 8 * T].rearrange("p (a t) -> p a t", a=8)
        rt = work[:, A2 + 8 * T:A2 + 16 * T].rearrange("p (a t) -> p a t", a=8)
        S1 = 3328
        bet, gg, xa, ax = (at(S1 + 24 * i, (3, NH)) for i in range(4))
        ea = work[:, S1 + 96:S1 + 104]
        s_sq, s_ss, s_rt = sem("squares"), sem("square_sums"), sem("roots")
        s_ea, s_ax, s_ex = sem("decay_rates"), sem("abs_a"), sem("log1p_a")
        with nc.Block() as block:
            @block.vector
            def _(dve):
                c = Chain(dve, s_dve)
                c.n = dve_n[0]
                for i in range(2):
                    dve.tensor_tensor(sq[:, 4 * i:4 * i + 4, :], gq[:, 4 * i:4 * i + 4, :], gq[:, 4 * i:4 * i + 4, :],
                                      ALU.mult).then_inc(s_sq, 1)
                c(dve.tensor_tensor(xa, ba[:, :, NH:2 * NH], dtb.unsqueeze(1).to_broadcast([P, 3, NH]), ALU.add))
                dve.scalar_tensor_tensor(out=ax, in0=xa, scalar=-1.0, in1=xa, op0=ALU.mult, op1=ALU.min).then_inc(s_ax, 1)
                dve.wait_ge(s_ex, 1)
                c(dve.scalar_tensor_tensor(out=gg, in0=xa, scalar=0.0, in1=ax, op0=ALU.max, op1=ALU.add))
                c(dve.scalar_tensor_tensor(out=gg, in0=gg, scalar=-1.0, in1=ea.unsqueeze(1).to_broadcast([P, 3, NH]),
                                           op0=ALU.mult, op1=ALU.mult))
                for i in range(2):
                    q = slice(4 * i, 4 * i + 4)
                    dve.wait_ge(s_rt, i + 1)
                    c(dve.reciprocal(rt[:, q, :], rt[:, q, :]))
                    c(dve.tensor_tensor(gq[:, q, :], gq[:, q, :], rt[:, q, :], ALU.mult))
                dve_n[0] = c.n

            @block.tensor
            def _(pe):
                for i in range(8):
                    pe.wait_ge(s_sq, i // 4 + 1)
                    pe.matmul(bank[:, i, 0:T], blk64, sq[:, i, :], start=True, stop=True).then_inc(s_ss, 1)

            @block.scalar
            def _(act):
                c = Chain(act, s_act)
                c.n = act_n[0]
                act.activation(bet, ba[:, :, 0:NH], ACT.Sigmoid)
                act.activation(ea, alog, ACT.Exp)
                act.wait_ge(s_ax, 1)
                c(act.activation(ax, ax, ACT.Exp))
                act.activation(ax, ax, ACT.Ln, bias=ones[:, 0:1]).then_inc(s_ex, 1)
                for i, sc in ((0, float(HD)), (1, 1.0)):
                    act.wait_ge(s_ss, 4 * i + 4)
                    act.activation(rt[:, 4 * i:4 * i + 4, :], bank[:, 4 * i:4 * i + 4, 0:T], ACT.Sqrt, scale=sc,
                                   bias=epst[:, 1 - i:2 - i]).then_inc(s_rt, 1)
                act_n[0] = c.n

        kbg, vb, ktail, vn, ob, wTb = (work[:, 512 * i:512 * (i + 1)] for i in range(6))
        St = at(3072, (HP, HD))
        Gs, eG, eL, eT, bG, ss, rs = (work[:, S1 + 104 + 16 * i:S1 + 120 + 16 * i] for i in range(7))
        eLs = work[:, S1 + 216:S1 + 220]
        s_ssm = sem("ssm_stored")
        s_s0 = sem("ssm_loaded")

        N = {k: sem(f"gdn_{k}") for k in (
            "gU", "G", "Gs", "R", "kv", "kvused", "kk", "qk", "tD", "dec", "exp", "decm", "L", "QK", "lm", "T0", "TTp",
            "TT", "Y", "Ye", "P", "Tn", "wu", "wTe", "vn", "qs", "o2", "S", "ss", "std", "oT", "sz", "ws", "vmr", "St")}

        def gdn_steps(k, ci):
            if k in ("lm", "Y", "Ye", "P", "Tn"):
                return 2 if ci == 2 else 12
            return {"Gs": (2, 2, 3), "dec": (2, 2, 2), "exp": (3, 3, 3), "decm": (2, 2, 2), "L": (2, 2, 2), "qs": (0, 1, 1),
                    "S": (1, 1, 2), "std": (2, 2, 2), "ws": (0, 0, 2), "vmr": (0, 0, 2)}.get(k, (1, 1, 1))[ci]

        def gdn_chunk(ci):
            n = ROWS[ci]
            R, dec = slice(0, n), ci == 2
            W = NH * n
            stp = W if dec else 1024
            Lb, Lm, Tb, TT, Y, QK = (work[R, A2 + stp * i:A2 + stp * i + W] for i in range(6))
            D0 = A2 + 6 * stp
            sz = work[R, D0:D0 + GW]
            if not dec:
                assert D0 + GW <= CONST_END
                D0 = A2
            S0 = at(D0 + 512, (NSEQ, HP, HD))
            vm = work[0:ND, D0 + 2560:D0 + 4608]
            WQ = work[:, D0 + 4608:D0 + 4864].rearrange("p (h s c) -> p h s c", h=HP, s=NSEQ)
            W1, Q1 = (work[:, D0 + 4864 + P * i:D0 + 4864 + P * (i + 1)] for i in range(2))
            gm, eGb, eGls = work[0:ND, 3840 - 264:3840 - 200], work[:, 3840 - 200:3840 - 136], work[:, 3840 - 136:3840 - 104]
            mU, mI, mS, mAll = (dUinc[R], dLinc[R], dLst[R], SM[R]) if dec else (Uinc, Linc, Lst, ones[:])
            hv = lambda v: v.rearrange("p (h i) -> p h i", h=NH)
            bc = lambda m, w: m.unsqueeze(1).to_broadcast([n, NH, w])
            hb = lambda v, w: v.unsqueeze(2).to_broadcast([n, NH, w])
            pv = lambda v: v.rearrange("p (a h i) -> p a h i", a=2, h=HP)
            pb = lambda v: v.rearrange("p (h a) -> p a h", a=2).unsqueeze(3).to_broadcast([n, 2, HP, n])
            rg = lambda b: bank[R, b:b + 2, 0:HP * n]
            rgh = lambda b, h: bank[R, b + h % 2, (h // 2) * n:(h // 2 + 1) * n]
            two = lambda v: v.rearrange("p (a c) -> p a c", a=2)
            hs = lambda h: slice(((h % 2) * HP + h // 2) * n, ((h % 2) * HP + h // 2 + 1) * n)
            hc = lambda h: slice(HD * h, HD * h + HD)
            pr = lambda h: slice(HD * (h % 2), HD * (h % 2) + HD)
            half = lambda a: slice(4 * n * a, 4 * n * (a + 1))
            nlev = 2 if dec else 7
            C = lambda k: sum(gdn_steps(k, c) for c in range(ci))
            with nc.Block() as block:
                @block.sync
                def _(sp):
                    if dec:
                        for par in range(2):
                            for s in range(NSEQ):
                                sp.dma_start(S0[HD * par:HD * par + HD, s],
                                             state_ssm[0, s].rearrange("(p two) k v -> two k p v", two=2)[par]).then_inc(s_s0, 16)
                    if ci:
                        sp.wait_ge(N["St"], C("St") + 1)
                        for par in range(2):
                            if dec:
                                for s in range(NSEQ):
                                    sp.dma_start(ssm_sample[0, s].rearrange("(p two) k v -> two k p v", two=2)[par],
                                                 S0[HD * par:HD * par + HD, s]).then_inc(s_ssm, 16)
                            else:
                                sp.dma_start(ssm_prompt[0, 0].rearrange("(p two) k v -> two k p v", two=2)[par],
                                             St[HD * par:HD * par + HD]).then_inc(s_ssm, 16)
                        sp.wait_ge(s_ssm, 32 if ci == 1 else 32 + 256)

                @block.tensor
                def _(pe):
                    pe.matmul(bank[R, 6, 0:NH], mU, gg[R, ci, :], start=True, stop=True)
                    ins = pe.matmul(bank[R, 6, NH:2 * NH], mAll[:, 0:n], gg[R, ci, :], start=True, stop=True)
                    pe.wait_ge(N["gU"], C("gU") + 1)
                    if dec:
                        ins = pe.matmul(bank[:, 7, 0:64], ones[0:ND, :], gm, start=True, stop=True)
                    ins.then_inc(N["G"], 1)
                    for a in range(2):
                        ins = pe.matmul(bank[R, a, 0:HP * n], ones[R, 0:n], Lm[:, half(a)], start=True, stop=True)
                    ins.then_inc(N["R"], 1)
                    for h in range(NH):
                        k = gq[pr(h), 4 + h // 2, toks(ci)]
                        ins = pe.matmul(rgh(2, h), k, k, start=True, stop=True)
                    ins.then_inc(N["kk"], 1)
                    for h in range(NH):
                        ins = pe.matmul(rgh(4, h), gq[pr(h), 4 + h // 2, toks(ci)], gq[pr(h), h // 2, toks(ci)],
                                        start=True, stop=True)
                    ins.then_inc(N["qk"], 1)
                    pe.wait_ge(N["Gs"], C("Gs") + (2 if dec else 1))
                    for p in range(HP):
                        pe.transpose(bank[R, 6, p * P:(p + 1) * P], gq[:, 4 + p, toks(ci)], ident[:])
                        ins = pe.transpose(bank[R, 7, p * P:(p + 1) * P], gq[:, 8 + p, toks(ci)], ident[:])
                    ins.then_inc(N["kv"], 1)
                    pe.wait_ge(N["T0"], C("T0") + 1)
                    for h in range(NH):
                        ins = pe.transpose(rgh(0, h), Tb[:, hs(h)], ident[R, 0:n])
                    ins.then_inc(N["TTp"], 1)
                    pe.wait_ge(N["TT"], C("TT") + 1)
                    pe.wait_ge(N["kvused"], C("kvused") + 1)
                    pe.wait_ge(N["QK"], C("QK") + 1)
                    for l in range(1, nlev):
                        for a in range(2):
                            pe.wait_ge(N["lm"], C("lm") + 2 * (l - 1) + a + 1)
                            if l > 1:
                                pe.wait_ge(N["Tn"], C("Tn") + 2 * (l - 2) + a + 1)
                            for h in range(a, NH, 2):
                                ins = pe.matmul(rgh(2, h), Lm[:, hs(h)], TT[:, hs(h)], start=True, stop=True)
                            ins.then_inc(N["Y"], 1)
                        for a in range(2):
                            pe.wait_ge(N["Ye"], C("Ye") + 2 * (l - 1) + a + 1)
                            for h in range(a, NH, 2):
                                if l < nlev - 1:
                                    pe.matmul(rgh(4, h), Y[:, hs(h)], Tb[:, hs(h)], start=True, stop=True)
                                ins = pe.matmul(rgh(6, h), Tb[:, hs(h)], Y[:, hs(h)], start=True, stop=True)
                            ins.then_inc(N["P"], 1)
                    pe.wait_ge(N["Tn"], C("Tn") + 2 * (nlev - 1))
                    for h in range(NH):
                        pe.matmul(bank[pr(h), 0, (h // 2) * n:(h // 2 + 1) * n], kbg[R, hc(h)], TT[:, hs(h)],
                                  start=True, stop=True)
                    for h in range(NH):
                        ins = pe.matmul(bank[R, 1, hc(h)], TT[:, hs(h)], vb[R, hc(h)], start=True, stop=True)
                    ins.then_inc(N["wu"], 1)
                    if ci == 1:
                        pe.wait_ge(N["wTe"], C("wTe") + 1)
                        for h in range(NH):
                            pe.matmul(bank[R, 4 + h % 2, hc(h // 2)], wTb[pr(h), (h // 2) * n:(h // 2 + 1) * n], St[pr(h), h // 2, :],
                                      start=True, stop=True)
                        for h in range(NH):
                            ins = pe.matmul(bank[R, 6 + h % 2, hc(h // 2)], gq[pr(h), h // 2, toks(ci)], St[pr(h), h // 2, :],
                                            start=True, stop=True)
                        ins.then_inc(N["qs"], 1)
                    if dec:
                        pe.wait_ge(N["wTe"], C("wTe") + 1)
                        pe.wait_ge(s_s0, 256)
                        for s in range(NSEQ):
                            for h in range(NH):
                                o = 64 * (h // 2) + 8 * s
                                ins = pe.matmul(bank[pr(h), 4, o:o + 8], S0[pr(h), s, h // 2, :], WQ[pr(h), h // 2, s, :],
                                                start=True, stop=True)
                        ins.then_inc(N["ws"], 1)
                        pe.wait_ge(N["ws"], C("ws") + 2)
                        for p in range(HP):
                            pe.transpose(bank[R, 5, p * P:(p + 1) * P], W1[:, 32 * p:32 * p + 32], ident[:])
                            ins = pe.transpose(bank[R, 6, p * P:(p + 1) * P], Q1[:, 32 * p:32 * p + 32], ident[:])
                        ins.then_inc(N["qs"], 1)
                    pe.wait_ge(N["vn"], C("vn") + 1)
                    for h in range(NH):
                        ins = pe.matmul(bank[R, 2, hc(h)], QK[:, hs(h)], vn[R, hc(h)], start=True, stop=True)
                    ins.then_inc(N["o2"], 1)
                    if not dec:
                        for h in range(NH):
                            ins = pe.matmul(bank[pr(h), 3, hc(h // 2)], ktail[R, hc(h)], vn[R, hc(h)], start=True, stop=True)
                        ins.then_inc(N["S"], 1)
                    else:
                        for a in range(2):
                            pe.wait_ge(N["vmr"], C("vmr") + a + 1)
                            for h in range(4 * a, 4 * a + 4):
                                ins = pe.matmul(bank[pr(h), (3, 4, 5, 7)[h // 2], :], ktail[R, hc(h)],
                                                vm[:, 512 * (h % 4):512 * (h % 4 + 1)], start=True, stop=True)
                            ins.then_inc(N["S"], 1)
                    pe.wait_ge(N["std"], C("std") + 2)
                    for p in range(HP):
                        ins = pe.transpose(bank[:, 0, p * n:(p + 1) * n], ob[R, p * P:(p + 1) * P], ident[R, 0:n])
                    ins.then_inc(N["oT"], 1)

                @block.scalar
                def _(act):
                    act.activation(sz, z_tok[R, ci, :], ACT.Sigmoid).then_inc(N["sz"], 1)
                    act.wait_ge(N["Gs"], C("Gs") + (3 if dec else 2))
                    act.activation(eG[R, 0:NH], Gs[R, 0:NH], ACT.Exp)
                    act.activation(eL[R, 0:NH], Gs[R, NH:2 * NH], ACT.Exp)
                    if dec:
                        act.activation(eGb, eGb, ACT.Exp)
                    act.activation(eT[R, 0:NH], eT[R, 0:NH], ACT.Exp).then_inc(N["exp"], 1)
                    act.wait_ge(N["dec"], C("dec") + 1)
                    act.activation(QK, QK, ACT.Exp).then_inc(N["exp"], 1)
                    act.wait_ge(N["dec"], C("dec") + 2)
                    act.activation(Y, Y, ACT.Exp, scale=-1.0).then_inc(N["exp"], 1)
                    act.wait_ge(N["TTp"], C("TTp") + 1)
                    act.activation(two(TT), rg(0), ACT.Copy).then_inc(N["TT"], 1)
                    for l in range(1, nlev):
                        for a in range(2):
                            act.wait_ge(N["Y"], C("Y") + 2 * (l - 1) + a + 1)
                            if l == 1 and a == 0:
                                act.wait_ge(N["L"], C("L") + 2)
                            if l > 1:
                                act.wait_ge(N["P"], C("P") + 2 * (l - 2) + a + 1)
                            act.activation(Y[:, half(a)], bank[R, 2 + a, 0:HP * n], ACT.Copy).then_inc(N["Ye"], 1)
                    act.wait_ge(N["wu"], C("wu") + 1)
                    if dec:
                        act.activation(WQ[:, :, :, 0:4], bank[:, 0, 0:HP * n].rearrange("p (h s i) -> p h s i", h=HP, s=NSEQ),
                                       ACT.Copy)
                        act.activation(WQ[:, :, :, 4:8], gq[:, 0:HP, SEQ:T].rearrange("p h (s i) -> p h s i", s=NSEQ),
                                       ACT.Copy).then_inc(N["wTe"], 1)
                        act.wait_ge(N["ws"], C("ws") + 1)
                        v = bank[:, 4, 0:256].rearrange("p (h s c) -> p h s c", h=HP, s=NSEQ)
                        act.activation(W1.rearrange("p (h s i) -> p h s i", h=HP, s=NSEQ), v[:, :, :, 0:4], ACT.Copy)
                        act.activation(Q1.rearrange("p (h s i) -> p h s i", h=HP, s=NSEQ), v[:, :, :, 4:8], ACT.Copy)\
                           .then_inc(N["ws"], 1)
                    else:
                        act.activation(wTb, bank[:, 0, :], ACT.Copy).then_inc(N["wTe"], 1)
                    act.wait_ge(N["ss"], C("ss") + 1)
                    act.activation(rs[R, 0:NH], ss[R, 0:NH], ACT.Sqrt, scale=1.0 / HD, bias=epst[R, 0:1]).then_inc(N["std"], 1)
                    act.wait_ge(N["oT"], C("oT") + 1)
                    act.activation(oT[:, 0:HP, toks(ci)], bank[:, 0, 0:HP * n].rearrange("p (h i) -> p h i", h=HP), ACT.Copy)

                @block.gpsimd
                def _(pool):
                    c = Chain(pool, s_pool)
                    c.n = pool_n[0]
                    pool.wait_ge(N["tD"], C("tD") + 1)
                    pool.tensor_scalar(QK, Tb, 0.0, None, ALU.min).then_inc(N["dec"], 1)
                    pool.tensor_scalar(Y, Tb, 0.0, None, ALU.max).then_inc(N["dec"], 1)
                    pool.wait_ge(N["exp"], C("exp") + 2)
                    pool.tensor_tensor(hv(QK), hv(QK), bc(mU, n), ALU.mult).then_inc(N["decm"], 1)
                    pool.wait_ge(N["exp"], C("exp") + 3)
                    pool.tensor_tensor(hv(Y), hv(Y), bc(mS, n), ALU.mult).then_inc(N["decm"], 1)
                    pool.wait_ge(N["L"], C("L") + 2)
                    pool.wait_ge(N["R"], C("R") + 1)
                    c(pool.tensor_tensor(hv(Lm), hv(Lb), bc(LVL[R, 0, 0:n], n), ALU.mult))
                    pool.tensor_tensor(hv(Tb), bc(ident[R, 0:n], n), hv(Lm), ALU.subtract).then_inc(N["T0"], 1)
                    pool.wait_ge(N["T0"], C("T0") + 1)
                    for l in range(1, nlev):
                        for a in range(2):
                            if l > 1:
                                pool.wait_ge(N["Y"], C("Y") + 2 * (l - 2) + a + 1)
                            hh = slice(4 * a, 4 * a + 4)
                            pool.tensor_tensor(hv(Lm)[:, hh, :], hv(Lb)[:, hh, :],
                                               LVL[R, l, 0:n].unsqueeze(1).to_broadcast([n, 4, n]), ALU.mult)\
                                .then_inc(N["lm"], 1)
                    pool_n[0] = c.n

                @block.vector
                def _(dve):
                    c = Chain(dve, s_dve)
                    c.n = dve_n[0]
                    g = gg[R, ci, :]
                    if dec:
                        sm8 = SM[0:ND].rearrange("p (s j) -> p s j", j=NDEC)[:, :, 0]
                        dve.tensor_tensor(gm.rearrange("p (s h) -> p s h", s=NSEQ), g.unsqueeze(1).to_broadcast([ND, NSEQ, NH]),
                                          sm8.unsqueeze(2).to_broadcast([ND, NSEQ, NH]), ALU.mult)
                    dve.tensor_tensor(pv(Lm), mU.unsqueeze(1).unsqueeze(1).to_broadcast([n, 2, HP, n]), pb(g), ALU.mult).then_inc(N["gU"], 1)
                    dve.wait_ge(N["G"], C("G") + 1)
                    ins = dve.tensor_copy(Gs[R, :], bank[R, 6, 0:2 * NH])
                    if dec:
                        ins.then_inc(N["Gs"], 1)
                        ins = dve.tensor_copy(eGb, bank[:, 7, 0:64])
                    ins.then_inc(N["Gs"], 1)
                    dve.wait_ge(N["Gs"], C("Gs") + (2 if dec else 1))
                    dve.tensor_tensor(eT[R, 0:NH], Gs[R, NH:2 * NH], Gs[R, 0:NH], ALU.subtract).then_inc(N["Gs"], 1)
                    dve.wait_ge(N["R"], C("R") + 1)
                    dve.tensor_tensor(pv(Tb), rg(0).rearrange("p a (h i) -> p a h i", h=HP), pb(Gs[R, 0:NH]), ALU.subtract).then_inc(N["tD"], 1)
                    dve.wait_ge(N["exp"], C("exp") + 1)
                    c(dve.tensor_tensor(bG[R, 0:NH], bet[R, ci, :], eG[R, 0:NH], ALU.mult))
                    dve.wait_ge(N["kv"], C("kv") + 1)
                    hd = lambda v: v.rearrange("p (h d) -> p h d", h=NH)
                    dve.tensor_tensor(hd(kbg[R]), hd(bank[R, 6, :]), hb(bG[R, 0:NH], HD), ALU.mult)
                    dve.tensor_tensor(hd(ktail[R]), hd(bank[R, 6, :]), hb(eT[R, 0:NH], HD), ALU.mult)
                    dve.tensor_tensor(hd(vb[R]), hd(bank[R, 7, :]), hb(bet[R, ci, :], HD), ALU.mult).then_inc(N["kvused"], 1)
                    dve.wait_ge(N["kk"], C("kk") + 1)
                    dve.tensor_tensor(pv(Lb), rg(2).rearrange("p a (h i) -> p a h i", h=HP), pb(bet[R, ci, :]), ALU.mult).then_inc(N["L"], 1)
                    dve.wait_ge(N["L"], C("L") + 1)
                    dve.wait_ge(N["decm"], C("decm") + 2)
                    dve.tensor_tensor(Lb, Lb, Y, ALU.mult).then_inc(N["L"], 1)
                    dve.wait_ge(N["qk"], C("qk") + 1)
                    dve.tensor_tensor(two(QK), rg(4), two(QK), ALU.mult).then_inc(N["QK"], 1)
                    dve.wait_ge(N["T0"], C("T0") + 1)
                    dve.wait_ge(N["TT"], C("TT") + 1)
                    for l in range(1, nlev):
                        for a in range(2):
                            dve.wait_ge(N["P"], C("P") + 2 * (l - 1) + a + 1)
                            if l < nlev - 1:
                                dve.tensor_tensor(Tb[:, half(a)], Tb[:, half(a)], bank[R, 4 + a, 0:HP * n], ALU.subtract)
                            dve.tensor_tensor(TT[:, half(a)], TT[:, half(a)], bank[R, 6 + a, 0:HP * n], ALU.subtract)\
                               .then_inc(N["Tn"], 1)
                            if l < nlev - 1:
                                dve.wait_ge(N["Tn"], C("Tn") + 2 * (l - 1) + a + 1)
                    dve.wait_ge(N["wu"], C("wu") + 1)
                    if ci == 0:
                        dve.tensor_copy(vn[R], bank[R, 1, :]).then_inc(N["vn"], 1)
                    else:
                        c(dve.tensor_copy(vn[R], bank[R, 1, :]))
                        dve.wait_ge(N["qs"], C("qs") + 1)
                        if dec:
                            dve.tensor_tensor(vn[R], vn[R], bank[R, 5, :], ALU.subtract).then_inc(N["vn"], 1)
                            c(dve.tensor_tensor(hd(ob[R]), hd(bank[R, 6, :]), hb(eG[R, 0:NH], HD), ALU.mult))
                        else:
                            for a in range(2):
                                par = lambda v: v.rearrange("p (h a d) -> p a h d", a=2, d=HD)[:, a]
                                ph = lambda b: bank[R, b + a, 0:HP * HD].rearrange("p (h d) -> p h d", h=HP)
                                ins = dve.tensor_tensor(par(vn[R]), par(vn[R]), ph(4), ALU.subtract)
                                ins2 = dve.tensor_tensor(par(ob[R]), ph(6), eG[R, a:NH:2].unsqueeze(2)
                                                         .to_broadcast([n, HP, HD]), ALU.mult)
                                if a:
                                    ins.then_inc(N["vn"], 1)
                                    c(ins2)
                    if dec:
                        dve.wait_ge(N["vn"], C("vn") + 1)
                        for a in range(2):
                            if a:
                                dve.wait_ge(N["S"], C("S") + 1)
                            dve.tensor_tensor(vm.rearrange("p (h s d) -> p h s d", h=4, s=NSEQ),
                                              vn[R, 256 * a:256 * a + 256].rearrange("p (h d) -> p h d", h=4).unsqueeze(2)
                                              .to_broadcast([ND, 4, NSEQ, HD]),
                                              sm8.unsqueeze(1).unsqueeze(3).to_broadcast([ND, 4, NSEQ, HD]), ALU.mult)\
                               .then_inc(N["vmr"], 1)
                    dve.wait_ge(N["o2"], C("o2") + 1)
                    if ci == 0:
                        c(dve.tensor_copy(ob[R], bank[R, 2, :]))
                    else:
                        c(dve.tensor_tensor(ob[R], ob[R], bank[R, 2, :], ALU.add))
                    osq = Lb[:, 0:GW] if not dec else vm[:, 0:GW]
                    if dec:
                        dve.wait_ge(N["S"], C("S") + 2)
                    c(dve.tensor_tensor(osq, ob[R], ob[R], ALU.mult))
                    dve.tensor_reduce(ss[R, 0:NH], hd(osq), AX.X, ALU.add).then_inc(N["ss"], 1)
                    dve.wait_ge(N["sz"], C("sz") + 1)
                    c(dve.tensor_tensor(sz, z_tok[R, ci, :], sz, ALU.mult))
                    c(dve.tensor_tensor(hd(sz), hd(sz), gnorm[R].unsqueeze(1).to_broadcast([n, NH, HD]), ALU.mult))
                    dve.wait_ge(N["std"], C("std") + 1)
                    c(dve.reciprocal(rs[R, 0:NH], rs[R, 0:NH]))
                    c(dve.tensor_tensor(hd(ob[R]), hd(ob[R]), hb(rs[R, 0:NH], HD), ALU.mult))
                    dve.tensor_tensor(ob[R], ob[R], sz, ALU.mult).then_inc(N["std"], 1)
                    dve.wait_ge(N["S"], C("S") + (2 if dec else 1))
                    if ci == 0:
                        dve.tensor_copy(St, bank[:, 3, 0:256].rearrange("p (h d) -> p h d", h=HP)).then_inc(N["St"], 1)
                    elif ci == 1:
                        dve.tensor_copy(eLs[0:HD, :], eL[0:HD, 0:NH:2])
                        c(dve.tensor_copy(eLs[HD:P, :], eL[HD:P, 1:NH:2]))
                        c(dve.tensor_tensor(St, St, eLs.unsqueeze(2).to_broadcast([P, HP, HD]), ALU.mult))
                        dve.tensor_tensor(St, St, bank[:, 3, 0:256].rearrange("p (h d) -> p h d", h=HP), ALU.add)\
                           .then_inc(N["St"], 1)
                    else:
                        v = eGb.rearrange("p (s h) -> p s h", s=NSEQ)
                        e = eGls.rearrange("p (s h) -> p s h", s=NSEQ)
                        dve.tensor_copy(e[0:HD], v[0:HD, :, 0:NH:2])
                        c(dve.tensor_copy(e[HD:P], v[HD:P, :, 1:NH:2]))
                        c(dve.tensor_tensor(S0.rearrange("p s h d -> p (s h) d"), S0.rearrange("p s h d -> p (s h) d"),
                                            eGls.unsqueeze(2).to_broadcast([P, NSEQ * HP, HD]), ALU.mult))
                        for p in range(HP):
                            ins = dve.tensor_tensor(S0[:, :, p, :], S0[:, :, p, :],
                                                    bank[:, (3, 4, 5, 7)[p], :].rearrange("p (s d) -> p s d", s=NSEQ), ALU.add)
                        ins.then_inc(N["St"], 1)
                    dve_n[0] = c.n

        for ci in range(3):
            gdn_chunk(ci)
        h2 = gq[:].rearrange("p a t -> p (a t)")[:, 0:3 * D].rearrange("p (t d) -> p t d", t=3)
        tab = gq[:].rearrange("p a t -> p (a t)")[:, 3 * D:]
        rk, gt = (tab[:, 102 * i:102 * (i + 1)].rearrange("p (t e) -> p t e", t=3) for i in range(2))
        iota = tab[:, 204:268]
        curP, curR, curG = (tab[:, 268 + 6 * i:274 + 6 * i].rearrange("p (t e) -> p t e", t=3) for i in range(3))
        npass = sb("npass", [1, 1], I32)
        rw, rbias = at(0, (KD, NE)), work[:, 256:288]
        s_rw = sem("router_loaded")
        s_wo, s_wor = sem("mixer_out"), sem("residual_added")
        with nc.Block() as block:
            @block.sync
            def _(sp):
                sp.dma_start(wb[:], norm_ffn[0].partition_broadcast(P)).then_inc(s_wb, 16)
                sp.dma_start(rw, router_w[0].rearrange("(k p) e -> p k e", p=P)).then_inc(s_rw, 16)
                sp.dma_start(rbias, router_b[0].partition_broadcast(P)).then_inc(s_rw, 16)
                sp.wait_ge(s_ringfree, L_WO + 2)
                for ch in range(8, NSLOT):
                    load_chunk(sp, 0, ch)

            @block.gpsimd
            def _(pool):
                pool.memset(h2[:, 2, :], 0.0)
                pool.memset(gt, 0.0)
                pool.memset(rk, -1.0e6)
                pool.iota(work[:, 300:364].bitcast(I32), pattern=[[1, CAP]], base=0, channel_multiplier=0)

            @block.tensor
            def _(pe):
                ring_wait(pe, L_WO)
                ring_wait(pe, L_WO + 1)
                for m in range(2):
                    w = rb(ring_buf(L_WO + m)).rearrange("p (k n) -> p k n", k=KD)
                    for t in range(3):
                        for k in range(KD):
                            ins = pe.matmul(bank[rows(t), 3 * m + t, :], oT[:, k, toks(t)], w[:, k, :], start=k == 0,
                                            stop=k == KD - 1)
                        ins.then_inc(s_wo, 1)
                pe.wait_ge(s_wo, 6)
                pe.sem_inc(s_ringfree, 2)

            @block.vector
            def _(dve):
                for m in range(2):
                    for t in range(3):
                        dve.wait_ge(s_wo, 3 * m + t + 1)
                        x = X[rows(t), t, 512 * m:512 * (m + 1)]
                        dve.tensor_tensor(x, x, bank[rows(t), 3 * m + t, :], ALU.add).then_inc(s_wor, 1)

        norm("ffnnorm", lambda t: h2[rows(t), t, :], lambda e: e.wait_ge(s_wb, 32), True)

        lg, mk, ex, gtr, eq, ce = (at(400 + 96 * i, (3, NE)) for i in range(6))
        m8 = at(980, (3, 8))
        ng, nd, nm, gs, mc = (work[:, 1010 + 4 * i:1014 + 4 * i] for i in range(5))
        s_lg, s_nm, s_exp, s_mk, s_rank = (sem(n) for n in ("logits", "neg_top", "exps", "chosen", "ranks"))
        with nc.Block() as block:
            @block.tensor
            def _(pe):
                pe.wait_ge(s_rw, 32)
                for t in range(3):
                    for k in range(KD):
                        ins = pe.matmul(bank[rows(t), t, 0:NE], hT[:, k, toks(t)], rw[:, k, :], start=k == 0, stop=k == KD - 1)
                ins.then_inc(s_lg, 1)
                pe.wait_ge(s_mk, 1)
                for t in range(3):
                    for u in range(t):
                        pe.matmul(bank[rows(t), 3 + t, 0:NE], ones[:, rows(t)], mk[:, u, :], start=u == 0, stop=False)
                    pe.matmul(bank[rows(t), 3 + t, 0:NE], Uinc[rows(t), rows(t)], mk[rows(t), t, :], start=t == 0, stop=True)
                for t in range(3):
                    ins = pe.matmul(bank[:, 6, 0:NE], ones[rows(t), :], mk[rows(t), t, :], start=t == 0, stop=t == 2)
                ins.then_inc(s_rank, 1)

            @block.scalar
            def _(act):
                act.wait_ge(s_nm, 1)
                for t in range(3):
                    ins = act.activation(ex[rows(t), t, :], lg[rows(t), t, :], ACT.Exp, bias=nm[rows(t), t:t + 1])
                ins.then_inc(s_exp, 1)

            @block.vector
            def _(dve):
                c = Chain(dve, s_dve)
                c.n = dve_n[0]
                dve.tensor_copy(iota, work[:, 300:364].bitcast(I32))
                dve.wait_ge(s_rw, 32)
                dve.wait_ge(s_lg, 1)
                for t in range(3):
                    r = rows(t)
                    c(dve.tensor_tensor(lg[r, t, :], bank[r, t, 0:NE], rbias[r], ALU.add))
                    c(dve.max(m8[r, t, :], lg[r, t, :]))
                    ins = dve.tensor_scalar(nm[r, t:t + 1], m8[r, t, 0:1], -1.0, None, ALU.mult)
                ins.then_inc(s_nm, 1)
                for t in range(3):
                    r = rows(t)
                    v4 = m8[r, t, TOPK - 1:TOPK]
                    dve.tensor_scalar(eq[r, t, :], lg[r, t, :], v4, None, ALU.is_equal)
                    c(dve.tensor_scalar(gtr[r, t, :], lg[r, t, :], v4, None, ALU.is_gt))
                    dve.tensor_reduce(ng[r, t:t + 1], gtr[r, t, :], AX.X, ALU.add)
                    c(dve.tensor_tensor_scan(ce[r, t, :], eq[r, t, :], eq[r, t, :], 0.0, ALU.add, ALU.bypass))
                    c(dve.tensor_scalar(nd[r, t:t + 1], ng[r, t:t + 1], -1.0, float(TOPK), ALU.mult, ALU.add))
                    c(dve.scalar_tensor_tensor(out=mk[r, t, :], in0=ce[r, t, :], scalar=nd[r, t:t + 1], in1=eq[r, t, :],
                                               op0=ALU.is_le, op1=ALU.mult))
                    ins = dve.tensor_tensor(mk[r, t, :], mk[r, t, :], gtr[r, t, :], ALU.add)
                ins.then_inc(s_mk, 1)
                dve.wait_ge(s_mk, 1)
                dve.wait_ge(s_exp, 1)
                for t in range(3):
                    r = rows(t)
                    c(dve.tensor_tensor(ex[r, t, :], ex[r, t, :], mk[r, t, :], ALU.mult))
                    c(dve.tensor_reduce(gs[r, t:t + 1], ex[r, t, :], AX.X, ALU.add))
                    c(dve.reciprocal(gs[r, t:t + 1], gs[r, t:t + 1]))
                    c(dve.tensor_scalar(gt[r, t, 0:NE], ex[r, t, :], gs[r, t:t + 1], None, ALU.mult))
                dve.tensor_copy(gt[:, :, NE:NE + 2], gt[:, :, 0:2])
                dve.wait_ge(s_rank, 1)
                for t in range(3):
                    r = rows(t)
                    c(dve.scalar_tensor_tensor(out=rk[r, t, 0:NE], in0=bank[r, 3 + t, 0:NE], scalar=1.0e6, in1=mk[r, t, :],
                                               op0=ALU.add, op1=ALU.mult))
                    c(dve.tensor_scalar(rk[r, t, 0:NE], rk[r, t, 0:NE], -1000001.0, None, ALU.add))
                dve.tensor_scalar(rk[:, :, NE:NE + 2], rk[:, :, 0:2], -float(CAP), None, ALU.add)
                c(dve.tensor_reduce(mc[:, 0:1], bank[:, 6, 0:NE], AX.X, ALU.max))
                c(dve.memset(mc[:, 1:2], 1.0))
                for k in range(1, -(-T // CAP)):
                    c(dve.scalar_tensor_tensor(out=mc[:, 1:2], in0=mc[:, 0:1], scalar=float(k * CAP), in1=mc[:, 1:2],
                                               op0=ALU.is_gt, op1=ALU.add))
                dve.tensor_copy(npass[:], mc[0:1, 1:2])
                dve_n[0] = c.n

        o_ = 0
        def take(n, parts=P):
            nonlocal o_
            o_ += n
            return work[0:parts, o_ - n:o_]
        xs, gb, ub, sg, ab, oo = take(D), take(512), take(512), take(512), take(D), take(D)
        xT = take(D).rearrange("p (k s) -> p k s", k=KD)
        aT = take(D).rearrange("p (k s) -> p k s", k=KD)
        PGT, Pm, PG = take(3 * P), take(3 * P), take(3 * P)
        bu, bd = take(D, 4), take(D, 2)
        bsel = take(4 * CAP, 4).rearrange("p (r s) -> p r s", r=4)
        assert o_ <= CONST_END
        names = ("P", "PG", "gathered", "x_copied", "xT_turned", "xT_copied", "up", "gate_clamped", "sigmoid", "act",
                 "aT_turned", "aT_copied", "out", "out_copied_act", "out_copied_dve", "PG_turned", "PGT_copied", "y",
                 "y_added", "dve_links", "bu_loaded", "bd_loaded", "bu_used", "bd_used", "ready")
        M = {k: sem("moe_" + k) for k in names}
        K_DVE = 6

        def expert_loops(eng, body, after_pass=None):
            n = eng.value_load(npass[0:1, 0:1], min_val=1, max_val=-(-T // CAP))
            with eng.Fori(0, n) as p:
                with eng.Fori(0, NPAIR) as j:
                    body(p * NPAIR + j, j)
                if after_pass:
                    after_pass(p)
            return n

        with nc.Block() as block:
            @block.sync
            def _(sp):
                sp.dma_start(wb[:], norm_final.partition_broadcast(P)).then_inc(s_wb, 16)
                with sp.Fori(0, NPAIR - 1) as j:
                    for ch in range(12, CH):
                        sp.wait_ge(s_wused, CH * j + ch - 11)
                        load_chunk(sp, j, ch)
                    for ch in range(12):
                        sp.wait_ge(s_wused, CH * j + 12 + ch + 1)
                        load_chunk(sp, j + 1, ch)
                for ch in range(12, CH):
                    sp.wait_ge(s_wused, CH * (NPAIR - 1) + ch - 11)
                    load_chunk(sp, NPAIR - 1, ch)
                n = sp.value_load(npass[0:1, 0:1], min_val=1, max_val=-(-T // CAP))
                with sp.If(n > 1):
                    with sp.Fori(1, n) as p:
                        with sp.Fori(0, NPAIR) as j:
                            for ch in range(CH):
                                sp.wait_ge(s_wused, CH * (p * NPAIR + j) + ch - 11)
                                load_chunk(sp, j, ch)

            @block.gpsimd
            def _(pool):
                c = Chain(pool, s_pool)
                c.n = pool_n[0]
                c(pool.memset(bsel, 0.0))
                c(pool.affine_select(out=bsel, in_=bsel, pattern=[[1, 4], [0, CAP]], compare_op=ALU.not_equal, fill=1.0,
                                     base=0, channel_multiplier=-1))
                c(pool.memset(PGT, 0.0))
                pool.memset(oo, 0.0).then_inc(M["ready"], 1)
                pool_n[0] = c.n

                def body(i, j):
                    pool.wait_ge(M["bu_used"], i + 1)
                    pool.dma_start(bu, b_up[0, bass.ds(2 * j, 2), :].rearrange("e (h c) -> (e h) c", h=2))\
                        .then_inc(M["bu_loaded"], 16)
                    pool.wait_ge(M["bd_used"], i + 1)
                    pool.dma_start(bd, b_down[0, bass.ds(2 * j, 2), :]).then_inc(M["bd_loaded"], 16)
                expert_loops(pool, body)

            @block.tensor
            def _(pe):
                def gather(n):
                    pe.wait_ge(M["P"], n)
                    for t in range(3):
                        for m in range(2):
                            ins = pe.matmul(bank[:, 4 + m, :], Pm[:, t * P:(t + 1) * P], h2[:, t, 512 * m:512 * (m + 1)],
                                            start=t == 0, stop=t == 2)
                    ins.then_inc(M["gathered"], 1)

                def turn_x(n):
                    pe.wait_ge(M["x_copied"], n)
                    for k in range(KD):
                        ins = pe.transpose(bank[:, 7 - k // 4, (k % 4) * P:(k % 4 + 1) * P], xs[:, k * P:(k + 1) * P], ident[:])
                        if k % 4 == 3:
                            ins.then_inc(M["xT_turned"], 1)

                def combine(i):
                    pe.wait_ge(M["out_copied_act"], i + 1)
                    pe.wait_ge(M["out_copied_dve"], i + 1)
                    pe.wait_ge(M["PGT_copied"], i + 1)
                    for n in range(6):
                        t, m = n // 2, n % 2
                        if n >= 4:
                            pe.wait_ge(M["y_added"], 6 * i + n - 3)
                        pe.matmul(bank[rows(t), 4 + n % 4, :], PGT[:, t * P:t * P + ROWS[t]], oo[:, 512 * m:512 * (m + 1)],
                                  start=True, stop=True).then_inc(M["y"], 1)

                def products(i, b0, ch0, lhs, k0=0):
                    for kp in range(4):
                        for e in range(2):
                            ch = ch0 + 2 * kp + e
                            pe.wait_ge(s_w[ch % NSLOT], 32 * i + 16 * (ch // NSLOT + 1))
                        for kk in range(2):
                            k = 2 * kp + kk
                            for m in range(2):
                                for e in range(2):
                                    ch = ch0 + 2 * kp + e
                                    w = ring[:, (ch % NSLOT) * RSLOT + kk * D + 512 * m:(ch % NSLOT) * RSLOT + kk * D + 512 * (m + 1)]
                                    ins = pe.matmul(bank[CAP * e:CAP * e + CAP, b0 + m, :], lhs[:, k, CAP * e:CAP * e + CAP], w,
                                                    start=False, stop=k == KD - 1)
                                    if kk == 1 and m == 1:
                                        ins.then_inc(s_wused, 1)
                    return ins

                def up(i, half):
                    for m in range(2):
                        for e in range(2):
                            ins = pe.matmul(bank[CAP * e:CAP * e + CAP, 2 * half + m, :], bsel[0:4, 2 * e + half, :],
                                            bu[0:4, 512 * m:512 * (m + 1)], start=True, stop=False)
                    if half:
                        ins.then_inc(M["bu_used"], 1)
                    products(i, 2 * half, 8 * half, xT)

                def turn_act(i, half):
                    pe.wait_ge(M["act"], 2 * i + half + 1)
                    for k in range(4):
                        ins = pe.transpose(bank[:, 6, k * P:(k + 1) * P], ab[:, 512 * half + k * P:512 * half + (k + 1) * P], ident[:])
                    ins.then_inc(M["aT_turned"], 1)

                pe.sem_inc(M["bu_used"], 1)
                pe.sem_inc(M["bd_used"], 1)
                gather(1)
                turn_x(1)
                pe.wait_ge(M["ready"], 1)

                def body(i, j):
                    pe.wait_ge(M["bu_loaded"], 16 * i + 16)
                    pe.wait_ge(M["xT_copied"], 2 * i + 2)
                    up(i, 0)
                    combine(i)
                    up(i, 1)
                    pe.wait_ge(M["y_added"], 6 * i + 6)
                    turn_act(i, 0)
                    gather(i + 2)
                    pe.wait_ge(M["PG"], i + 1)
                    for t in range(3):
                        ins = pe.transpose(bank[:, 7, t * P:(t + 1) * P], PG[:, t * P:(t + 1) * P], ident[:])
                    ins.then_inc(M["PG_turned"], 1)
                    pe.wait_ge(M["aT_copied"], 2 * i + 1)
                    turn_act(i, 1)
                    pe.wait_ge(M["PGT_copied"], i + 2)
                    pe.wait_ge(M["aT_copied"], 2 * i + 2)
                    turn_x(i + 2)
                    pe.wait_ge(M["bd_loaded"], 16 * i + 16)
                    for m in range(2):
                        for e in range(2):
                            ins = pe.matmul(bank[CAP * e:CAP * e + CAP, 4 + m, :], bsel[0:2, e, :],
                                            bd[0:2, 512 * m:512 * (m + 1)], start=True, stop=False)
                    ins.then_inc(M["bd_used"], 1)
                    products(i, 4, 16, aT)
                n = expert_loops(pe, body)
                pe.wait_ge(M["xT_copied"], 2 * (n * NPAIR) + 2)
                combine(n * NPAIR)

            @block.scalar
            def _(act):
                def copy_x(n):
                    act.wait_ge(M["gathered"], n)
                    act.activation(xs, bank[:, 4:6, :].rearrange("p b n -> p (b n)"), ACT.Copy).then_inc(M["x_copied"], 1)

                def copy_xT(n):
                    for q in range(2):
                        act.wait_ge(M["xT_turned"], 2 * n - 1 + q)
                        act.activation(xT[:, 4 * q:4 * q + 4, :].rearrange("p k s -> p (k s)"), bank[:, 7 - q, :], ACT.Copy)\
                           .then_inc(M["xT_copied"], 1)

                act.sem_inc(M["out_copied_act"], 1)
                copy_x(1)
                copy_xT(1)

                def body(i, j):
                    def sigmoid(half):
                        act.wait_ge(M["gate_clamped"], 2 * i + half + 1)
                        act.activation(sg, gb, ACT.Sigmoid, scale=1.702).then_inc(M["sigmoid"], 1)

                    def copy_aT(half):
                        act.wait_ge(M["aT_turned"], 2 * i + half + 1)
                        act.activation(aT[:, 4 * half:4 * half + 4, :].rearrange("p k s -> p (k s)"), bank[:, 6, :], ACT.Copy)\
                           .then_inc(M["aT_copied"], 1)
                    sigmoid(0)
                    copy_aT(0)
                    sigmoid(1)
                    copy_x(i + 2)
                    copy_aT(1)
                    copy_xT(i + 2)
                    act.wait_ge(s_wused, CH * i + CH)
                    act.activation(oo[:, 0:512], bank[:, 4, :], ACT.Copy).then_inc(M["out_copied_act"], 1)
                expert_loops(act, body)

            @block.vector
            def _(dve):
                c = Chain(dve, M["dve_links"])

                def place(dst, cur, gate, col):
                    ins = dve.tensor_copy(cur, rk[:, :, bass.ds(col, 2)])
                    if gate is not None:
                        ins = dve.tensor_copy(gate, gt[:, :, bass.ds(col, 2)])
                    c(ins)
                    for t in range(3):
                        for e in range(2):
                            d = dst[:, t * P + CAP * e:t * P + CAP * e + CAP]
                            if gate is None:
                                ins = dve.tensor_scalar(d, iota, cur[:, t, e:e + 1], None, ALU.is_equal)
                            else:
                                ins = dve.tensor_scalar(d, iota, cur[:, t, e:e + 1], gate[:, t, e:e + 1], ALU.is_equal, ALU.mult)
                    return ins

                def add_y(i):
                    for n in range(6):
                        t, m = n // 2, n % 2
                        dve.wait_ge(M["y"], 6 * i + n + 1)
                        x = X[rows(t), t, 512 * m:512 * (m + 1)]
                        dve.tensor_tensor(x, x, bank[rows(t), 4 + n % 4, :], ALU.add).then_inc(M["y_added"], 1)

                place(Pm, curP, None, 0).then_inc(M["P"], 1)
                dve.sem_inc(M["out_copied_dve"], 1)
                dve.sem_inc(M["PGT_copied"], 1)
                n0 = c.n

                def body(i, j, p):
                    c.base, c.n = K_DVE * i + p + n0, 0
                    place(PG, curR, curG, 2 * j).then_inc(M["PG"], 1)
                    dve.wait_ge(M["gathered"], i + 1)
                    place(Pm, curP, None, 2 * j + 2).then_inc(M["P"], 1)

                    def activation(half):
                        dve.wait_ge(s_wused, CH * i + 8 * half + 8)
                        hu = bank[:, 2 * half:2 * half + 2, :].rearrange("p b (f two) -> p (b f) two", two=2)
                        dve.tensor_scalar(gb, hu[:, :, 0], 7.0, None, ALU.min).then_inc(M["gate_clamped"], 1)
                        c(dve.tensor_scalar(ub, hu[:, :, 1], 7.0, -7.0, ALU.min, ALU.max))
                        c(dve.scalar_tensor_tensor(out=ub, in0=ub, scalar=1.0, in1=gb, op0=ALU.add, op1=ALU.mult))
                        dve.wait_ge(M["sigmoid"], 2 * i + half + 1)
                        dve.tensor_tensor(ab[:, 512 * half:512 * (half + 1)], ub, sg, ALU.mult).then_inc(M["act"], 1)
                    activation(0)
                    add_y(i)
                    activation(1)
                    dve.wait_ge(M["PG_turned"], i + 1)
                    dve.tensor_copy(PGT, bank[:, 7, 0:3 * P]).then_inc(M["PGT_copied"], 1)
                    dve.wait_ge(s_wused, CH * i + CH)
                    dve.tensor_copy(oo[:, 512:D], bank[:, 5, :]).then_inc(M["out_copied_dve"], 1)
                    assert c.n == K_DVE, c.n

                nn = dve.value_load(npass[0:1, 0:1], min_val=1, max_val=-(-T // CAP))
                with dve.Fori(0, nn) as p:
                    with dve.Fori(0, NPAIR) as j:
                        body(p * NPAIR + j, j, p)
                    c.base, c.n = (K_DVE * NPAIR + 1) * p + K_DVE * NPAIR + n0, 0
                    c(dve.tensor_scalar(rk, rk, -float(CAP), None, ALU.add))
                add_y(nn * NPAIR)

        yrow = lambda t: work[rows(t), D * t:D * (t + 1)]
        s_yout = sem("y_stored")
        norm("final", yrow, lambda e: e.wait_ge(s_wb, 48), False)
        with nc.Block() as block:
            @block.sync
            def _(sp):
                sp.dma_start(y_prompt[0].rearrange("(t p) d -> p t d", p=P), work[:, 0:2 * D].rearrange("p (t d) -> p t d", t=2))\
                  .then_inc(s_yout, 16)
                sp.dma_start(y_sample.rearrange("s i d -> (s i) d"), yrow(2)).then_inc(s_yout, 16)
                sp.wait_ge(s_yout, 32)


_INS = ['x_prompt', 'x_sample', 'cache_k', 'cache_v', 'page_table', 'state_conv', 'state_ssm', 'norm_mix', 'w_in', 'conv_w',
        'a_log', 'dt_bias', 'gdn_norm', 'sb_bias', 'w_out', 'norm_ffn', 'router_w', 'router_b', 'w_up', 'b_up', 'w_down',
        'b_down', 'norm_final']
_OUTS = [(1, SEQ, D), (NSEQ, NDEC, D), (1, 1, SEQ, NH, HD), (1, 1, SEQ, NH, HD), (1, 1, CONV - 1, CONVD),
         (1, 1, NH, HD, HD), (1, NSEQ, NDEC, NH, HD), (1, NSEQ, NDEC, NH, HD), (1, NSEQ, CONV - 1, CONVD),
         (1, NSEQ, NH, HD, HD)]


def kernel(**inputs):
    import concourse.bacc as bacc
    from concourse.bass_utils import run_bass_kernel_spmd

    nc = bacc.Bacc("TRN2", target_bir_lowering=False, num_devices=1)
    arrays, args = {}, []
    for name in _INS:
        a = np.ascontiguousarray(inputs[name])
        arrays[f"in_{name}"] = a
        args.append(nc.dram_tensor(f"in_{name}", a.shape, mybir.dt.from_np(a.dtype), kind="ExternalInput").ap())
    for i, shape in enumerate(_OUTS):
        args.append(nc.dram_tensor(f"out_{i}", shape, F32, kind="ExternalOutput").ap())
    build(nc, *args)
    r = run_bass_kernel_spmd(nc, [arrays], core_ids=[0])
    return tuple(r.results[0][f"out_{i}"] for i in range(len(_OUTS)))
```

```python
from contextlib import ExitStack

import numpy as np
import concourse.bass as bass
from concourse import mybir

F32 = mybir.dt.float32
I32 = mybir.dt.int32
ALU = mybir.AluOpType
ACT = mybir.ActivationFunctionType
AX = mybir.AxisListType

P = 128
D = 1024
KD = D // P
HD = 64
NH = 8
HP = NH // 2
GW = NH * HD
CONV = 4
NSEQ, NDEC = 8, 4
ND = NSEQ * NDEC
SEQ = 256
T = SEQ + ND
ROWS = [P, P, ND]
TOK0 = [0, P, 2 * P]
PAGE, NPG = 128, 8
PAST = PAGE * NPG
POOL = 80
NE, TOPK, FF = 32, 4, 1024
CAP = 64
RSLOT = 2048
NSLOT = 12
BIG = 1.0e30
EPS = 1e-6
SCALE = HD ** -0.5
CONVD = 3 * GW
WORK = 15900
C_Z, C_BA, C_S = CONVD, CONVD + GW, CONVD + GW + 2 * NH


class Chain:

    def __init__(self, eng, sem):
        self.eng, self.sem, self.n, self.base = eng, sem, 0, 0

    def __call__(self, ins):
        self.n += 1
        ins.then_inc(self.sem, 1)
        self.eng.wait_ge(self.sem, self.base + self.n)


def build(nc, x_prompt, x_sample, cache_k, cache_v, page_table, state_conv, state_ssm, norm_mix, w_in, conv_w,
          a_log, dt_bias, gdn_norm, sb_bias, w_out, norm_ffn, router_w, router_b, w_up, b_up, w_down, b_down,
          norm_final, y_prompt, y_sample, k_prompt, v_prompt, conv_prompt, ssm_prompt, k_sample, v_sample,
          conv_sample, ssm_sample):
    ctx = ExitStack()
    with ctx:
        def sb(name, shape, dt=F32):
            return ctx.enter_context(nc.sbuf_tensor(name, shape, dt))

        def sem(name):
            return ctx.enter_context(nc.semaphore(name))

        bank = ctx.enter_context(nc.psum_tensor("bank", [P, 8, 512], F32))

        ring = sb("ring", [P, NSLOT * RSLOT])
        X = sb("X", [P, 3, D])
        wb = sb("wb", [P, D])
        hT = sb("hT", [P, KD, T])
        oT = sb("oT", [P, KD, T])
        ident = sb("ident", [P, P])
        ones = sb("ones", [P, P])
        stat = sb("stat", [P, 3, 4])
        epst = sb("epst", [P, 2])
        work = sb("work", [P, WORK])

        def at(off, shape, parts=P):
            n = int(np.prod(shape))
            v = work[0:parts, off:off + n]
            if len(shape) == 2:
                v = v.rearrange("p (a b) -> p a b", a=shape[0])
            elif len(shape) == 3:
                v = v.rearrange("p (a b c) -> p a b c", a=shape[0], b=shape[1])
            return v

        def slot(u, n=1):
            i = (u + 10) % NSLOT
            return ring[:, i * RSLOT:(i + n) * RSLOT]

        def rows(t):
            return slice(0, ROWS[t])

        def toks(t):
            return slice(TOK0[t], TOK0[t] + ROWS[t])

        c0 = WORK
        def const(*shape):
            nonlocal c0
            c0 -= int(np.prod(shape))
            return at(c0, shape) if len(shape) > 1 else work[:, c0:c0 + shape[0]]

        Uinc = const(P)
        negS, negU = const(P), const(P)
        LVL = const(7, P)
        blk64 = const(P)
        SM = const(ND)
        dLst, dUinc, dneg, dnegU = const(ND), const(ND), const(ND), const(ND)
        E = const(2, P)
        Sel = const(2, 16)
        headmask = const(512)
        sel8, hch = const(P), const(512)
        sbcol, sbb, sbrow, nsbrow, nsbb = const(1), const(NH), const(1), const(1), const(NH)
        alog, dtb = const(NH), const(NH)
        gnorm = const(HD)
        convw = const(12, CONV)
        scT = const(12, 24)
        pt = work[0:1, c0 - 64:c0].bitcast(I32)
        c0 -= 64
        CONST_END = c0

        qsT, ksT = at(0, (HP, T)), at(HP * T, (HP, T))
        A1 = 2 * HP * T
        vs_tok, z_tok = at(A1, (3, GW)), at(A1 + 3 * GW, (3, GW))
        A2 = A1 + 6 * GW
        ba = at(A2, (3, 2 * NH))
        A2 += 48

        s_x = sem("x_loaded")
        s_small, s_small2 = sem("conv_state_loaded"), sem("small_loaded")
        s_wb = sem("norm_weight_loaded")
        s_pool = sem("pool_chain")
        s_act = sem("act_chain")
        s_dve = sem("dve_chain")
        s_pe = sem("pe_chain")
        s_slot = [sem(f"slot_loaded{i}") for i in range(NSLOT)]
        s_ringfree = sem("ring_used")
        s_ba_w = sem("ba_weights_loaded")
        wba = sb("wba", [P, KD, 2 * NH])
        scrow = work[0:24, 0:CONVD]
        cwrow = work[0:CONV, CONVD:2 * CONVD]

        w_in_v = w_in[0].rearrange("(k p) n -> p k n", p=P)
        w_out_v = w_out[0].rearrange("(k p) n -> p k n", p=P)
        GROUP_COL = [0, GW, 2 * GW, C_Z, C_S, C_S + GW, C_S + 2 * GW]

        U_C, U_WO, U_END = 14, 46, 50
        PGL = 4

        def slot_sem(u):
            return s_slot[(u + 10) % NSLOT]

        def slot_count(u):
            return sum(16 * (PGL if U_C <= v < U_WO else 1) for v in range(u % NSLOT, u + 1, NSLOT)
                       if U_C <= v < U_WO or v % 2 == 0)

        def slot_wait(eng, u):
            return eng.wait_ge(slot_sem(u), slot_count(u))

        def slot_free(eng, u, n):
            if u + n > NSLOT:
                eng.wait_ge(s_ringfree, u + n - NSLOT)

        def load_w_in(eng, n):
            slot_free(eng, 2 * n, 2)
            eng.dma_start(slot(2 * n, 2).rearrange("p (k n) -> p k n", k=KD),
                          w_in_v[:, :, GROUP_COL[n]:GROUP_COL[n] + GW]).then_inc(slot_sem(2 * n), 16)

        def load_cache(eng, m):
            g, kv, ph, s = m // 16, m // 8 % 2, m // 4 % 2, m % 4
            slot_free(eng, U_C + m, 1)
            for pg in range(PGL):
                col = NPG * (4 * g + s) + PGL * ph + pg
                page = eng.value_load(pt[0:1, col:col + 1], min_val=0, max_val=POOL - 1)
                eng.dma_start(slot(U_C + m)[:, pg * GW:(pg + 1) * GW],
                              (cache_k, cache_v)[kv][0, bass.ds(page, 1)].rearrange("o p h d -> (o p) (h d)"))\
                   .then_inc(slot_sem(U_C + m), 16)

        act_n, dve_n, pool_n, pe_n = [0], [0], [0], [0]

        s_nsq, s_nstd, s_nrow, s_ntp, s_nev = (
            sem(f"norm_{n}") for n in ("squares", "std", "rows", "turned", "copied"))

        class Norm:

            def __init__(self, nth, rowbuf, weight_wait, turned, ready=lambda e: None):
                self.rowbuf, self.weight_wait, self.turned, self.ready = rowbuf, weight_wait, turned, ready
                self.base = 3 * nth

            def scalar(self, act):
                self.ready(act)
                for t in range(3):
                    r = rows(t)
                    act.activation(self.rowbuf(t), X[r, t, :], ACT.Square, accum_out=stat[r, t, 0:1]).then_inc(s_nsq, 1)
                for t in range(3):
                    r = rows(t)
                    act.wait_ge(s_nsq, self.base + t + 1)
                    act.activation(stat[r, t, 1:2], stat[r, t, 0:1], ACT.Sqrt, scale=1.0 / D,
                                   bias=epst[r, 0:1]).then_inc(s_nstd, 1)
                if self.turned:
                    for t in range(3):
                        act.wait_ge(s_ntp, self.base + t + 1)
                        b = 2 * (t % 2)
                        n = ROWS[t]
                        act.activation(hT[:, :, toks(t)],
                                       bank[:, b:b + 2, :].rearrange("p b n -> p (b n)")[:, 0:KD * n]
                                       .rearrange("p (k n) -> p k n", k=KD), ACT.Copy).then_inc(s_nev, 1)

            def vector(self, dve):
                c = Chain(dve, s_dve)
                c.n = dve_n[0]
                self.weight_wait(dve)
                for t in range(3):
                    r = rows(t)
                    dve.wait_ge(s_nstd, self.base + t + 1)
                    c(dve.reciprocal(stat[r, t, 2:3], stat[r, t, 1:2]))
                    dve.scalar_tensor_tensor(out=self.rowbuf(t), in0=X[r, t, :], scalar=stat[r, t, 2:3], in1=wb[r, :],
                                             op0=ALU.mult, op1=ALU.mult).then_inc(s_nrow, 1)
                dve_n[0] = c.n

            def tensor(self, pe):
                for t in range(3):
                    pe.wait_ge(s_nrow, self.base + t + 1)
                    if t == 2:
                        pe.wait_ge(s_nev, self.base + 1)
                    b, n = 2 * (t % 2), ROWS[t]
                    dst = bank[:, b:b + 2, :].rearrange("p b n -> p (b n)")
                    for k in range(KD):
                        ins = pe.transpose(dst[:, k * n:(k + 1) * n], self.rowbuf(t)[:, k * P:(k + 1) * P],
                                           ident[0:n, 0:n])
                    ins.then_inc(s_ntp, 1)

        hrow = lambda t: work[rows(t), A2 + D * t:A2 + D * (t + 1)]
        s_id, s_t, s_zero = sem("identity_ready"), sem("turned"), sem("zeros_written")

        def x_ready(eng):
            eng.wait_ge(s_id, 1)
            eng.wait_ge(s_x, 32)
        mixnorm = Norm(0, hrow, lambda e: (e.wait_ge(s_wb, 16), x_ready(e)), True, x_ready)
        with nc.Block() as block:
            @block.sync
            def _(sp):
                sp.dma_start(X[:, 0:2, :], x_prompt[0].rearrange("(t p) d -> p t d", p=P)).then_inc(s_x, 16)
                sp.dma_start(X[0:ND, 2, :], x_sample.rearrange("s i d -> (s i) d")).then_inc(s_x, 16)
                sp.dma_start(wb[:], norm_mix[0].partition_broadcast(P)).then_inc(s_wb, 16)
                sp.dma_start(scrow, state_conv[0].rearrange("s w c -> (s w) c")).then_inc(s_small, 16)
                sp.dma_start(cwrow, conv_w[0]).then_inc(s_small, 16)
                for n in range(6):
                    load_w_in(sp, n)
                    if n == 0:
                        sp.dma_start(sbcol[0:NH, :], sb_bias.rearrange("o h -> h o")).then_inc(s_small2, 16)
                        sp.dma_start(sbb, sb_bias[0].partition_broadcast(P)).then_inc(s_small2, 16)
                        sp.dma_start(alog, a_log[0].partition_broadcast(P)).then_inc(s_small2, 16)
                        sp.dma_start(dtb, dt_bias[0].partition_broadcast(P)).then_inc(s_small2, 16)
                        sp.dma_start(gnorm, gdn_norm[0].partition_broadcast(P)).then_inc(s_small2, 16)
                        sp.dma_start(pt, page_table.rearrange("(o s) n -> o (s n)", o=1)).then_inc(s_small2, 16)
                        sp.dma_start(wba[:], w_in_v[:, :, C_BA:C_BA + 2 * NH]).then_inc(s_ba_w, 16)

            @block.gpsimd
            def _(pool):
                c = Chain(pool, s_pool)
                pool.memset(epst[:, 0:1], EPS)
                pool.memset(epst[:, 1:2], HD * EPS)
                c(pool.memset(ident[:], 0.0))
                pool.affine_select(out=ident[:], in_=ident[:], pattern=[[-1, P]], compare_op=ALU.not_equal, fill=1.0, base=0,
                                   channel_multiplier=1).then_inc(s_id, 1)
                c(pool.memset(ones[:], 1.0))
                pool_n[0] = c.n

            @block.scalar
            def _(act):
                mixnorm.scalar(act)

            @block.tensor
            def _(pe):
                pe.wait_ge(s_id, 1)
                pe.wait_ge(s_small, 32)
                for t in range(12):
                    pe.transpose(bank[:, 6, 24 * t:24 * t + 24], scrow[:, t * P:(t + 1) * P], ident[0:24, 0:24])
                    ins = pe.transpose(bank[:, 7, CONV * t:CONV * (t + 1)], cwrow[:, t * P:(t + 1) * P], ident[0:CONV, 0:CONV])
                ins.then_inc(s_t, 1)
                mixnorm.tensor(pe)

            @block.vector
            def _(dve):
                dve.memset(z_tok, 0.0)
                dve.memset(ba, 0.0)
                dve.wait_ge(s_t, 1)
                dve.tensor_copy(scT, bank[:, 6, 0:288].rearrange("p (a b) -> p a b", a=12))
                dve.tensor_copy(convw, bank[:, 7, 0:48].rearrange("p (a b) -> p a b", a=12))
                mixnorm.vector(dve)

        B0 = A2
        pad = [work[:, B0 + 316 * i:B0 + 316 * i + 315] for i in range(2)]
        B1 = B0 + 632
        turnT = [work[:, B1 + T * i:B1 + T * (i + 1)] for i in range(2)]
        B2 = B1 + 2 * T
        csig = work[:, B2:B2 + 2 * T].rearrange("p (b n) -> p b n", b=2)
        B3 = B2 + 2 * T
        cdec, cpro = work[0:NSEQ * 7, B3:B3 + CONVD], work[64:67, B3:B3 + CONVD]
        kst = at(B3 + CONVD, (3, GW))
        assert B3 + 2 * CONVD <= CONST_END
        gq = sb("gq", [P, 12, T])
        tiles = [("conv", j) for j in range(12)] + [("z", j) for j in range(4)] + \
                [("q", j) for j in range(4)] + [("k", j) for j in range(4)] + [("v", j) for j in range(4)] + [("ba", 0)]
        turned_tiles = [i for i, (kind, _) in enumerate(tiles) if kind in ("z", "k", "v", "ba")]
        s_pj, s_pje = sem("projected"), sem("projection_copied")
        s_tt, s_tte = sem("proj_turned"), sem("proj_turned_copied")
        s_cu, s_cue = sem("convstate_turned"), sem("convstate_copied")
        s_cv, s_sg, s_pb = sem("conv_summed"), sem("conv_sigmoid"), sem("conv_state_placed")
        s_cs = sem("conv_state_stored")
        s_kvout = sem("kv_stored")
        s_silu, s_masks = sem("conv_silu"), sem("masks_ready")

        def padx(i):
            return pad[i % 2][:, 3:259], pad[i % 2][:, 259:315].rearrange("p (s w) -> p s w", w=7)

        with nc.Block() as block:
            @block.sync
            def _(sp):
                load_w_in(sp, 6)
                sp.wait_ge(s_small2, 96)
                for m in range(NSLOT):
                    load_cache(sp, m)
                sp.wait_ge(s_cue, 3)
                for s in range(NSEQ):
                    sp.dma_start(conv_sample[0, s], cdec[7 * s + 4:7 * s + 7, :]).then_inc(s_cs, 16)
                sp.dma_start(conv_prompt[0, 0], cpro).then_inc(s_cs, 16)
                i_k = [turned_tiles.index(tiles.index(("k", 3))), turned_tiles.index(tiles.index(("v", 3)))]
                for i, (src, dp, ds_) in zip(i_k, ((kst, k_prompt, k_sample), (vs_tok, v_prompt, v_sample))):
                    sp.wait_ge(s_tte, i + 1)
                    sp.dma_start(dp[0, 0].rearrange("(t p) h d -> p t (h d)", p=P), src[:, 0:2, :]).then_inc(s_kvout, 16)
                    sp.dma_start(ds_[0].rearrange("s i h d -> (s i) (h d)"), src[0:ND, 2, :]).then_inc(s_kvout, 16)

            @block.tensor
            def _(pe):
                done_turn = [0]

                def turn(i):
                    kind, j = tiles[i]
                    if kind == "conv":
                        pe.wait_ge(s_pje, i + 1)
                        if j % 4 == 0 and j:
                            pe.wait_ge(s_cue, j // 4)
                        px, pd = padx(i)
                        pe.transpose(bank[0:3, 4, (j % 4) * P:(j % 4 + 1) * P], px[:, SEQ - 3:SEQ], ident[:])
                        pe.transpose(bank[0:NSEQ * 7, 5, (j % 4) * P:(j % 4 + 1) * P], pad[i % 2][:, 259:315],
                                     ident[:]).then_inc(s_cu, 1)
                    elif i in turned_tiles:
                        pe.wait_ge(s_pje, i + 1)
                        m = done_turn[0]
                        done_turn[0] += 1
                        if m >= 2:
                            pe.wait_ge(s_tte, m - 1)
                        n = 2 * NH if kind == "ba" else P
                        src = ksT[:, j, :] if kind == "k" else turnT[m % 2]
                        for t in range(3):
                            ins = pe.transpose(bank[rows(t), 2 + m % 2, t * P:t * P + n], src[0:n, toks(t)],
                                               ident[0:n, 0:n])
                        ins.then_inc(s_tt, 1)

                for i, (kind, j) in enumerate(tiles):
                    if i >= 2:
                        pe.wait_ge(s_pje, i - 1)
                    n = i // 4
                    if kind == "ba":
                        pe.wait_ge(s_ba_w, 16)
                    elif i % 4 == 0:
                        slot_wait(pe, 2 * n)
                    m = 2 * NH if kind == "ba" else P
                    w = wba[:] if kind == "ba" else slot(2 * n, 2).rearrange("p (k n) -> p k n", k=KD)[:, :, j % 4 * P:(j % 4 + 1) * P]
                    for k in range(KD):
                        ins = pe.matmul(bank[0:m, i % 2, 0:T], w[:, k, :], hT[:, k, :], start=k == 0, stop=k == KD - 1)
                    ins.then_inc(s_pj, 1)
                    if i % 4 == 3:
                        pe.wait_ge(s_pj, i + 1)
                        pe.sem_inc(s_ringfree, 2)
                    if i >= 1:
                        turn(i - 1)
                turn(len(tiles) - 1)
                pe.wait_ge(s_masks, 1)
                for g in range(2):
                    pe.transpose(bank[:, 6, 32 * g:32 * g + 32], E[0:ND, g, :], ident[0:ND, 0:ND])
                pe.matmul(bank[:, 7, :], sel8[0:NH, :], hch[0:NH, :], start=True, stop=True)
                pe.matmul(bank[:, 6, 64:65], sel8[0:NH, :], sbcol[0:NH, :], start=True, stop=True).then_inc(s_t, 1)

            @block.scalar
            def _(act):
                m = 0
                for i, (kind, j) in enumerate(tiles):
                    act.wait_ge(s_pj, i + 1)
                    src = bank[:, i % 2, 0:T]
                    if kind == "conv":
                        if i == 0:
                            act.wait_ge(s_pb, 1)
                        if i >= 2:
                            act.wait_ge(s_cv, i - 1)
                            act.wait_ge(s_cu, i - 1)
                        px, pd = padx(i)
                        act.activation(pd[:, :, 0:3], scT[:, i, :].rearrange("p (s w) -> p s w", w=3), ACT.Copy)
                        act.activation(px, src[:, 0:SEQ], ACT.Copy)
                        act.activation(pd[:, :, 3:7], src[:, SEQ:T].rearrange("p (s i) -> p s i", i=NDEC),
                                       ACT.Copy).then_inc(s_pje, 1)
                        if j >= 1:
                            act.wait_ge(s_cv, i)
                            if i >= 3:
                                act.wait_ge(s_silu, i - 2)
                            act.activation(csig[:, (i - 1) % 2, :], gq[:, i - 1, :], ACT.Sigmoid).then_inc(s_sg, 1)
                        continue
                    if i == 12:
                        act.wait_ge(s_cv, 12)
                        act.wait_ge(s_silu, 10)
                        act.activation(csig[:, 1, :], gq[:, 11, :], ACT.Sigmoid).then_inc(s_sg, 1)
                    if kind == "q":
                        dst = qsT[:, j, :]
                    elif kind == "k":
                        dst = ksT[:, j, :]
                        m += 1
                    else:
                        if m >= 2:
                            act.wait_ge(s_tt, m - 1)
                        dst = turnT[m % 2]
                        m += 1
                    n = 2 * NH if kind == "ba" else P
                    act.activation(dst[0:n, :], src[0:n, :], ACT.Copy).then_inc(s_pje, 1)

            @block.gpsimd
            def _(pool):
                c = Chain(pool, s_pool)
                c.n = pool_n[0]

                def keep(v, pattern, cmp, base, cm, fill=0.0):
                    c(pool.affine_select(out=v, in_=v, pattern=pattern, compare_op=cmp, fill=fill, base=base,
                                         channel_multiplier=cm))

                for m, v in ((Uinc, 1.0), (negS, 0.0), (negU, 0.0)):
                    c(pool.memset(m, v))
                keep(Uinc, [[1, P]], ALU.is_ge, 0, -1)
                keep(negS, [[-1, P]], ALU.is_gt, 0, 1, -BIG)
                keep(negU, [[1, P]], ALU.is_ge, 0, -1, -BIG)
                c(pool.memset(LVL, 0.0))
                for l in range(7):
                    b = 1 << l
                    nb = P // (2 * b)
                    v = LVL[:, l, :].rearrange("p (n h b) -> p n h b", h=2, b=b)[:, :, 0, :]
                    c(pool.memset(v, 1.0))
                    keep(v, [[-2 * b, nb], [0, b]], ALU.is_ge, -b, 1)
                    keep(v, [[2 * b, nb], [0, b]], ALU.is_ge, 2 * b - 1, -1)
                c(pool.memset(blk64, 0.0))
                c(pool.memset(blk64[0:HD, 0:HD], 1.0))
                c(pool.memset(blk64[HD:P, HD:P], 1.0))
                d = slice(0, ND)
                for m in (SM, dLst, dUinc):
                    c(pool.memset(m[d, :], 1.0))
                    v = m[d, :].rearrange("p (s j) -> p s j", j=NDEC)
                    keep(v, [[-NDEC, NSEQ], [0, NDEC]], ALU.is_ge, 0, 1)
                    keep(v, [[NDEC, NSEQ], [0, NDEC]], ALU.is_ge, NDEC - 1, -1)
                keep(dLst[d, :], [[-1, ND]], ALU.is_gt, 0, 1)
                keep(dUinc[d, :], [[1, ND]], ALU.is_ge, 0, -1)
                c(pool.tensor_scalar(dneg[d, :], dLst[d, :], 1.0, BIG, ALU.subtract, ALU.mult))
                c(pool.tensor_scalar(dnegU[d, :], dUinc[d, :], 1.0, BIG, ALU.subtract, ALU.mult))
                for g in range(2):
                    v = E[d, g, :].rearrange("p (s h i) -> p s h i", s=4, h=NH)
                    c(pool.memset(v, 0.0))
                    keep(v, [[NDEC, 4], [0, NH], [1, NDEC]], ALU.not_equal, 16 * g, -1, 1.0)
                c(pool.memset(sel8[0:NH, :], 0.0))
                keep(sel8[0:NH, :].rearrange("p (s h i) -> p s h i", s=4, h=NH), [[0, 4], [1, NH], [0, NDEC]],
                     ALU.not_equal, 0, -1, 1.0)
                c(pool.memset(hch[0:NH, :], 0.0))
                keep(hch[0:NH, :].rearrange("p (h c) -> p h c", c=HD), [[1, NH], [0, HD]], ALU.not_equal, 0, -1, 1.0)
                pool.wait_ge(s_small2, 96)
                pool.tensor_scalar(nsbb, sbb, -1.0, None, ALU.mult).then_inc(s_masks, 1)
                pool_n[0] = c.n

            @block.vector
            def _(dve):
                c = Chain(dve, s_dve)
                c.n = dve_n[0]
                state = {"m": 0}

                def conv(i):
                    dve.wait_ge(s_pje, i + 1)
                    px, pd = pad[i % 2], padx(i)[1]
                    op, od = gq[:, i, 0:SEQ], gq[:, i, SEQ:T].rearrange("p (s i) -> p s i", i=NDEC)
                    for w in range(CONV):
                        sp_, sd = px[:, w:w + SEQ], pd[:, :, w:w + NDEC]
                        sc = convw[:, i, w:w + 1]
                        if w == 0:
                            dve.tensor_scalar(op, sp_, sc, None, ALU.mult)
                            c(dve.tensor_scalar(od, sd, sc, None, ALU.mult))
                        else:
                            dve.scalar_tensor_tensor(out=op, in0=sp_, scalar=sc, in1=op, op0=ALU.mult, op1=ALU.add)
                            ins = dve.scalar_tensor_tensor(out=od, in0=sd, scalar=sc, in1=od, op0=ALU.mult, op1=ALU.add)
                            if w < CONV - 1:
                                c(ins)
                            else:
                                ins.then_inc(s_cv, 1)

                def silu(i):
                    dve.wait_ge(s_sg, i + 1)
                    dve.tensor_tensor(gq[:, i, :], gq[:, i, :], csig[:, i % 2, :], ALU.mult).then_inc(s_silu, 1)

                def turned(i):
                    kind, j = tiles[i]
                    m = state["m"]
                    state["m"] += 1
                    dve.wait_ge(s_tt, m + 1)
                    n = 2 * NH if kind == "ba" else P
                    dst = {"z": z_tok, "k": kst, "v": vs_tok, "ba": ba}[kind]
                    src = bank[:, 2 + m % 2, 0:3 * P].rearrange("p (t n) -> p t n", t=3)
                    dve.tensor_copy(dst[:, 0:2, j * P:j * P + n], src[:, 0:2, 0:n])
                    dve.tensor_copy(dst[0:ND, 2, j * P:j * P + n], src[0:ND, 2, 0:n]).then_inc(s_tte, 1)

                for i in range(2):
                    ins = dve.memset(pad[i][:, 0:3], 0.0)
                ins.then_inc(s_pb, 1)
                for i, (kind, j) in enumerate(tiles):
                    if kind == "conv":
                        conv(i)
                        if i:
                            silu(i - 1)
                        if j % 4 == 3:
                            dve.wait_ge(s_cu, j + 1)
                            cols = slice(512 * (j // 4), 512 * (j // 4 + 1))
                            dve.tensor_copy(cpro[:, cols], bank[0:3, 4, :])
                            dve.tensor_copy(cdec[:, cols], bank[0:NSEQ * 7, 5, :]).then_inc(s_cue, 1)
                    else:
                        if i == 12:
                            silu(11)
                        if i in turned_tiles:
                            turned(i)
                dve.wait_ge(s_t, 2)
                dve.tensor_copy(Sel[:, 0, :], bank[:, 6, 0:16])
                dve.tensor_copy(Sel[:, 1, :], bank[:, 6, 48:64])
                dve.tensor_copy(headmask, bank[:, 7, :])
                dve.tensor_copy(sbrow, bank[:, 6, 64:65])
                dve.tensor_scalar(nsbrow, bank[:, 6, 64:65], -1.0, None, ALU.mult)
                dve_n[0] = c.n


        NPAIR, CH = NE // 2, 24
        s_wused = sem("expert_chunk_used")

        def load_chunk(sp, j, ch):
            kp, e = (ch % 8) // 2, ch % 2
            src, col = (w_up, D * (ch // 8)) if ch < 16 else (w_down, 0)
            sp.dma_start(ring[:, (ch % NSLOT) * RSLOT:(ch % NSLOT + 1) * RSLOT].rearrange("p (k n) -> p k n", k=2),
                         src[0, bass.ds(2 * j + e, 1), 256 * kp:256 * kp + 256, col:col + D]
                         .rearrange("o (k p) n -> p (o k) n", p=P)).then_inc(s_slot[ch % NSLOT], 16)


        G = 4
        NK = PAST + ND
        KT = [hT[:].rearrange("p k t -> p (k t)")[:, 0:RSLOT].rearrange("p (s h k) -> p s h k", s=G, h=HP),
              work[:, A2:A2 + RSLOT].rearrange("p (s h k) -> p s h k", s=G, h=HP)]
        AT = work[:, A2:A2 + PAST].rearrange("p (g r) -> p g r", g=NPG)
        D1 = A2 + RSLOT
        beta, incl, rem = work[:, D1:D1 + NK], work[:, D1 + NK:D1 + 2 * NK + 1], work[:, D1 + 2 * NK + 1:D1 + 3 * NK + 1]
        D2 = D1 + 3 * NK + 1
        ATn, qbd = work[0:ND, D2:D2 + P], at(D2 + P, (HP, NSEQ, 32))
        om = rem[:, 0:GW]
        assert D2 + P + HP * NSEQ * 32 <= CONST_END
        s_qbd, s_kt, s_kta, s_ktd, s_sc, s_new = (sem(n) for n in (
            "query_blocks", "keys_turned", "keys_copied_act", "keys_copied_dve", "scores_done", "new_scores"))
        s_beta, s_A, s_AT, s_ATe, s_av, s_om, s_oT, s_oTe = (sem(n) for n in (
            "betas", "weights_A", "A_turned", "A_copied", "values_summed", "own_heads", "heads_turned", "heads_copied"))

        with nc.Block() as block:
            @block.sync
            def _(sp):
                for m in range(NSLOT, U_WO - U_C):
                    load_cache(sp, m)
                for m in range(2):
                    slot_free(sp, U_WO + 2 * m, 2)
                    sp.dma_start(slot(U_WO + 2 * m, 2).rearrange("p (k n) -> p k n", k=KD),
                                 w_out_v[:, :, m * 512:(m + 1) * 512]).then_inc(slot_sem(U_WO + 2 * m), 16)
                sp.wait_ge(s_ringfree, U_WO)
                for ch in range(8):
                    load_chunk(sp, 0, ch)

            @block.tensor
            def _(pe):
                def turn_keys(g, pg):
                    q = NPG * g + pg
                    if q >= 1:
                        pe.wait_ge(s_kta, q)
                        pe.wait_ge(s_ktd, q)
                    if g == 1 and pg == 0:
                        pe.wait_ge(s_ATe, 1)
                    for s in range(G):
                        u = U_C + 16 * g + 4 * (pg // PGL) + s
                        if pg % PGL == 0:
                            slot_wait(pe, u)
                        for p in range(HP):
                            ins = pe.transpose(bank[:, 1 + s, p * P:(p + 1) * P],
                                               slot(u)[:, pg % PGL * GW + p * P:pg % PGL * GW + (p + 1) * P], ident[:])
                    ins.then_inc(s_kt, 1)
                    if pg % PGL == PGL - 1:
                        pe.wait_ge(s_kt, q + 1)
                        pe.sem_inc(s_ringfree, G)

                def scores(g, pg):
                    q = NPG * g + pg
                    pe.wait_ge(s_kta, q + 1)
                    pe.wait_ge(s_ktd, q + 1)
                    if g == 1 and pg == 0:
                        pe.wait_ge(s_beta, 1)
                    c = (pg % 4) * PAGE
                    for p in range(HP):
                        for s in range(G):
                            ins = pe.matmul(bank[32 * s:32 * s + 32, 6 + pg // 4, c:c + PAGE], qbd[:, p, G * g + s, :],
                                            KT[q % 2][:, s, p, :], start=p == 0, stop=p == HP - 1)
                    ins.then_inc(s_sc, 1)

                pe.wait_ge(s_qbd, 1)
                for g in range(2):
                    if g == 1:
                        pe.wait_ge(s_oTe, 1)
                    for p in range(HP):
                        for s in range(G):
                            pe.matmul(bank[32 * s:32 * s + 32, 0, 0:ND], qbd[:, p, G * g + s, :], ksT[:, p, SEQ:T],
                                      start=p == 0, stop=False, skip_group_check=True)
                    pe.matmul(bank[:, 0, 0:ND], E[0:ND, g, :], dneg[0:ND, :], start=False, stop=True,
                              skip_group_check=True).then_inc(s_new, 1)
                    for pg in range(NPG):
                        turn_keys(g, pg)
                        if pg:
                            scores(g, pg - 1)
                    scores(g, NPG - 1)
                    pe.wait_ge(s_A, g + 1)
                    for pg in range(NPG):
                        pe.transpose(bank[:, 1 + pg // 4, (pg % 4) * P:(pg % 4 + 1) * P], beta[:, pg * PAGE:(pg + 1) * PAGE],
                                     ident[:])
                    pe.transpose(bank[0:ND, 3, 0:P], beta[:, PAST:NK], ident[:]).then_inc(s_AT, 1)
                    pe.wait_ge(s_ATe, g + 1)
                    if g == 1:
                        pe.wait_ge(s_om, 1)
                    for ph in range(2):
                        for s in range(G):
                            slot_wait(pe, U_C + 16 * g + 8 + 4 * ph + s)
                        for pg in range(PGL):
                            for s in range(G):
                                ins = pe.matmul(bank[32 * s:32 * s + 32, 5, :], AT[:, PGL * ph + pg, 32 * s:32 * s + 32],
                                                slot(U_C + 16 * g + 8 + 4 * ph + s)[:, pg * GW:(pg + 1) * GW],
                                                start=ph == 0 and pg == 0, stop=False)
                        if ph == 0:
                            ins.then_inc(s_av, 1)
                            pe.wait_ge(s_av, 2 * g + 1)
                            pe.sem_inc(s_ringfree, G)
                    for s in range(G):
                        ins = pe.matmul(bank[32 * s:32 * s + 32, 5, :], ATn[:, 32 * s:32 * s + 32], vs_tok[0:ND, 2, :],
                                        start=False, stop=True)
                    ins.then_inc(s_av, 1)
                    pe.wait_ge(s_av, 2 * g + 2)
                    pe.sem_inc(s_ringfree, G)
                    pe.wait_ge(s_om, g + 1)
                    for p in range(HP):
                        ins = pe.matmul(bank[:, 0, 64 + 16 * p:80 + 16 * p], om[:, p * P:(p + 1) * P], Sel[:, g, :],
                                        start=True, stop=True)
                    ins.then_inc(s_oT, 1)

            @block.scalar
            def _(act):
                for g in range(2):
                    for pg in range(NPG):
                        q = NPG * g + pg
                        act.wait_ge(s_kt, q + 1)
                        if q >= 2:
                            act.wait_ge(s_sc, q - 1)
                        if q == 9:
                            act.wait_ge(s_av, 2)
                        if q == 1:
                            act.wait_ge(s_cs, 16 * 9)
                        act.activation(KT[q % 2][:, 0:2, :, :].rearrange("p s h k -> p (s h k)"),
                                       bank[:, 1:3, :].rearrange("p b n -> p (b n)"), ACT.Copy).then_inc(s_kta, 1)
                    act.wait_ge(s_sc, NPG * (g + 1))
                    act.wait_ge(s_new, g + 1)
                    if g == 0:
                        act.wait_ge(s_kvout, 64)
                    else:
                        act.wait_ge(s_AT, 1)
                        act.wait_ge(s_oT, 1)
                    z = bank[:, 6:8, :].rearrange("p b n -> p (b n)")
                    act.activation(rem[:, 0:PAST], z, ACT.Sigmoid, scale=-SCALE, bias=nsbrow)
                    act.activation(rem[:, PAST:NK], bank[:, 0, 0:ND], ACT.Sigmoid, scale=-SCALE, bias=nsbrow)
                    act.activation(beta[:, 0:PAST], z, ACT.Sigmoid, scale=SCALE, bias=sbrow)
                    act.activation(beta[:, PAST:NK], bank[:, 0, 0:ND], ACT.Sigmoid, scale=SCALE, bias=sbrow)\
                       .then_inc(s_beta, 1)
                    act.wait_ge(s_oT, g + 1)
                    act.activation(oT[:, HP:KD, SEQ + 16 * g:SEQ + 16 * g + 16],
                                   bank[:, 0, 64:128].rearrange("p (h c) -> p h c", h=HP), ACT.Copy).then_inc(s_oTe, 1)

            @block.vector
            def _(dve):
                c = Chain(dve, s_dve)
                c.n = dve_n[0]
                c(dve.memset(qbd, 0.0))
                for p in range(HP):
                    for half in range(2):
                        r, col = slice(HD * half, HD * half + HD), NDEC * (2 * p + half)
                        ins = dve.tensor_copy(qbd[r, p, :, col:col + NDEC],
                                              qsT[r, p, SEQ:T].rearrange("p (s i) -> p s i", i=NDEC))
                ins.then_inc(s_qbd, 1)
                for g in range(2):
                    for pg in range(NPG):
                        q = NPG * g + pg
                        dve.wait_ge(s_kt, q + 1)
                        if q >= 2:
                            dve.wait_ge(s_sc, q - 1)
                        if q == 9:
                            dve.wait_ge(s_av, 2)
                        if q == 1:
                            dve.wait_ge(s_cs, 16 * 9)
                        dve.tensor_copy(KT[q % 2][:, 2:4, :, :].rearrange("p s h k -> p (s h k)"),
                                        bank[:, 3:5, :].rearrange("p b n -> p (b n)")).then_inc(s_ktd, 1)
                    dve.wait_ge(s_beta, g + 1)
                    if g == 0:
                        c(dve.memset(incl[:, NK:NK + 1], 1.0))
                    c(dve.tensor_tensor_scan(incl[:, 0:NK][:, ::-1], rem[:, ::-1], rem[:, ::-1], 1.0, ALU.mult, ALU.bypass))
                    dve.tensor_tensor(beta, beta, incl[:, 1:NK + 1], ALU.mult).then_inc(s_A, 1)
                    dve.wait_ge(s_AT, g + 1)
                    dve.wait_ge(s_sc, NPG * (g + 1))
                    dve.tensor_copy(AT.rearrange("p g r -> p (g r)"), bank[:, 1:3, :].rearrange("p b n -> p (b n)"))
                    dve.tensor_copy(ATn, bank[0:ND, 3, 0:P]).then_inc(s_ATe, 1)
                    dve.wait_ge(s_av, 2 * g + 2)
                    dve.tensor_tensor(om, bank[:, 5, :], headmask, ALU.mult).then_inc(s_om, 1)
                dve_n[0] = c.n

        W3 = 3 * P
        pbeta = [work[:, A2 + W3 * i:A2 + W3 * (i + 1)] for i in range(2)]
        prem = [work[:, A2 + W3 * (2 + i):A2 + W3 * (3 + i)] for i in range(2)]
        D3 = A2 + 4 * W3
        pincl = [work[:, D3 + 386 * i:D3 + 386 * (i + 1)] for i in range(2)]
        D4 = D3 + 772
        pAT = [work[:, D4 + W3 * i:D4 + W3 * (i + 1)] for i in range(2)]
        assert D4 + 2 * W3 <= CONST_END
        s_pz, s_pbeta, s_pA, s_pAT, s_pATe, s_po, s_poe = (sem(n) for n in (
            "prompt_scores", "prompt_betas", "prompt_A", "prompt_A_turned", "prompt_A_copied", "prompt_heads",
            "prompt_heads_copied"))
        with nc.Block() as block:
            @block.tensor
            def _(pe):
                def scores(h):
                    p, r = h // 2, slice(HD * (h % 2), HD * (h % 2) + HD)
                    if h >= 2:
                        pe.wait_ge(s_pbeta, h - 1)
                    z = bank[:, h % 2, :]
                    pe.matmul(z[:, 0:P], qsT[r, p, 0:P], ksT[r, p, 0:P], start=True, stop=False, skip_group_check=True)
                    pe.matmul(z[:, 0:P], ident[:], negS, start=False, stop=True, skip_group_check=True)
                    pe.matmul(z[:, P:W3], qsT[r, p, P:SEQ], ksT[r, p, 0:SEQ], start=True, stop=False, skip_group_check=True)
                    pe.matmul(z[:, 2 * P:W3], ident[:], negS, start=False, stop=True, skip_group_check=True)\
                      .then_inc(s_pz, 1)

                def turn(h):
                    pe.wait_ge(s_pA, h + 1)
                    if h >= 2:
                        pe.wait_ge(s_pATe, h - 1)
                    for b in range(3):
                        ins = pe.transpose(bank[:, 2 + h % 2, b * P:(b + 1) * P], pbeta[h % 2][:, b * P:(b + 1) * P], ident[:])
                    ins.then_inc(s_pAT, 1)

                def values(h):
                    pe.wait_ge(s_pATe, h + 1)
                    if h >= 4 and h % 2 == 0:
                        pe.wait_ge(s_poe, h // 2 - 1)
                    r = slice(HD * (h % 2), HD * (h % 2) + HD)
                    o = bank[r, 4 + (h // 2) % 2, :]
                    a = pAT[h % 2]
                    hc = slice(HD * h, HD * h + HD)
                    pe.matmul(o[:, 0:P], vs_tok[:, 0, hc], a[:, 0:P], start=True, stop=True)
                    pe.matmul(o[:, P:SEQ], vs_tok[:, 0, hc], a[:, P:2 * P], start=True, stop=False)
                    pe.matmul(o[:, P:SEQ], vs_tok[:, 1, hc], a[:, 2 * P:W3], start=False, stop=True).then_inc(s_po, 1)

                scores(0)
                for h in range(NH):
                    if h + 1 < NH:
                        scores(h + 1)
                    turn(h)
                    if h:
                        values(h - 1)
                values(NH - 1)

            @block.scalar
            def _(act):
                for h in range(NH):
                    act.wait_ge(s_pz, h + 1)
                    if h >= 2:
                        act.wait_ge(s_pAT, h - 1)
                    act.activation(prem[h % 2], bank[:, h % 2, 0:W3], ACT.Sigmoid, scale=-SCALE, bias=nsbb[:, h:h + 1])
                    act.activation(pbeta[h % 2], bank[:, h % 2, 0:W3], ACT.Sigmoid, scale=SCALE, bias=sbb[:, h:h + 1])\
                       .then_inc(s_pbeta, 1)
                    if h >= 1:
                        act.wait_ge(s_pAT, h)
                        if h >= 3:
                            act.wait_ge(s_po, h - 2)
                        act.activation(pAT[(h - 1) % 2], bank[:, 2 + (h - 1) % 2, 0:W3], ACT.Copy).then_inc(s_pATe, 1)
                act.wait_ge(s_pAT, NH)
                act.wait_ge(s_po, NH - 2)
                act.activation(pAT[(NH - 1) % 2], bank[:, 2 + (NH - 1) % 2, 0:W3], ACT.Copy).then_inc(s_pATe, 1)

            def copy_heads(dve, p):
                dve.wait_ge(s_po, 2 * p + 2)
                dve.tensor_copy(oT[:, HP + p, 0:SEQ], bank[:, 4 + p % 2, 0:SEQ]).then_inc(s_poe, 1)

            @block.vector
            def _(dve):
                c = Chain(dve, s_dve)
                c.n = dve_n[0]
                for i in range(2):
                    for col in (P, 385):
                        ins = dve.memset(pincl[i][:, col:col + 1], 1.0)
                c(ins)
                for h in range(NH):
                    dve.wait_ge(s_pbeta, h + 1)
                    b, m, i = pbeta[h % 2], prem[h % 2], pincl[h % 2]
                    dve.tensor_tensor_scan(i[:, 0:P][:, ::-1], m[:, 0:P][:, ::-1], m[:, 0:P][:, ::-1], 1.0, ALU.mult, ALU.bypass)
                    c(dve.tensor_tensor_scan(i[:, 129:385][:, ::-1], m[:, P:W3][:, ::-1], m[:, P:W3][:, ::-1], 1.0, ALU.mult,
                                             ALU.bypass))
                    dve.tensor_tensor(b[:, 0:P], b[:, 0:P], i[:, 1:P + 1], ALU.mult)
                    dve.tensor_tensor(b[:, P:W3], b[:, P:W3], i[:, 130:386], ALU.mult).then_inc(s_pA, 1)
                    if h % 2 == 1:
                        if h >= 3:
                            copy_heads(dve, h // 2 - 1)
                copy_heads(dve, HP - 1)
                dve_n[0] = c.n

        sq = work[:, A2:A2 + 8 * T].rearrange("p (a t) -> p a t", a=8)
        rt = work[:, A2 + 8 * T:A2 + 16 * T].rearrange("p (a t) -> p a t", a=8)
        S1 = 3328
        bet, gg, xa, ax = (at(S1 + 24 * i, (3, NH)) for i in range(4))
        ea = work[:, S1 + 96:S1 + 104]
        s_sq, s_ss, s_rt = sem("squares"), sem("square_sums"), sem("roots")
        s_ea, s_ax, s_ex = sem("decay_rates"), sem("abs_a"), sem("log1p_a")
        with nc.Block() as block:
            @block.vector
            def _(dve):
                c = Chain(dve, s_dve)
                c.n = dve_n[0]
                for i in range(2):
                    dve.tensor_tensor(sq[:, 4 * i:4 * i + 4, :], gq[:, 4 * i:4 * i + 4, :], gq[:, 4 * i:4 * i + 4, :],
                                      ALU.mult).then_inc(s_sq, 1)
                c(dve.tensor_tensor(xa, ba[:, :, NH:2 * NH], dtb.unsqueeze(1).to_broadcast([P, 3, NH]), ALU.add))
                dve.scalar_tensor_tensor(out=ax, in0=xa, scalar=-1.0, in1=xa, op0=ALU.mult, op1=ALU.min).then_inc(s_ax, 1)
                dve.wait_ge(s_ex, 1)
                c(dve.scalar_tensor_tensor(out=gg, in0=xa, scalar=0.0, in1=ax, op0=ALU.max, op1=ALU.add))
                c(dve.scalar_tensor_tensor(out=gg, in0=gg, scalar=-1.0, in1=ea.unsqueeze(1).to_broadcast([P, 3, NH]),
                                           op0=ALU.mult, op1=ALU.mult))
                for i in range(2):
                    q = slice(4 * i, 4 * i + 4)
                    dve.wait_ge(s_rt, i + 1)
                    c(dve.reciprocal(rt[:, q, :], rt[:, q, :]))
                    c(dve.tensor_tensor(gq[:, q, :], gq[:, q, :], rt[:, q, :], ALU.mult))
                dve_n[0] = c.n

            @block.tensor
            def _(pe):
                for i in range(8):
                    pe.wait_ge(s_sq, i // 4 + 1)
                    pe.matmul(bank[:, i, 0:T], blk64, sq[:, i, :], start=True, stop=True).then_inc(s_ss, 1)

            @block.scalar
            def _(act):
                c = Chain(act, s_act)
                c.n = act_n[0]
                act.activation(bet, ba[:, :, 0:NH], ACT.Sigmoid)
                act.activation(ea, alog, ACT.Exp)
                act.wait_ge(s_ax, 1)
                c(act.activation(ax, ax, ACT.Exp))
                act.activation(ax, ax, ACT.Ln, bias=ones[:, 0:1]).then_inc(s_ex, 1)
                for i, sc in ((0, float(HD)), (1, 1.0)):
                    act.wait_ge(s_ss, 4 * i + 4)
                    act.activation(rt[:, 4 * i:4 * i + 4, :], bank[:, 4 * i:4 * i + 4, 0:T], ACT.Sqrt, scale=sc,
                                   bias=epst[:, 1 - i:2 - i]).then_inc(s_rt, 1)
                act_n[0] = c.n

        kbg, vb, ktail, vn, ob, wTb = (work[:, 512 * i:512 * (i + 1)] for i in range(6))
        St = at(3072, (HP, HD))
        S0 = at(A2 + 2048, (NSEQ, HP, HD))
        Gs, eG, eL, eT, bG, ss, rs = (work[:, S1 + 104 + 16 * i:S1 + 120 + 16 * i] for i in range(7))
        eLs = work[:, S1 + 216:S1 + 220]
        s_ssm = sem("ssm_stored")
        s_s0 = sem("ssm_loaded")

        N = {k: sem(f"gdn_{k}") for k in (
            "gU", "G", "Gs", "R", "kv", "kvused", "kk", "qk", "dec", "exp", "L", "QK", "lm", "T0", "TTp",
            "TT", "Y", "Ye", "P", "Tn", "wu", "wTe", "vn", "qs", "o2", "S", "ss", "std", "oT", "sz", "ws", "vmr", "St")}

        def gdn_steps(k, ci):
            if k in ("lm", "Y", "Ye", "P", "Tn"):
                return 2 if ci == 2 else 12
            return {"Gs": (2, 2, 3), "dec": (2, 2, 2), "exp": (3, 3, 3), "L": (2, 2, 2), "qs": (0, 1, 1),
                    "S": (1, 1, 2), "std": (2, 2, 2), "ws": (0, 0, 2), "vmr": (0, 0, 2)}.get(k, (1, 1, 1))[ci]

        def gdn_chunk(ci):
            n = ROWS[ci]
            R, dec = slice(0, n), ci == 2
            W = NH * n
            stp = W if dec else 1024
            Lb, Lm, Tb, TT, Y, QK = (work[R, A2 + stp * i:A2 + stp * i + W] for i in range(6))
            D0 = A2 + 6 * stp
            sz = work[R, D0:D0 + GW]
            if not dec:
                assert D0 + GW <= CONST_END
                D0 = A2
            vm = work[0:ND, D0 + 2560:D0 + 4608]
            WQ = work[:, D0 + 4608:D0 + 4864].rearrange("p (h s c) -> p h s c", h=HP, s=NSEQ)
            W1, Q1 = (work[:, D0 + 4864 + P * i:D0 + 4864 + P * (i + 1)] for i in range(2))
            gm, eGb, eGls = work[0:ND, 3840 - 264:3840 - 200], work[:, 3840 - 200:3840 - 136], work[:, 3840 - 136:3840 - 104]
            mU, nU, nS, mAll = (dUinc[R], dnegU[R], dneg[R], SM[R]) if dec else (Uinc, negU, negS, ones[:])
            hv = lambda v: v.rearrange("p (h i) -> p h i", h=NH)
            bc = lambda m, w: m.unsqueeze(1).to_broadcast([n, NH, w])
            hb = lambda v, w: v.unsqueeze(2).to_broadcast([n, NH, w])
            pv = lambda v: v.rearrange("p (a h i) -> p a h i", a=2, h=HP)
            pb = lambda v: v.rearrange("p (h a) -> p a h", a=2).unsqueeze(3).to_broadcast([n, 2, HP, n])
            rg = lambda b: bank[R, b:b + 2, 0:HP * n]
            rgh = lambda b, h: bank[R, b + h % 2, (h // 2) * n:(h // 2 + 1) * n]
            two = lambda v: v.rearrange("p (a c) -> p a c", a=2)
            hs = lambda h: slice(((h % 2) * HP + h // 2) * n, ((h % 2) * HP + h // 2 + 1) * n)
            hc = lambda h: slice(HD * h, HD * h + HD)
            pr = lambda h: slice(HD * (h % 2), HD * (h % 2) + HD)
            half = lambda a: slice(4 * n * a, 4 * n * (a + 1))
            nlev = 2 if dec else 7
            C = lambda k: sum(gdn_steps(k, c) for c in range(ci))
            with nc.Block() as block:
                @block.sync
                def _(sp):
                    if dec:
                        for par in range(2):
                            for s in range(NSEQ):
                                sp.dma_start(S0[HD * par:HD * par + HD, s],
                                             state_ssm[0, s].rearrange("(p two) k v -> two k p v", two=2)[par]).then_inc(s_s0, 16)

                @block.tensor
                def _(pe):
                    pe.matmul(bank[R, 6, 0:NH], mU, gg[R, ci, :], start=True, stop=True)
                    ins = pe.matmul(bank[R, 6, NH:2 * NH], mAll[:, 0:n], gg[R, ci, :], start=True, stop=True)
                    pe.wait_ge(N["gU"], C("gU") + 1)
                    if dec:
                        ins = pe.matmul(bank[:, 7, 0:64], ones[0:ND, :], gm, start=True, stop=True)
                    ins.then_inc(N["G"], 1)
                    for a in range(2):
                        ins = pe.matmul(bank[R, a, 0:HP * n], ones[R, 0:n], Lm[:, half(a)], start=True, stop=True)
                    ins.then_inc(N["R"], 1)
                    for h in range(NH):
                        k = gq[pr(h), 4 + h // 2, toks(ci)]
                        ins = pe.matmul(rgh(2, h), k, k, start=True, stop=True)
                    ins.then_inc(N["kk"], 1)
                    for h in range(NH):
                        ins = pe.matmul(rgh(4, h), gq[pr(h), 4 + h // 2, toks(ci)], gq[pr(h), h // 2, toks(ci)],
                                        start=True, stop=True)
                    ins.then_inc(N["qk"], 1)
                    pe.wait_ge(N["Gs"], C("Gs") + (2 if dec else 1))
                    for p in range(HP):
                        pe.transpose(bank[R, 6, p * P:(p + 1) * P], gq[:, 4 + p, toks(ci)], ident[:])
                        ins = pe.transpose(bank[R, 7, p * P:(p + 1) * P], gq[:, 8 + p, toks(ci)], ident[:])
                    ins.then_inc(N["kv"], 1)
                    pe.wait_ge(N["T0"], C("T0") + 1)
                    for h in range(NH):
                        ins = pe.transpose(rgh(0, h), Tb[:, hs(h)], ident[R, 0:n])
                    ins.then_inc(N["TTp"], 1)
                    pe.wait_ge(N["TT"], C("TT") + 1)
                    pe.wait_ge(N["kvused"], C("kvused") + 1)
                    pe.wait_ge(N["QK"], C("QK") + 1)
                    for l in range(1, nlev):
                        for a in range(2):
                            pe.wait_ge(N["lm"], C("lm") + 2 * (l - 1) + a + 1)
                            if l > 1:
                                pe.wait_ge(N["Tn"], C("Tn") + 2 * (l - 2) + a + 1)
                            for h in range(a, NH, 2):
                                ins = pe.matmul(rgh(2, h), Lm[:, hs(h)], TT[:, hs(h)], start=True, stop=True)
                            ins.then_inc(N["Y"], 1)
                        for a in range(2):
                            pe.wait_ge(N["Ye"], C("Ye") + 2 * (l - 1) + a + 1)
                            for h in range(a, NH, 2):
                                if l < nlev - 1:
                                    pe.matmul(rgh(4, h), Y[:, hs(h)], Tb[:, hs(h)], start=True, stop=True)
                                ins = pe.matmul(rgh(6, h), Tb[:, hs(h)], Y[:, hs(h)], start=True, stop=True)
                            ins.then_inc(N["P"], 1)
                    pe.wait_ge(N["Tn"], C("Tn") + 2 * (nlev - 1))
                    for h in range(NH):
                        pe.matmul(bank[pr(h), 0, (h // 2) * n:(h // 2 + 1) * n], kbg[R, hc(h)], TT[:, hs(h)],
                                  start=True, stop=True)
                    for h in range(NH):
                        ins = pe.matmul(bank[R, 1, hc(h)], TT[:, hs(h)], vb[R, hc(h)], start=True, stop=True)
                    ins.then_inc(N["wu"], 1)
                    if ci == 1:
                        pe.wait_ge(N["wTe"], C("wTe") + 1)
                        for h in range(NH):
                            pe.matmul(bank[R, 4 + h % 2, hc(h // 2)], wTb[pr(h), (h // 2) * n:(h // 2 + 1) * n], St[pr(h), h // 2, :],
                                      start=True, stop=True)
                        for h in range(NH):
                            ins = pe.matmul(bank[R, 6 + h % 2, hc(h // 2)], gq[pr(h), h // 2, toks(ci)], St[pr(h), h // 2, :],
                                            start=True, stop=True)
                        ins.then_inc(N["qs"], 1)
                    if dec:
                        pe.wait_ge(N["wTe"], C("wTe") + 1)
                        pe.wait_ge(s_s0, 256)
                        for s in range(NSEQ):
                            for h in range(NH):
                                o = 64 * (h // 2) + 8 * s
                                ins = pe.matmul(bank[pr(h), 4, o:o + 8], S0[pr(h), s, h // 2, :], WQ[pr(h), h // 2, s, :],
                                                start=True, stop=True)
                        ins.then_inc(N["ws"], 1)
                        pe.wait_ge(N["ws"], C("ws") + 2)
                        for p in range(HP):
                            pe.transpose(bank[R, 5, p * P:(p + 1) * P], W1[:, 32 * p:32 * p + 32], ident[:])
                            ins = pe.transpose(bank[R, 6, p * P:(p + 1) * P], Q1[:, 32 * p:32 * p + 32], ident[:])
                        ins.then_inc(N["qs"], 1)
                    pe.wait_ge(N["vn"], C("vn") + 1)
                    for h in range(NH):
                        ins = pe.matmul(bank[R, 2, hc(h)], QK[:, hs(h)], vn[R, hc(h)], start=True, stop=True)
                    ins.then_inc(N["o2"], 1)
                    if not dec:
                        for h in range(NH):
                            ins = pe.matmul(bank[pr(h), 3, hc(h // 2)], ktail[R, hc(h)], vn[R, hc(h)], start=True, stop=True)
                        ins.then_inc(N["S"], 1)
                    else:
                        for a in range(2):
                            pe.wait_ge(N["vmr"], C("vmr") + a + 1)
                            for h in range(4 * a, 4 * a + 4):
                                ins = pe.matmul(bank[pr(h), (3, 4, 5, 7)[h // 2], :], ktail[R, hc(h)],
                                                vm[:, 512 * (h % 4):512 * (h % 4 + 1)], start=True, stop=True)
                            ins.then_inc(N["S"], 1)
                    pe.wait_ge(N["std"], C("std") + 2)
                    for p in range(HP):
                        ins = pe.transpose(bank[:, 0, p * n:(p + 1) * n], ob[R, p * P:(p + 1) * P], ident[R, 0:n])
                    ins.then_inc(N["oT"], 1)

                @block.scalar
                def _(act):
                    act.activation(sz, z_tok[R, ci, :], ACT.Sigmoid).then_inc(N["sz"], 1)
                    act.wait_ge(N["Gs"], C("Gs") + (3 if dec else 2))
                    act.activation(eG[R, 0:NH], Gs[R, 0:NH], ACT.Exp)
                    act.activation(eL[R, 0:NH], Gs[R, NH:2 * NH], ACT.Exp)
                    if dec:
                        act.activation(eGb, eGb, ACT.Exp)
                    act.activation(eT[R, 0:NH], eT[R, 0:NH], ACT.Exp).then_inc(N["exp"], 1)
                    act.wait_ge(N["dec"], C("dec") + 1)
                    act.activation(Y, Y, ACT.Exp).then_inc(N["exp"], 1)
                    act.wait_ge(N["dec"], C("dec") + 2)
                    act.activation(QK, QK, ACT.Exp).then_inc(N["exp"], 1)
                    act.wait_ge(N["TTp"], C("TTp") + 1)
                    act.activation(two(TT), rg(0), ACT.Copy).then_inc(N["TT"], 1)
                    for l in range(1, nlev):
                        for a in range(2):
                            act.wait_ge(N["Y"], C("Y") + 2 * (l - 1) + a + 1)
                            if l == 1 and a == 0:
                                act.wait_ge(N["L"], C("L") + 2)
                            if l > 1:
                                act.wait_ge(N["P"], C("P") + 2 * (l - 2) + a + 1)
                            act.activation(Y[:, half(a)], bank[R, 2 + a, 0:HP * n], ACT.Copy).then_inc(N["Ye"], 1)
                    act.wait_ge(N["wu"], C("wu") + 1)
                    if dec:
                        act.activation(WQ[:, :, :, 0:4], bank[:, 0, 0:HP * n].rearrange("p (h s i) -> p h s i", h=HP, s=NSEQ),
                                       ACT.Copy)
                        act.activation(WQ[:, :, :, 4:8], gq[:, 0:HP, SEQ:T].rearrange("p h (s i) -> p h s i", s=NSEQ),
                                       ACT.Copy).then_inc(N["wTe"], 1)
                        act.wait_ge(N["ws"], C("ws") + 1)
                        v = bank[:, 4, 0:256].rearrange("p (h s c) -> p h s c", h=HP, s=NSEQ)
                        act.activation(W1.rearrange("p (h s i) -> p h s i", h=HP, s=NSEQ), v[:, :, :, 0:4], ACT.Copy)
                        act.activation(Q1.rearrange("p (h s i) -> p h s i", h=HP, s=NSEQ), v[:, :, :, 4:8], ACT.Copy)\
                           .then_inc(N["ws"], 1)
                    else:
                        act.activation(wTb, bank[:, 0, :], ACT.Copy).then_inc(N["wTe"], 1)
                    act.wait_ge(N["ss"], C("ss") + 1)
                    act.activation(rs[R, 0:NH], ss[R, 0:NH], ACT.Sqrt, scale=1.0 / HD, bias=epst[R, 0:1]).then_inc(N["std"], 1)
                    act.wait_ge(N["oT"], C("oT") + 1)
                    act.activation(oT[:, 0:HP, toks(ci)], bank[:, 0, 0:HP * n].rearrange("p (h i) -> p h i", h=HP), ACT.Copy)

                @block.gpsimd
                def _(pool):
                    pool.wait_ge(N["T0"], C("T0") + 1)
                    for l in range(1, nlev):
                        for a in range(2):
                            if l > 1:
                                pool.wait_ge(N["Y"], C("Y") + 2 * (l - 2) + a + 1)
                            hh = slice(4 * a, 4 * a + 4)
                            pool.tensor_tensor(hv(Lm)[:, hh, :], hv(Lb)[:, hh, :],
                                               LVL[R, l, 0:n].unsqueeze(1).to_broadcast([n, 4, n]), ALU.mult)\
                                .then_inc(N["lm"], 1)

                @block.vector
                def _(dve):
                    c = Chain(dve, s_dve)
                    c.n = dve_n[0]
                    g = gg[R, ci, :]
                    if dec:
                        sm8 = SM[0:ND].rearrange("p (s j) -> p s j", j=NDEC)[:, :, 0]
                        dve.tensor_tensor(gm.rearrange("p (s h) -> p s h", s=NSEQ), g.unsqueeze(1).to_broadcast([ND, NSEQ, NH]),
                                          sm8.unsqueeze(2).to_broadcast([ND, NSEQ, NH]), ALU.mult)
                    dve.tensor_tensor(pv(Lm), mU.unsqueeze(1).unsqueeze(1).to_broadcast([n, 2, HP, n]), pb(g), ALU.mult).then_inc(N["gU"], 1)
                    dve.wait_ge(N["G"], C("G") + 1)
                    ins = dve.tensor_copy(Gs[R, :], bank[R, 6, 0:2 * NH])
                    if dec:
                        ins.then_inc(N["Gs"], 1)
                        ins = dve.tensor_copy(eGb, bank[:, 7, 0:64])
                    ins.then_inc(N["Gs"], 1)
                    dve.wait_ge(N["Gs"], C("Gs") + (2 if dec else 1))
                    dve.tensor_tensor(eT[R, 0:NH], Gs[R, NH:2 * NH], Gs[R, 0:NH], ALU.subtract).then_inc(N["Gs"], 1)
                    dve.wait_ge(N["R"], C("R") + 1)
                    c(dve.tensor_tensor(pv(Tb), rg(0).rearrange("p a (h i) -> p a h i", h=HP), pb(Gs[R, 0:NH]), ALU.subtract))
                    dve.scalar_tensor_tensor(out=hv(Y), in0=hv(Tb), scalar=-1.0, in1=bc(nS, n), op0=ALU.mult,
                                             op1=ALU.add).then_inc(N["dec"], 1)
                    dve.tensor_tensor(hv(QK), hv(Tb), bc(nU, n), ALU.add).then_inc(N["dec"], 1)
                    dve.wait_ge(N["exp"], C("exp") + 1)
                    c(dve.tensor_tensor(bG[R, 0:NH], bet[R, ci, :], eG[R, 0:NH], ALU.mult))
                    dve.wait_ge(N["kv"], C("kv") + 1)
                    hd = lambda v: v.rearrange("p (h d) -> p h d", h=NH)
                    dve.tensor_tensor(hd(kbg[R]), hd(bank[R, 6, :]), hb(bG[R, 0:NH], HD), ALU.mult)
                    dve.tensor_tensor(hd(ktail[R]), hd(bank[R, 6, :]), hb(eT[R, 0:NH], HD), ALU.mult)
                    dve.tensor_tensor(hd(vb[R]), hd(bank[R, 7, :]), hb(bet[R, ci, :], HD), ALU.mult).then_inc(N["kvused"], 1)
                    dve.wait_ge(N["kk"], C("kk") + 1)
                    dve.tensor_tensor(pv(Lb), rg(2).rearrange("p a (h i) -> p a h i", h=HP), pb(bet[R, ci, :]), ALU.mult).then_inc(N["L"], 1)
                    dve.wait_ge(N["L"], C("L") + 1)
                    dve.wait_ge(N["exp"], C("exp") + 2)
                    dve.tensor_tensor(Lb, Lb, Y, ALU.mult).then_inc(N["L"], 1)
                    dve.wait_ge(N["L"], C("L") + 2)
                    dve.wait_ge(N["R"], C("R") + 1)
                    c(dve.tensor_tensor(hv(Lm), hv(Lb), bc(LVL[R, 0, 0:n], n), ALU.mult))
                    dve.tensor_tensor(hv(Tb), bc(ident[R, 0:n], n), hv(Lm), ALU.subtract).then_inc(N["T0"], 1)
                    dve.wait_ge(N["qk"], C("qk") + 1)
                    dve.wait_ge(N["exp"], C("exp") + 3)
                    dve.tensor_tensor(two(QK), rg(4), two(QK), ALU.mult).then_inc(N["QK"], 1)
                    dve.wait_ge(N["TT"], C("TT") + 1)
                    for l in range(1, nlev):
                        for a in range(2):
                            dve.wait_ge(N["P"], C("P") + 2 * (l - 1) + a + 1)
                            if l < nlev - 1:
                                dve.tensor_tensor(Tb[:, half(a)], Tb[:, half(a)], bank[R, 4 + a, 0:HP * n], ALU.subtract)
                            dve.tensor_tensor(TT[:, half(a)], TT[:, half(a)], bank[R, 6 + a, 0:HP * n], ALU.subtract)\
                               .then_inc(N["Tn"], 1)
                            if l < nlev - 1:
                                dve.wait_ge(N["Tn"], C("Tn") + 2 * (l - 1) + a + 1)
                    dve.wait_ge(N["wu"], C("wu") + 1)
                    if ci == 0:
                        dve.tensor_copy(vn[R], bank[R, 1, :]).then_inc(N["vn"], 1)
                    else:
                        c(dve.tensor_copy(vn[R], bank[R, 1, :]))
                        dve.wait_ge(N["qs"], C("qs") + 1)
                        if dec:
                            dve.tensor_tensor(vn[R], vn[R], bank[R, 5, :], ALU.subtract).then_inc(N["vn"], 1)
                            c(dve.tensor_tensor(hd(ob[R]), hd(bank[R, 6, :]), hb(eG[R, 0:NH], HD), ALU.mult))
                        else:
                            for a in range(2):
                                par = lambda v: v.rearrange("p (h a d) -> p a h d", a=2, d=HD)[:, a]
                                ph = lambda b: bank[R, b + a, 0:HP * HD].rearrange("p (h d) -> p h d", h=HP)
                                ins = dve.tensor_tensor(par(vn[R]), par(vn[R]), ph(4), ALU.subtract)
                                ins2 = dve.tensor_tensor(par(ob[R]), ph(6), eG[R, a:NH:2].unsqueeze(2)
                                                         .to_broadcast([n, HP, HD]), ALU.mult)
                                if a:
                                    ins.then_inc(N["vn"], 1)
                                    c(ins2)
                    if dec:
                        dve.wait_ge(N["vn"], C("vn") + 1)
                        for a in range(2):
                            if a:
                                dve.wait_ge(N["S"], C("S") + 1)
                            dve.tensor_tensor(vm.rearrange("p (h s d) -> p h s d", h=4, s=NSEQ),
                                              vn[R, 256 * a:256 * a + 256].rearrange("p (h d) -> p h d", h=4).unsqueeze(2)
                                              .to_broadcast([ND, 4, NSEQ, HD]),
                                              sm8.unsqueeze(1).unsqueeze(3).to_broadcast([ND, 4, NSEQ, HD]), ALU.mult)\
                               .then_inc(N["vmr"], 1)
                    dve.wait_ge(N["o2"], C("o2") + 1)
                    if ci == 0:
                        c(dve.tensor_copy(ob[R], bank[R, 2, :]))
                    else:
                        c(dve.tensor_tensor(ob[R], ob[R], bank[R, 2, :], ALU.add))
                    osq = Lb[:, 0:GW] if not dec else vm[:, 0:GW]
                    if dec:
                        dve.wait_ge(N["S"], C("S") + 2)
                    c(dve.tensor_tensor(osq, ob[R], ob[R], ALU.mult))
                    dve.tensor_reduce(ss[R, 0:NH], hd(osq), AX.X, ALU.add).then_inc(N["ss"], 1)
                    dve.wait_ge(N["sz"], C("sz") + 1)
                    c(dve.tensor_tensor(sz, z_tok[R, ci, :], sz, ALU.mult))
                    c(dve.tensor_tensor(hd(sz), hd(sz), gnorm[R].unsqueeze(1).to_broadcast([n, NH, HD]), ALU.mult))
                    dve.wait_ge(N["std"], C("std") + 1)
                    c(dve.reciprocal(rs[R, 0:NH], rs[R, 0:NH]))
                    c(dve.tensor_tensor(hd(ob[R]), hd(ob[R]), hb(rs[R, 0:NH], HD), ALU.mult))
                    dve.tensor_tensor(ob[R], ob[R], sz, ALU.mult).then_inc(N["std"], 1)
                    dve.wait_ge(N["S"], C("S") + (2 if dec else 1))
                    if ci == 0:
                        dve.tensor_copy(St, bank[:, 3, 0:256].rearrange("p (h d) -> p h d", h=HP)).then_inc(N["St"], 1)
                    elif ci == 1:
                        dve.tensor_copy(eLs[0:HD, :], eL[0:HD, 0:NH:2])
                        c(dve.tensor_copy(eLs[HD:P, :], eL[HD:P, 1:NH:2]))
                        c(dve.tensor_tensor(St, St, eLs.unsqueeze(2).to_broadcast([P, HP, HD]), ALU.mult))
                        dve.tensor_tensor(St, St, bank[:, 3, 0:256].rearrange("p (h d) -> p h d", h=HP), ALU.add)\
                           .then_inc(N["St"], 1)
                    else:
                        v = eGb.rearrange("p (s h) -> p s h", s=NSEQ)
                        e = eGls.rearrange("p (s h) -> p s h", s=NSEQ)
                        dve.tensor_copy(e[0:HD], v[0:HD, :, 0:NH:2])
                        c(dve.tensor_copy(e[HD:P], v[HD:P, :, 1:NH:2]))
                        c(dve.tensor_tensor(S0.rearrange("p s h d -> p (s h) d"), S0.rearrange("p s h d -> p (s h) d"),
                                            eGls.unsqueeze(2).to_broadcast([P, NSEQ * HP, HD]), ALU.mult))
                        for p in range(HP):
                            ins = dve.tensor_tensor(S0[:, :, p, :], S0[:, :, p, :],
                                                    bank[:, (3, 4, 5, 7)[p], :].rearrange("p (s d) -> p s d", s=NSEQ), ALU.add)
                        ins.then_inc(N["St"], 1)
                    dve_n[0] = c.n

        for ci in range(3):
            gdn_chunk(ci)
        h2 = gq[:].rearrange("p a t -> p (a t)")[:, 0:3 * D].rearrange("p (t d) -> p t d", t=3)
        tab = gq[:].rearrange("p a t -> p (a t)")[:, 3 * D:]
        rk, gt = (tab[:, 102 * i:102 * (i + 1)].rearrange("p (t e) -> p t e", t=3) for i in range(2))
        iota = tab[:, 204:268]
        curP, curR, curG = (tab[:, 268 + 6 * i:274 + 6 * i].rearrange("p (t e) -> p t e", t=3) for i in range(3))
        npass = sb("npass", [1, 1], I32)
        rw, rbias = at(0, (KD, NE)), work[:, 256:288]
        s_rw = sem("router_loaded")
        s_wo, s_wor = sem("mixer_out"), sem("residual_added")
        with nc.Block() as block:
            @block.sync
            def _(sp):
                sp.dma_start(wb[:], norm_ffn[0].partition_broadcast(P)).then_inc(s_wb, 16)
                sp.dma_start(rw, router_w[0].rearrange("(k p) e -> p k e", p=P)).then_inc(s_rw, 16)
                sp.dma_start(rbias, router_b[0].partition_broadcast(P)).then_inc(s_rw, 16)
                for par in range(2):
                    sp.dma_start(ssm_prompt[0, 0].rearrange("(p two) k v -> two k p v", two=2)[par],
                                 St[HD * par:HD * par + HD]).then_inc(s_ssm, 16)
                    for s in range(NSEQ):
                        sp.dma_start(ssm_sample[0, s].rearrange("(p two) k v -> two k p v", two=2)[par],
                                     S0[HD * par:HD * par + HD, s]).then_inc(s_ssm, 16)
                sp.wait_ge(s_ringfree, U_END)
                for ch in range(8, NSLOT):
                    load_chunk(sp, 0, ch)

            @block.gpsimd
            def _(pool):
                pool.memset(h2[:, 2, :], 0.0)
                pool.memset(gt, 0.0)
                pool.memset(rk, -1.0e6)
                pool.iota(work[:, 300:364].bitcast(I32), pattern=[[1, CAP]], base=0, channel_multiplier=0)

            @block.tensor
            def _(pe):
                slot_wait(pe, U_WO)
                slot_wait(pe, U_WO + 2)
                for m in range(2):
                    w = slot(U_WO + 2 * m, 2).rearrange("p (k n) -> p k n", k=KD)
                    for t in range(3):
                        for k in range(KD):
                            ins = pe.matmul(bank[rows(t), 3 * m + t, :], oT[:, k, toks(t)], w[:, k, :], start=k == 0,
                                            stop=k == KD - 1)
                        ins.then_inc(s_wo, 1)
                pe.wait_ge(s_wo, 6)
                pe.sem_inc(s_ringfree, U_END - U_WO)

            @block.vector
            def _(dve):
                for m in range(2):
                    for t in range(3):
                        dve.wait_ge(s_wo, 3 * m + t + 1)
                        x = X[rows(t), t, 512 * m:512 * (m + 1)]
                        dve.tensor_tensor(x, x, bank[rows(t), 3 * m + t, :], ALU.add).then_inc(s_wor, 1)

        ffnnorm = Norm(1, lambda t: h2[rows(t), t, :], lambda e: e.wait_ge(s_wb, 32), True)
        with nc.Block() as block:
            @block.scalar
            def _(act):
                ffnnorm.scalar(act)

            @block.vector
            def _(dve):
                ffnnorm.vector(dve)

            @block.tensor
            def _(pe):
                ffnnorm.tensor(pe)

        lg, mk, ex, gtr, eq, ce = (at(400 + 96 * i, (3, NE)) for i in range(6))
        m8 = at(980, (3, 8))
        ng, nd, nm, gs, mc = (work[:, 1010 + 4 * i:1014 + 4 * i] for i in range(5))
        s_lg, s_nm, s_exp, s_mk, s_rank = (sem(n) for n in ("logits", "neg_top", "exps", "chosen", "ranks"))
        with nc.Block() as block:
            @block.sync
            def _(sp):
                sp.wait_ge(s_ssm, 32 + 256)

            @block.tensor
            def _(pe):
                pe.wait_ge(s_rw, 32)
                for t in range(3):
                    for k in range(KD):
                        ins = pe.matmul(bank[rows(t), t, 0:NE], hT[:, k, toks(t)], rw[:, k, :], start=k == 0, stop=k == KD - 1)
                ins.then_inc(s_lg, 1)
                pe.wait_ge(s_mk, 1)
                for t in range(3):
                    for u in range(t):
                        pe.matmul(bank[rows(t), 3 + t, 0:NE], ones[:, rows(t)], mk[:, u, :], start=u == 0, stop=False)
                    pe.matmul(bank[rows(t), 3 + t, 0:NE], Uinc[rows(t), rows(t)], mk[rows(t), t, :], start=t == 0, stop=True)
                for t in range(3):
                    ins = pe.matmul(bank[:, 6, 0:NE], ones[rows(t), :], mk[rows(t), t, :], start=t == 0, stop=t == 2)
                ins.then_inc(s_rank, 1)

            @block.scalar
            def _(act):
                act.wait_ge(s_nm, 1)
                for t in range(3):
                    ins = act.activation(ex[rows(t), t, :], lg[rows(t), t, :], ACT.Exp, bias=nm[rows(t), t:t + 1])
                ins.then_inc(s_exp, 1)

            @block.vector
            def _(dve):
                c = Chain(dve, s_dve)
                c.n = dve_n[0]
                dve.tensor_copy(iota, work[:, 300:364].bitcast(I32))
                dve.wait_ge(s_rw, 32)
                dve.wait_ge(s_lg, 1)
                for t in range(3):
                    r = rows(t)
                    c(dve.tensor_tensor(lg[r, t, :], bank[r, t, 0:NE], rbias[r], ALU.add))
                    c(dve.max(m8[r, t, :], lg[r, t, :]))
                    ins = dve.tensor_scalar(nm[r, t:t + 1], m8[r, t, 0:1], -1.0, None, ALU.mult)
                ins.then_inc(s_nm, 1)
                for t in range(3):
                    r = rows(t)
                    v4 = m8[r, t, TOPK - 1:TOPK]
                    dve.tensor_scalar(eq[r, t, :], lg[r, t, :], v4, None, ALU.is_equal)
                    c(dve.tensor_scalar(gtr[r, t, :], lg[r, t, :], v4, None, ALU.is_gt))
                    dve.tensor_reduce(ng[r, t:t + 1], gtr[r, t, :], AX.X, ALU.add)
                    c(dve.tensor_tensor_scan(ce[r, t, :], eq[r, t, :], eq[r, t, :], 0.0, ALU.add, ALU.bypass))
                    c(dve.tensor_scalar(nd[r, t:t + 1], ng[r, t:t + 1], -1.0, float(TOPK), ALU.mult, ALU.add))
                    c(dve.scalar_tensor_tensor(out=mk[r, t, :], in0=ce[r, t, :], scalar=nd[r, t:t + 1], in1=eq[r, t, :],
                                               op0=ALU.is_le, op1=ALU.mult))
                    ins = dve.tensor_tensor(mk[r, t, :], mk[r, t, :], gtr[r, t, :], ALU.add)
                ins.then_inc(s_mk, 1)
                dve.wait_ge(s_mk, 1)
                dve.wait_ge(s_exp, 1)
                for t in range(3):
                    r = rows(t)
                    c(dve.tensor_tensor(ex[r, t, :], ex[r, t, :], mk[r, t, :], ALU.mult))
                    c(dve.tensor_reduce(gs[r, t:t + 1], ex[r, t, :], AX.X, ALU.add))
                    c(dve.reciprocal(gs[r, t:t + 1], gs[r, t:t + 1]))
                    c(dve.tensor_scalar(gt[r, t, 0:NE], ex[r, t, :], gs[r, t:t + 1], None, ALU.mult))
                dve.tensor_copy(gt[:, :, NE:NE + 2], gt[:, :, 0:2])
                dve.wait_ge(s_rank, 1)
                for t in range(3):
                    r = rows(t)
                    c(dve.scalar_tensor_tensor(out=rk[r, t, 0:NE], in0=bank[r, 3 + t, 0:NE], scalar=1.0e6, in1=mk[r, t, :],
                                               op0=ALU.add, op1=ALU.mult))
                    c(dve.tensor_scalar(rk[r, t, 0:NE], rk[r, t, 0:NE], -1000001.0, None, ALU.add))
                dve.tensor_scalar(rk[:, :, NE:NE + 2], rk[:, :, 0:2], -float(CAP), None, ALU.add)
                c(dve.tensor_reduce(mc[:, 0:1], bank[:, 6, 0:NE], AX.X, ALU.max))
                c(dve.memset(mc[:, 1:2], 1.0))
                for k in range(1, -(-T // CAP)):
                    c(dve.scalar_tensor_tensor(out=mc[:, 1:2], in0=mc[:, 0:1], scalar=float(k * CAP), in1=mc[:, 1:2],
                                               op0=ALU.is_gt, op1=ALU.add))
                dve.tensor_copy(npass[:], mc[0:1, 1:2])
                dve_n[0] = c.n

        o_ = 0
        def take(n, parts=P):
            nonlocal o_
            o_ += n
            return work[0:parts, o_ - n:o_]
        xs, gb, ub, sg, ab, oo = take(D), take(512), take(512), take(512), take(D), take(D)
        xT = take(D).rearrange("p (k s) -> p k s", k=KD)
        aT = take(D).rearrange("p (k s) -> p k s", k=KD)
        PGT, Pm, PG = take(3 * P), take(3 * P), take(3 * P)
        bu, bd = take(D, 4), take(D, 2)
        bsel = take(4 * CAP, 4).rearrange("p (r s) -> p r s", r=4)
        assert o_ <= CONST_END
        names = ("P", "PG", "gathered", "x_copied", "xT_turned", "xT_copied", "up", "gate_clamped", "sigmoid", "act",
                 "aT_turned", "aT_copied", "out", "out_copied_act", "out_copied_dve", "PG_turned", "PGT_copied", "y",
                 "y_added", "dve_links", "bu_loaded", "bd_loaded", "bu_used", "bd_used", "ready")
        M = {k: sem("moe_" + k) for k in names}
        before = [slot_count(max(u for u in range(U_END) if (u + 10) % NSLOT == i)) for i in range(NSLOT)]
        K_DVE = 6

        def expert_loops(eng, body, after_pass=None):
            n = eng.value_load(npass[0:1, 0:1], min_val=1, max_val=-(-T // CAP))
            with eng.Fori(0, n) as p:
                with eng.Fori(0, NPAIR) as j:
                    body(p * NPAIR + j, j)
                if after_pass:
                    after_pass(p)
            return n

        with nc.Block() as block:
            @block.sync
            def _(sp):
                sp.dma_start(wb[:], norm_final.partition_broadcast(P)).then_inc(s_wb, 16)
                with sp.Fori(0, NPAIR - 1) as j:
                    for ch in range(12, CH):
                        sp.wait_ge(s_wused, CH * j + ch - 11)
                        load_chunk(sp, j, ch)
                    for ch in range(12):
                        sp.wait_ge(s_wused, CH * j + 12 + ch + 1)
                        load_chunk(sp, j + 1, ch)
                for ch in range(12, CH):
                    sp.wait_ge(s_wused, CH * (NPAIR - 1) + ch - 11)
                    load_chunk(sp, NPAIR - 1, ch)
                n = sp.value_load(npass[0:1, 0:1], min_val=1, max_val=-(-T // CAP))
                with sp.If(n > 1):
                    with sp.Fori(1, n) as p:
                        with sp.Fori(0, NPAIR) as j:
                            for ch in range(CH):
                                sp.wait_ge(s_wused, CH * (p * NPAIR + j) + ch - 11)
                                load_chunk(sp, j, ch)

            @block.gpsimd
            def _(pool):
                c = Chain(pool, s_pool)
                c.n = pool_n[0]
                c(pool.memset(bsel, 0.0))
                c(pool.affine_select(out=bsel, in_=bsel, pattern=[[1, 4], [0, CAP]], compare_op=ALU.not_equal, fill=1.0,
                                     base=0, channel_multiplier=-1))
                c(pool.memset(PGT, 0.0))
                pool.memset(oo, 0.0).then_inc(M["ready"], 1)
                pool_n[0] = c.n

                def body(i, j):
                    pool.wait_ge(M["bu_used"], i + 1)
                    pool.dma_start(bu, b_up[0, bass.ds(2 * j, 2), :].rearrange("e (h c) -> (e h) c", h=2))\
                        .then_inc(M["bu_loaded"], 16)
                    pool.wait_ge(M["bd_used"], i + 1)
                    pool.dma_start(bd, b_down[0, bass.ds(2 * j, 2), :]).then_inc(M["bd_loaded"], 16)
                expert_loops(pool, body)

            @block.tensor
            def _(pe):
                def gather(n):
                    pe.wait_ge(M["P"], n)
                    for t in range(3):
                        for m in range(2):
                            ins = pe.matmul(bank[:, 4 + m, :], Pm[:, t * P:(t + 1) * P], h2[:, t, 512 * m:512 * (m + 1)],
                                            start=t == 0, stop=t == 2)
                    ins.then_inc(M["gathered"], 1)

                def turn_x(n):
                    pe.wait_ge(M["x_copied"], n)
                    for k in range(KD):
                        ins = pe.transpose(bank[:, 7 - k // 4, (k % 4) * P:(k % 4 + 1) * P], xs[:, k * P:(k + 1) * P], ident[:])
                        if k % 4 == 3:
                            ins.then_inc(M["xT_turned"], 1)

                def combine(i):
                    pe.wait_ge(M["out_copied_act"], i + 1)
                    pe.wait_ge(M["out_copied_dve"], i + 1)
                    pe.wait_ge(M["PGT_copied"], i + 1)
                    for n in range(6):
                        t, m = n // 2, n % 2
                        if n >= 4:
                            pe.wait_ge(M["y_added"], 6 * i + n - 3)
                        pe.matmul(bank[rows(t), 4 + n % 4, :], PGT[:, t * P:t * P + ROWS[t]], oo[:, 512 * m:512 * (m + 1)],
                                  start=True, stop=True).then_inc(M["y"], 1)

                def products(i, b0, ch0, lhs, k0=0):
                    for kp in range(4):
                        for e in range(2):
                            ch = ch0 + 2 * kp + e
                            pe.wait_ge(s_slot[ch % NSLOT], 32 * i + (16 * (ch // NSLOT + 1) + before[ch % NSLOT]))
                        for kk in range(2):
                            k = 2 * kp + kk
                            for m in range(2):
                                for e in range(2):
                                    ch = ch0 + 2 * kp + e
                                    w = ring[:, (ch % NSLOT) * RSLOT + kk * D + 512 * m:(ch % NSLOT) * RSLOT + kk * D + 512 * (m + 1)]
                                    ins = pe.matmul(bank[CAP * e:CAP * e + CAP, b0 + m, :], lhs[:, k, CAP * e:CAP * e + CAP], w,
                                                    start=False, stop=k == KD - 1)
                                    if kk == 1 and m == 1:
                                        ins.then_inc(s_wused, 1)
                    return ins

                def up(i, half):
                    for m in range(2):
                        for e in range(2):
                            ins = pe.matmul(bank[CAP * e:CAP * e + CAP, 2 * half + m, :], bsel[0:4, 2 * e + half, :],
                                            bu[0:4, 512 * m:512 * (m + 1)], start=True, stop=False)
                    if half:
                        ins.then_inc(M["bu_used"], 1)
                    products(i, 2 * half, 8 * half, xT)

                def turn_act(i, half):
                    pe.wait_ge(M["act"], 2 * i + half + 1)
                    for k in range(4):
                        ins = pe.transpose(bank[:, 6, k * P:(k + 1) * P], ab[:, 512 * half + k * P:512 * half + (k + 1) * P], ident[:])
                    ins.then_inc(M["aT_turned"], 1)

                pe.sem_inc(M["bu_used"], 1)
                pe.sem_inc(M["bd_used"], 1)
                gather(1)
                turn_x(1)
                pe.wait_ge(M["ready"], 1)

                def body(i, j):
                    pe.wait_ge(M["bu_loaded"], 16 * i + 16)
                    pe.wait_ge(M["xT_copied"], 2 * i + 2)
                    up(i, 0)
                    combine(i)
                    up(i, 1)
                    pe.wait_ge(M["y_added"], 6 * i + 6)
                    turn_act(i, 0)
                    gather(i + 2)
                    pe.wait_ge(M["PG"], i + 1)
                    for t in range(3):
                        ins = pe.transpose(bank[:, 7, t * P:(t + 1) * P], PG[:, t * P:(t + 1) * P], ident[:])
                    ins.then_inc(M["PG_turned"], 1)
                    pe.wait_ge(M["aT_copied"], 2 * i + 1)
                    turn_act(i, 1)
                    pe.wait_ge(M["PGT_copied"], i + 2)
                    pe.wait_ge(M["aT_copied"], 2 * i + 2)
                    turn_x(i + 2)
                    pe.wait_ge(M["bd_loaded"], 16 * i + 16)
                    for m in range(2):
                        for e in range(2):
                            ins = pe.matmul(bank[CAP * e:CAP * e + CAP, 4 + m, :], bsel[0:2, e, :],
                                            bd[0:2, 512 * m:512 * (m + 1)], start=True, stop=False)
                    ins.then_inc(M["bd_used"], 1)
                    products(i, 4, 16, aT)
                n = expert_loops(pe, body)
                pe.wait_ge(M["xT_copied"], 2 * (n * NPAIR) + 2)
                combine(n * NPAIR)

            @block.scalar
            def _(act):
                def copy_x(n):
                    act.wait_ge(M["gathered"], n)
                    act.activation(xs, bank[:, 4:6, :].rearrange("p b n -> p (b n)"), ACT.Copy).then_inc(M["x_copied"], 1)

                def copy_xT(n):
                    for q in range(2):
                        act.wait_ge(M["xT_turned"], 2 * n - 1 + q)
                        act.activation(xT[:, 4 * q:4 * q + 4, :].rearrange("p k s -> p (k s)"), bank[:, 7 - q, :], ACT.Copy)\
                           .then_inc(M["xT_copied"], 1)

                act.sem_inc(M["out_copied_act"], 1)
                copy_x(1)
                copy_xT(1)

                def body(i, j):
                    def sigmoid(half):
                        act.wait_ge(M["gate_clamped"], 2 * i + half + 1)
                        act.activation(sg, gb, ACT.Sigmoid, scale=1.702).then_inc(M["sigmoid"], 1)

                    def copy_aT(half):
                        act.wait_ge(M["aT_turned"], 2 * i + half + 1)
                        act.activation(aT[:, 4 * half:4 * half + 4, :].rearrange("p k s -> p (k s)"), bank[:, 6, :], ACT.Copy)\
                           .then_inc(M["aT_copied"], 1)
                    sigmoid(0)
                    copy_aT(0)
                    sigmoid(1)
                    copy_x(i + 2)
                    copy_aT(1)
                    copy_xT(i + 2)
                    act.wait_ge(s_wused, CH * i + CH)
                    act.activation(oo[:, 0:512], bank[:, 4, :], ACT.Copy).then_inc(M["out_copied_act"], 1)
                expert_loops(act, body)

            @block.vector
            def _(dve):
                c = Chain(dve, M["dve_links"])

                def place(dst, cur, gate, col):
                    ins = dve.tensor_copy(cur, rk[:, :, bass.ds(col, 2)])
                    if gate is not None:
                        ins = dve.tensor_copy(gate, gt[:, :, bass.ds(col, 2)])
                    c(ins)
                    for t in range(3):
                        for e in range(2):
                            d = dst[:, t * P + CAP * e:t * P + CAP * e + CAP]
                            if gate is None:
                                ins = dve.tensor_scalar(d, iota, cur[:, t, e:e + 1], None, ALU.is_equal)
                            else:
                                ins = dve.tensor_scalar(d, iota, cur[:, t, e:e + 1], gate[:, t, e:e + 1], ALU.is_equal, ALU.mult)
                    return ins

                def add_y(i):
                    for n in range(6):
                        t, m = n // 2, n % 2
                        dve.wait_ge(M["y"], 6 * i + n + 1)
                        x = X[rows(t), t, 512 * m:512 * (m + 1)]
                        dve.tensor_tensor(x, x, bank[rows(t), 4 + n % 4, :], ALU.add).then_inc(M["y_added"], 1)

                place(Pm, curP, None, 0).then_inc(M["P"], 1)
                dve.sem_inc(M["out_copied_dve"], 1)
                dve.sem_inc(M["PGT_copied"], 1)
                n0 = c.n

                def body(i, j, p):
                    c.base, c.n = K_DVE * i + p + n0, 0
                    place(PG, curR, curG, 2 * j).then_inc(M["PG"], 1)
                    dve.wait_ge(M["gathered"], i + 1)
                    place(Pm, curP, None, 2 * j + 2).then_inc(M["P"], 1)

                    def activation(half):
                        dve.wait_ge(s_wused, CH * i + 8 * half + 8)
                        hu = bank[:, 2 * half:2 * half + 2, :].rearrange("p b (f two) -> p (b f) two", two=2)
                        dve.tensor_scalar(gb, hu[:, :, 0], 7.0, None, ALU.min).then_inc(M["gate_clamped"], 1)
                        c(dve.tensor_scalar(ub, hu[:, :, 1], 7.0, -7.0, ALU.min, ALU.max))
                        c(dve.scalar_tensor_tensor(out=ub, in0=ub, scalar=1.0, in1=gb, op0=ALU.add, op1=ALU.mult))
                        dve.wait_ge(M["sigmoid"], 2 * i + half + 1)
                        dve.tensor_tensor(ab[:, 512 * half:512 * (half + 1)], ub, sg, ALU.mult).then_inc(M["act"], 1)
                    activation(0)
                    add_y(i)
                    activation(1)
                    dve.wait_ge(M["PG_turned"], i + 1)
                    dve.tensor_copy(PGT, bank[:, 7, 0:3 * P]).then_inc(M["PGT_copied"], 1)
                    dve.wait_ge(s_wused, CH * i + CH)
                    dve.tensor_copy(oo[:, 512:D], bank[:, 5, :]).then_inc(M["out_copied_dve"], 1)
                    assert c.n == K_DVE, c.n

                nn = dve.value_load(npass[0:1, 0:1], min_val=1, max_val=-(-T // CAP))
                with dve.Fori(0, nn) as p:
                    with dve.Fori(0, NPAIR) as j:
                        body(p * NPAIR + j, j, p)
                    c.base, c.n = (K_DVE * NPAIR + 1) * p + K_DVE * NPAIR + n0, 0
                    c(dve.tensor_scalar(rk, rk, -float(CAP), None, ALU.add))
                add_y(nn * NPAIR)

        yrow = lambda t: work[rows(t), D * t:D * (t + 1)]
        s_yout = sem("y_stored")
        final = Norm(2, yrow, lambda e: e.wait_ge(s_wb, 48), False)
        with nc.Block() as block:
            @block.scalar
            def _(act):
                final.scalar(act)

            @block.vector
            def _(dve):
                final.vector(dve)

            @block.sync
            def _(sp):
                for t in range(2):
                    sp.wait_ge(s_nrow, final.base + t + 1)
                    sp.dma_start(y_prompt[0, toks(t), :], yrow(t)).then_inc(s_yout, 16)
                sp.wait_ge(s_nrow, final.base + 3)
                sp.dma_start(y_sample.rearrange("s i d -> (s i) d"), yrow(2)).then_inc(s_yout, 16)
                sp.wait_ge(s_yout, 48)


_INS = ['x_prompt', 'x_sample', 'cache_k', 'cache_v', 'page_table', 'state_conv', 'state_ssm', 'norm_mix', 'w_in', 'conv_w',
        'a_log', 'dt_bias', 'gdn_norm', 'sb_bias', 'w_out', 'norm_ffn', 'router_w', 'router_b', 'w_up', 'b_up', 'w_down',
        'b_down', 'norm_final']
_OUTS = [(1, SEQ, D), (NSEQ, NDEC, D), (1, 1, SEQ, NH, HD), (1, 1, SEQ, NH, HD), (1, 1, CONV - 1, CONVD),
         (1, 1, NH, HD, HD), (1, NSEQ, NDEC, NH, HD), (1, NSEQ, NDEC, NH, HD), (1, NSEQ, CONV - 1, CONVD),
         (1, NSEQ, NH, HD, HD)]


def kernel(**inputs):
    import concourse.bacc as bacc
    from concourse.bass_utils import run_bass_kernel_spmd

    nc = bacc.Bacc("TRN2", target_bir_lowering=False, num_devices=1)
    arrays, args = {}, []
    for name in _INS:
        a = np.ascontiguousarray(inputs[name])
        arrays[f"in_{name}"] = a
        args.append(nc.dram_tensor(f"in_{name}", a.shape, mybir.dt.from_np(a.dtype), kind="ExternalInput").ap())
    for i, shape in enumerate(_OUTS):
        args.append(nc.dram_tensor(f"out_{i}", shape, F32, kind="ExternalOutput").ap())
    build(nc, *args)
    r = run_bass_kernel_spmd(nc, [arrays], core_ids=[0])
    return tuple(r.results[0][f"out_{i}"] for i in range(len(_OUTS)))
```

```python
from contextlib import ExitStack

import numpy as np
import concourse.bass as bass
from concourse import mybir

F32 = mybir.dt.float32
I32 = mybir.dt.int32
ALU = mybir.AluOpType
ACT = mybir.ActivationFunctionType
AX = mybir.AxisListType

P = 128
D = 1024
KD = D // P
HD = 64
NH = 8
HP = NH // 2
GW = NH * HD
CONV = 4
NSEQ, NDEC = 8, 4
ND = NSEQ * NDEC
SEQ = 256
T = SEQ + ND
ROWS = [P, P, ND]
TOK0 = [0, P, 2 * P]
PAGE, NPG = 128, 8
PAST = PAGE * NPG
POOL = 80
NE, TOPK, FF = 32, 4, 1024
CAP = 64
RSLOT = 2048
NSLOT = 12
BIG = 1.0e30
EPS = 1e-6
SCALE = HD ** -0.5
CONVD = 3 * GW
WORK = 15900
C_Z, C_BA, C_S = CONVD, CONVD + GW, CONVD + GW + 2 * NH


class Chain:

    def __init__(self, eng, sem):
        self.eng, self.sem, self.n, self.base = eng, sem, 0, 0

    def __call__(self, ins):
        self.n += 1
        ins.then_inc(self.sem, 1)
        self.eng.wait_ge(self.sem, self.base + self.n)


def build(nc, x_prompt, x_sample, cache_k, cache_v, page_table, state_conv, state_ssm, norm_mix, w_in, conv_w,
          a_log, dt_bias, gdn_norm, sb_bias, w_out, norm_ffn, router_w, router_b, w_up, b_up, w_down, b_down,
          norm_final, y_prompt, y_sample, k_prompt, v_prompt, conv_prompt, ssm_prompt, k_sample, v_sample,
          conv_sample, ssm_sample):
    ctx = ExitStack()
    with ctx:
        def sb(name, shape, dt=F32):
            return ctx.enter_context(nc.sbuf_tensor(name, shape, dt))

        def sem(name):
            return ctx.enter_context(nc.semaphore(name))

        bank = ctx.enter_context(nc.psum_tensor("bank", [P, 8, 512], F32))

        ring = sb("ring", [P, NSLOT * RSLOT])
        X = sb("X", [P, 3, D])
        wb = sb("wb", [P, D])
        hT = sb("hT", [P, KD, T])
        oT = sb("oT", [P, KD, T])
        ident = sb("ident", [P, P])
        ones = sb("ones", [P, P])
        stat = sb("stat", [P, 3, 4])
        epst = sb("epst", [P, 2])
        work = sb("work", [P, WORK])

        def at(off, shape, parts=P):
            n = int(np.prod(shape))
            v = work[0:parts, off:off + n]
            if len(shape) == 2:
                v = v.rearrange("p (a b) -> p a b", a=shape[0])
            elif len(shape) == 3:
                v = v.rearrange("p (a b c) -> p a b c", a=shape[0], b=shape[1])
            return v

        def slot(u, n=1):
            i = (u + 10) % NSLOT
            return ring[:, i * RSLOT:(i + n) * RSLOT]

        def rows(t):
            return slice(0, ROWS[t])

        def toks(t):
            return slice(TOK0[t], TOK0[t] + ROWS[t])

        c0 = WORK
        def const(*shape):
            nonlocal c0
            c0 -= int(np.prod(shape))
            return at(c0, shape) if len(shape) > 1 else work[:, c0:c0 + shape[0]]

        Uinc = const(P)
        negS, negU = const(P), const(P)
        LVL = const(7, P)
        blk64 = const(P)
        SM = const(ND)
        dLst, dUinc, dneg, dnegU = const(ND), const(ND), const(ND), const(ND)
        E = const(2, P)
        Sel = const(2, 16)
        headmask = const(512)
        sel8, hch = const(P), const(512)
        sbcol, sbb, sbrow, nsbrow, nsbb = const(1), const(NH), const(1), const(1), const(NH)
        alog, dtb = const(NH), const(NH)
        gnorm = const(HD)
        convw = const(12, CONV)
        scT = const(12, 24)
        pt = work[0:1, c0 - 64:c0].bitcast(I32)
        c0 -= 64
        CONST_END = c0

        qsT, ksT = at(0, (HP, T)), at(HP * T, (HP, T))
        A1 = 2 * HP * T
        vs_tok, z_tok = at(A1, (3, GW)), at(A1 + 3 * GW, (3, GW))
        A2 = A1 + 6 * GW
        ba = at(A2, (3, 2 * NH))
        A2 += 48

        s_x = sem("x_loaded")
        s_small, s_small2 = sem("conv_state_loaded"), sem("small_loaded")
        s_wb = sem("norm_weight_loaded")
        s_pool = sem("pool_chain")
        s_act = sem("act_chain")
        s_dve = sem("dve_chain")
        s_slot = [sem(f"slot_loaded{i}") for i in range(NSLOT)]
        s_ringfree = sem("ring_used")
        s_ba_w = sem("ba_weights_loaded")
        wba = sb("wba", [P, KD, 2 * NH])
        scrow = work[0:24, 0:CONVD]
        cwrow = work[0:CONV, CONVD:2 * CONVD]

        w_in_v = w_in[0].rearrange("(k p) n -> p k n", p=P)
        w_out_v = w_out[0].rearrange("(k p) n -> p k n", p=P)
        GROUP_COL = [0, GW, 2 * GW, C_Z, C_S, C_S + GW, C_S + 2 * GW]

        U_C, U_WO, U_END = 14, 46, 50
        PGL = 4

        def slot_sem(u):
            return s_slot[(u + 10) % NSLOT]

        def slot_count(u):
            return sum(16 * (PGL if U_C <= v < U_WO else 1) for v in range(u % NSLOT, u + 1, NSLOT)
                       if U_C <= v < U_WO or v % 2 == 0)

        def slot_wait(eng, u):
            return eng.wait_ge(slot_sem(u), slot_count(u))

        def slot_free(eng, u, n):
            if u + n > NSLOT:
                eng.wait_ge(s_ringfree, u + n - NSLOT)

        def load_w_in(eng, n):
            slot_free(eng, 2 * n, 2)
            eng.dma_start(slot(2 * n, 2).rearrange("p (k n) -> p k n", k=KD),
                          w_in_v[:, :, GROUP_COL[n]:GROUP_COL[n] + GW]).then_inc(slot_sem(2 * n), 16)

        def load_cache(eng, m):
            g, kv, ph, s = m // 16, m // 8 % 2, m // 4 % 2, m % 4
            slot_free(eng, U_C + m, 1)
            for pg in range(PGL):
                col = NPG * (4 * g + s) + PGL * ph + pg
                page = eng.value_load(pt[0:1, col:col + 1], min_val=0, max_val=POOL - 1)
                eng.dma_start(slot(U_C + m)[:, pg * GW:(pg + 1) * GW],
                              (cache_k, cache_v)[kv][0, bass.ds(page, 1)].rearrange("o p h d -> (o p) (h d)"))\
                   .then_inc(slot_sem(U_C + m), 16)

        act_n, dve_n, pool_n = [0], [0], [0]

        s_nsq, s_nstd, s_nrow, s_ntp, s_nev = (
            sem(f"norm_{n}") for n in ("squares", "std", "rows", "turned", "copied"))

        class Norm:

            def __init__(self, nth, rowbuf, weight_wait, turned, ready=lambda e: None):
                self.rowbuf, self.weight_wait, self.turned, self.ready = rowbuf, weight_wait, turned, ready
                self.base = 3 * nth

            def scalar(self, act):
                self.ready(act)
                for t in range(3):
                    r = rows(t)
                    act.activation(self.rowbuf(t), X[r, t, :], ACT.Square, accum_out=stat[r, t, 0:1]).then_inc(s_nsq, 1)
                for t in range(3):
                    r = rows(t)
                    act.wait_ge(s_nsq, self.base + t + 1)
                    act.activation(stat[r, t, 1:2], stat[r, t, 0:1], ACT.Sqrt, scale=1.0 / D,
                                   bias=epst[r, 0:1]).then_inc(s_nstd, 1)
                if self.turned:
                    for t in range(3):
                        act.wait_ge(s_ntp, self.base + t + 1)
                        b = 2 * (t % 2)
                        n = ROWS[t]
                        act.activation(hT[:, :, toks(t)],
                                       bank[:, b:b + 2, :].rearrange("p b n -> p (b n)")[:, 0:KD * n]
                                       .rearrange("p (k n) -> p k n", k=KD), ACT.Copy).then_inc(s_nev, 1)

            def vector(self, dve):
                c = Chain(dve, s_dve)
                c.n = dve_n[0]
                self.weight_wait(dve)
                for t in range(3):
                    r = rows(t)
                    dve.wait_ge(s_nstd, self.base + t + 1)
                    c(dve.reciprocal(stat[r, t, 2:3], stat[r, t, 1:2]))
                    dve.scalar_tensor_tensor(out=self.rowbuf(t), in0=X[r, t, :], scalar=stat[r, t, 2:3], in1=wb[r, :],
                                             op0=ALU.mult, op1=ALU.mult).then_inc(s_nrow, 1)
                dve_n[0] = c.n

            def tensor(self, pe):
                for t in range(3):
                    pe.wait_ge(s_nrow, self.base + t + 1)
                    if t == 2:
                        pe.wait_ge(s_nev, self.base + 1)
                    b, n = 2 * (t % 2), ROWS[t]
                    dst = bank[:, b:b + 2, :].rearrange("p b n -> p (b n)")
                    for k in range(KD):
                        ins = pe.transpose(dst[:, k * n:(k + 1) * n], self.rowbuf(t)[:, k * P:(k + 1) * P],
                                           ident[0:n, 0:n])
                    ins.then_inc(s_ntp, 1)

        hrow = lambda t: work[rows(t), A2 + D * t:A2 + D * (t + 1)]
        s_id, s_t, s_zero = sem("identity_ready"), sem("turned"), sem("zeros_written")

        def x_ready(eng):
            eng.wait_ge(s_id, 1)
            eng.wait_ge(s_x, 32)
        mixnorm = Norm(0, hrow, lambda e: (e.wait_ge(s_wb, 16), x_ready(e)), True, x_ready)
        with nc.Block() as block:
            @block.sync
            def _(sp):
                sp.dma_start(X[:, 0:2, :], x_prompt[0].rearrange("(t p) d -> p t d", p=P)).then_inc(s_x, 16)
                sp.dma_start(X[0:ND, 2, :], x_sample.rearrange("s i d -> (s i) d")).then_inc(s_x, 16)
                sp.dma_start(wb[:], norm_mix[0].partition_broadcast(P)).then_inc(s_wb, 16)
                sp.dma_start(scrow, state_conv[0].rearrange("s w c -> (s w) c")).then_inc(s_small, 16)
                sp.dma_start(cwrow, conv_w[0]).then_inc(s_small, 16)
                for n in range(6):
                    load_w_in(sp, n)
                    if n == 0:
                        sp.dma_start(sbcol[0:NH, :], sb_bias.rearrange("o h -> h o")).then_inc(s_small2, 16)
                        sp.dma_start(sbb, sb_bias[0].partition_broadcast(P)).then_inc(s_small2, 16)
                        sp.dma_start(alog, a_log[0].partition_broadcast(P)).then_inc(s_small2, 16)
                        sp.dma_start(dtb, dt_bias[0].partition_broadcast(P)).then_inc(s_small2, 16)
                        sp.dma_start(gnorm, gdn_norm[0].partition_broadcast(P)).then_inc(s_small2, 16)
                        sp.dma_start(pt, page_table.rearrange("(o s) n -> o (s n)", o=1)).then_inc(s_small2, 16)
                        sp.dma_start(wba[:], w_in_v[:, :, C_BA:C_BA + 2 * NH]).then_inc(s_ba_w, 16)

            @block.gpsimd
            def _(pool):
                c = Chain(pool, s_pool)
                pool.memset(epst[:, 0:1], EPS)
                pool.memset(epst[:, 1:2], HD * EPS)
                c(pool.memset(ident[:], 0.0))
                pool.affine_select(out=ident[:], in_=ident[:], pattern=[[-1, P]], compare_op=ALU.not_equal, fill=1.0, base=0,
                                   channel_multiplier=1).then_inc(s_id, 1)
                c(pool.memset(ones[:], 1.0))
                pool_n[0] = c.n

            @block.scalar
            def _(act):
                mixnorm.scalar(act)

            @block.tensor
            def _(pe):
                pe.wait_ge(s_id, 1)
                pe.wait_ge(s_small, 32)
                for t in range(12):
                    pe.transpose(bank[:, 6, 24 * t:24 * t + 24], scrow[:, t * P:(t + 1) * P], ident[0:24, 0:24])
                    ins = pe.transpose(bank[:, 7, CONV * t:CONV * (t + 1)], cwrow[:, t * P:(t + 1) * P], ident[0:CONV, 0:CONV])
                ins.then_inc(s_t, 1)
                mixnorm.tensor(pe)

            @block.vector
            def _(dve):
                dve.memset(z_tok, 0.0)
                dve.memset(ba, 0.0)
                dve.wait_ge(s_t, 1)
                dve.tensor_copy(scT, bank[:, 6, 0:288].rearrange("p (a b) -> p a b", a=12))
                dve.tensor_copy(convw, bank[:, 7, 0:48].rearrange("p (a b) -> p a b", a=12))
                mixnorm.vector(dve)

        B0 = A2
        pad = [work[:, B0 + 316 * i:B0 + 316 * i + 315] for i in range(2)]
        B1 = B0 + 632
        turnT = [work[:, B1 + T * i:B1 + T * (i + 1)] for i in range(2)]
        B2 = B1 + 2 * T
        csig = work[:, B2:B2 + 2 * T].rearrange("p (b n) -> p b n", b=2)
        B3 = B2 + 2 * T
        cdec, cpro = work[0:NSEQ * 7, B3:B3 + CONVD], work[64:67, B3:B3 + CONVD]
        kst = at(B3 + CONVD, (3, GW))
        assert B3 + 2 * CONVD <= CONST_END
        gq = sb("gq", [P, 12, T])
        tiles = [("conv", j) for j in range(12)] + [("z", j) for j in range(4)] + \
                [("q", j) for j in range(4)] + [("k", j) for j in range(4)] + [("v", j) for j in range(4)] + [("ba", 0)]
        turned_tiles = [i for i, (kind, _) in enumerate(tiles) if kind in ("z", "k", "v", "ba")]
        s_pj, s_pje = sem("projected"), sem("projection_copied")
        s_tt, s_tte = sem("proj_turned"), sem("proj_turned_copied")
        s_cu, s_cue = sem("convstate_turned"), sem("convstate_copied")
        s_cv, s_sg, s_pb = sem("conv_summed"), sem("conv_sigmoid"), sem("conv_state_placed")
        s_cs = sem("conv_state_stored")
        s_kvout = sem("kv_stored")
        s_silu, s_masks = sem("conv_silu"), sem("masks_ready")

        def padx(i):
            return pad[i % 2][:, 3:259], pad[i % 2][:, 259:315].rearrange("p (s w) -> p s w", w=7)

        with nc.Block() as block:
            @block.sync
            def _(sp):
                load_w_in(sp, 6)
                sp.wait_ge(s_small2, 96)
                for m in range(NSLOT):
                    load_cache(sp, m)
                sp.wait_ge(s_cue, 3)
                for s in range(NSEQ):
                    sp.dma_start(conv_sample[0, s], cdec[7 * s + 4:7 * s + 7, :]).then_inc(s_cs, 16)
                sp.dma_start(conv_prompt[0, 0], cpro).then_inc(s_cs, 16)
                i_k = [turned_tiles.index(tiles.index(("k", 3))), turned_tiles.index(tiles.index(("v", 3)))]
                for i, (src, dp, ds_) in zip(i_k, ((kst, k_prompt, k_sample), (vs_tok, v_prompt, v_sample))):
                    sp.wait_ge(s_tte, i + 1)
                    sp.dma_start(dp[0, 0].rearrange("(t p) h d -> p t (h d)", p=P), src[:, 0:2, :]).then_inc(s_kvout, 16)
                    sp.dma_start(ds_[0].rearrange("s i h d -> (s i) (h d)"), src[0:ND, 2, :]).then_inc(s_kvout, 16)

            @block.tensor
            def _(pe):
                done_turn = [0]

                def turn(i):
                    kind, j = tiles[i]
                    if kind == "conv":
                        pe.wait_ge(s_pje, i + 1)
                        if j % 4 == 0 and j:
                            pe.wait_ge(s_cue, j // 4)
                        px, pd = padx(i)
                        pe.transpose(bank[0:3, 4, (j % 4) * P:(j % 4 + 1) * P], px[:, SEQ - 3:SEQ], ident[:])
                        pe.transpose(bank[0:NSEQ * 7, 5, (j % 4) * P:(j % 4 + 1) * P], pad[i % 2][:, 259:315],
                                     ident[:]).then_inc(s_cu, 1)
                    elif i in turned_tiles:
                        pe.wait_ge(s_pje, i + 1)
                        m = done_turn[0]
                        done_turn[0] += 1
                        if m >= 2:
                            pe.wait_ge(s_tte, m - 1)
                        n = 2 * NH if kind == "ba" else P
                        src = ksT[:, j, :] if kind == "k" else turnT[m % 2]
                        for t in range(3):
                            ins = pe.transpose(bank[rows(t), 2 + m % 2, t * P:t * P + n], src[0:n, toks(t)],
                                               ident[0:n, 0:n])
                        ins.then_inc(s_tt, 1)

                for i, (kind, j) in enumerate(tiles):
                    if i >= 2:
                        pe.wait_ge(s_pje, i - 1)
                    n = i // 4
                    if kind == "ba":
                        pe.wait_ge(s_ba_w, 16)
                    elif i % 4 == 0:
                        slot_wait(pe, 2 * n)
                    m = 2 * NH if kind == "ba" else P
                    w = wba[:] if kind == "ba" else slot(2 * n, 2).rearrange("p (k n) -> p k n", k=KD)[:, :, j % 4 * P:(j % 4 + 1) * P]
                    for k in range(KD):
                        ins = pe.matmul(bank[0:m, i % 2, 0:T], w[:, k, :], hT[:, k, :], start=k == 0, stop=k == KD - 1)
                    ins.then_inc(s_pj, 1)
                    if i % 4 == 3:
                        pe.wait_ge(s_pj, i + 1)
                        pe.sem_inc(s_ringfree, 2)
                    if i >= 1:
                        turn(i - 1)
                turn(len(tiles) - 1)
                pe.wait_ge(s_masks, 1)
                for g in range(2):
                    pe.transpose(bank[:, 6, 32 * g:32 * g + 32], E[0:ND, g, :], ident[0:ND, 0:ND])
                pe.matmul(bank[:, 7, :], sel8[0:NH, :], hch[0:NH, :], start=True, stop=True)
                pe.matmul(bank[:, 6, 64:65], sel8[0:NH, :], sbcol[0:NH, :], start=True, stop=True).then_inc(s_t, 1)

            @block.scalar
            def _(act):
                m = 0
                for i, (kind, j) in enumerate(tiles):
                    act.wait_ge(s_pj, i + 1)
                    src = bank[:, i % 2, 0:T]
                    if kind == "conv":
                        if i == 0:
                            act.wait_ge(s_pb, 1)
                        if i >= 2:
                            act.wait_ge(s_cv, i - 1)
                            act.wait_ge(s_cu, i - 1)
                        px, pd = padx(i)
                        act.activation(pd[:, :, 0:3], scT[:, i, :].rearrange("p (s w) -> p s w", w=3), ACT.Copy)
                        act.activation(px, src[:, 0:SEQ], ACT.Copy)
                        act.activation(pd[:, :, 3:7], src[:, SEQ:T].rearrange("p (s i) -> p s i", i=NDEC),
                                       ACT.Copy).then_inc(s_pje, 1)
                        if j >= 1:
                            act.wait_ge(s_cv, i)
                            if i >= 3:
                                act.wait_ge(s_silu, i - 2)
                            act.activation(csig[:, (i - 1) % 2, :], gq[:, i - 1, :], ACT.Sigmoid).then_inc(s_sg, 1)
                        continue
                    if i == 12:
                        act.wait_ge(s_cv, 12)
                        act.wait_ge(s_silu, 10)
                        act.activation(csig[:, 1, :], gq[:, 11, :], ACT.Sigmoid).then_inc(s_sg, 1)
                    if kind == "q":
                        dst = qsT[:, j, :]
                    elif kind == "k":
                        dst = ksT[:, j, :]
                        m += 1
                    else:
                        if m >= 2:
                            act.wait_ge(s_tt, m - 1)
                        dst = turnT[m % 2]
                        m += 1
                    n = 2 * NH if kind == "ba" else P
                    act.activation(dst[0:n, :], src[0:n, :], ACT.Copy).then_inc(s_pje, 1)

            @block.gpsimd
            def _(pool):
                c = Chain(pool, s_pool)
                c.n = pool_n[0]

                def keep(v, pattern, cmp, base, cm, fill=0.0):
                    c(pool.affine_select(out=v, in_=v, pattern=pattern, compare_op=cmp, fill=fill, base=base,
                                         channel_multiplier=cm))

                for m, v in ((Uinc, 1.0), (negS, 0.0), (negU, 0.0)):
                    c(pool.memset(m, v))
                keep(Uinc, [[1, P]], ALU.is_ge, 0, -1)
                keep(negS, [[-1, P]], ALU.is_gt, 0, 1, -BIG)
                keep(negU, [[1, P]], ALU.is_ge, 0, -1, -BIG)
                c(pool.memset(LVL, 0.0))
                for l in range(7):
                    b = 1 << l
                    nb = P // (2 * b)
                    v = LVL[:, l, :].rearrange("p (n h b) -> p n h b", h=2, b=b)[:, :, 0, :]
                    c(pool.memset(v, 1.0))
                    keep(v, [[-2 * b, nb], [0, b]], ALU.is_ge, -b, 1)
                    keep(v, [[2 * b, nb], [0, b]], ALU.is_ge, 2 * b - 1, -1)
                c(pool.memset(blk64, 0.0))
                c(pool.memset(blk64[0:HD, 0:HD], 1.0))
                c(pool.memset(blk64[HD:P, HD:P], 1.0))
                d = slice(0, ND)
                for m in (SM, dLst, dUinc):
                    c(pool.memset(m[d, :], 1.0))
                    v = m[d, :].rearrange("p (s j) -> p s j", j=NDEC)
                    keep(v, [[-NDEC, NSEQ], [0, NDEC]], ALU.is_ge, 0, 1)
                    keep(v, [[NDEC, NSEQ], [0, NDEC]], ALU.is_ge, NDEC - 1, -1)
                keep(dLst[d, :], [[-1, ND]], ALU.is_gt, 0, 1)
                keep(dUinc[d, :], [[1, ND]], ALU.is_ge, 0, -1)
                c(pool.tensor_scalar(dneg[d, :], dLst[d, :], 1.0, BIG, ALU.subtract, ALU.mult))
                c(pool.tensor_scalar(dnegU[d, :], dUinc[d, :], 1.0, BIG, ALU.subtract, ALU.mult))
                for g in range(2):
                    v = E[d, g, :].rearrange("p (s h i) -> p s h i", s=4, h=NH)
                    c(pool.memset(v, 0.0))
                    keep(v, [[NDEC, 4], [0, NH], [1, NDEC]], ALU.not_equal, 16 * g, -1, 1.0)
                c(pool.memset(sel8[0:NH, :], 0.0))
                keep(sel8[0:NH, :].rearrange("p (s h i) -> p s h i", s=4, h=NH), [[0, 4], [1, NH], [0, NDEC]],
                     ALU.not_equal, 0, -1, 1.0)
                c(pool.memset(hch[0:NH, :], 0.0))
                keep(hch[0:NH, :].rearrange("p (h c) -> p h c", c=HD), [[1, NH], [0, HD]], ALU.not_equal, 0, -1, 1.0)
                pool.wait_ge(s_small2, 96)
                pool.tensor_scalar(nsbb, sbb, -1.0, None, ALU.mult).then_inc(s_masks, 1)
                pool_n[0] = c.n

            @block.vector
            def _(dve):
                c = Chain(dve, s_dve)
                c.n = dve_n[0]
                state = {"m": 0}

                def conv(i):
                    dve.wait_ge(s_pje, i + 1)
                    px, pd = pad[i % 2], padx(i)[1]
                    op, od = gq[:, i, 0:SEQ], gq[:, i, SEQ:T].rearrange("p (s i) -> p s i", i=NDEC)
                    for w in range(CONV):
                        sp_, sd = px[:, w:w + SEQ], pd[:, :, w:w + NDEC]
                        sc = convw[:, i, w:w + 1]
                        if w == 0:
                            dve.tensor_scalar(op, sp_, sc, None, ALU.mult)
                            c(dve.tensor_scalar(od, sd, sc, None, ALU.mult))
                        else:
                            dve.scalar_tensor_tensor(out=op, in0=sp_, scalar=sc, in1=op, op0=ALU.mult, op1=ALU.add)
                            ins = dve.scalar_tensor_tensor(out=od, in0=sd, scalar=sc, in1=od, op0=ALU.mult, op1=ALU.add)
                            if w < CONV - 1:
                                c(ins)
                            else:
                                ins.then_inc(s_cv, 1)

                def silu(i):
                    dve.wait_ge(s_sg, i + 1)
                    dve.tensor_tensor(gq[:, i, :], gq[:, i, :], csig[:, i % 2, :], ALU.mult).then_inc(s_silu, 1)

                def turned(i):
                    kind, j = tiles[i]
                    m = state["m"]
                    state["m"] += 1
                    dve.wait_ge(s_tt, m + 1)
                    n = 2 * NH if kind == "ba" else P
                    dst = {"z": z_tok, "k": kst, "v": vs_tok, "ba": ba}[kind]
                    src = bank[:, 2 + m % 2, 0:3 * P].rearrange("p (t n) -> p t n", t=3)
                    dve.tensor_copy(dst[:, 0:2, j * P:j * P + n], src[:, 0:2, 0:n])
                    dve.tensor_copy(dst[0:ND, 2, j * P:j * P + n], src[0:ND, 2, 0:n]).then_inc(s_tte, 1)

                for i in range(2):
                    ins = dve.memset(pad[i][:, 0:3], 0.0)
                ins.then_inc(s_pb, 1)
                for i, (kind, j) in enumerate(tiles):
                    if kind == "conv":
                        conv(i)
                        if i:
                            silu(i - 1)
                        if j % 4 == 3:
                            dve.wait_ge(s_cu, j + 1)
                            cols = slice(512 * (j // 4), 512 * (j // 4 + 1))
                            dve.tensor_copy(cpro[:, cols], bank[0:3, 4, :])
                            dve.tensor_copy(cdec[:, cols], bank[0:NSEQ * 7, 5, :]).then_inc(s_cue, 1)
                    else:
                        if i == 12:
                            silu(11)
                        if i in turned_tiles:
                            turned(i)
                dve.wait_ge(s_t, 2)
                dve.tensor_copy(Sel[:, 0, :], bank[:, 6, 0:16])
                dve.tensor_copy(Sel[:, 1, :], bank[:, 6, 48:64])
                dve.tensor_copy(headmask, bank[:, 7, :])
                dve.tensor_copy(sbrow, bank[:, 6, 64:65])
                dve.tensor_scalar(nsbrow, bank[:, 6, 64:65], -1.0, None, ALU.mult)
                dve_n[0] = c.n


        NPAIR, CH = NE // 2, 24
        s_wused = sem("expert_chunk_used")

        def load_chunk(sp, j, ch):
            kp, e = (ch % 8) // 2, ch % 2
            src, col = (w_up, D * (ch // 8)) if ch < 16 else (w_down, 0)
            sp.dma_start(ring[:, (ch % NSLOT) * RSLOT:(ch % NSLOT + 1) * RSLOT].rearrange("p (k n) -> p k n", k=2),
                         src[0, bass.ds(2 * j + e, 1), 256 * kp:256 * kp + 256, col:col + D]
                         .rearrange("o (k p) n -> p (o k) n", p=P)).then_inc(s_slot[ch % NSLOT], 16)


        G = 4
        NK = PAST + ND
        KT = [hT[:].rearrange("p k t -> p (k t)")[:, 0:RSLOT].rearrange("p (s h k) -> p s h k", s=G, h=HP),
              work[:, A2:A2 + RSLOT].rearrange("p (s h k) -> p s h k", s=G, h=HP)]
        AT = work[:, A2:A2 + PAST].rearrange("p (g r) -> p g r", g=NPG)
        D1 = A2 + RSLOT
        beta, incl, rem = work[:, D1:D1 + NK], work[:, D1 + NK:D1 + 2 * NK + 1], work[:, D1 + 2 * NK + 1:D1 + 3 * NK + 1]
        D2 = D1 + 3 * NK + 1
        ATn, qbd = work[0:ND, D2:D2 + P], at(D2 + P, (HP, NSEQ, 32))
        om = rem[:, 0:GW]
        assert D2 + P + HP * NSEQ * 32 <= CONST_END
        sq, rt = oT[:, 0:2, :], oT[:, 2:4, :]
        gates = hT[:].rearrange("p k t -> p (k t)")[:, RSLOT:]
        bet, gg, xa, ax = (gates[:, 24 * i:24 * i + 24].rearrange("p (t h) -> p t h", t=3) for i in range(4))
        ea = gates[:, 96:104]
        s_sq, s_ss, s_rt = sem("squares"), sem("square_sums"), sem("roots")
        s_rc, s_l2p = sem("roots_inverted"), sem("l2_normed")
        s_ax, s_ex = sem("abs_a"), sem("log1p_a")
        s_qbd, s_kt, s_kta, s_ktd, s_sc, s_new = (sem(n) for n in (
            "query_blocks", "keys_turned", "keys_copied_act", "keys_copied_dve", "scores_done", "new_scores"))
        s_beta, s_A, s_AT, s_ATe, s_av, s_om, s_oT, s_oTe = (sem(n) for n in (
            "betas", "weights_A", "A_turned", "A_copied", "values_summed", "own_heads", "heads_turned", "heads_copied"))

        with nc.Block() as block:
            @block.sync
            def _(sp):
                for m in range(NSLOT, U_WO - U_C):
                    load_cache(sp, m)
                for m in range(2):
                    slot_free(sp, U_WO + 2 * m, 2)
                    sp.dma_start(slot(U_WO + 2 * m, 2).rearrange("p (k n) -> p k n", k=KD),
                                 w_out_v[:, :, m * 512:(m + 1) * 512]).then_inc(slot_sem(U_WO + 2 * m), 16)
                sp.wait_ge(s_ringfree, U_WO)
                for ch in range(5, 8):
                    load_chunk(sp, 0, ch)

            @block.gpsimd
            def _(pool):
                for i in range(9):
                    if i < 8:
                        if i >= 2:
                            pool.wait_ge(s_ss, i - 1)
                        pool.tensor_tensor(sq[:, i % 2, :], gq[:, i, :], gq[:, i, :], ALU.mult).then_inc(s_sq, 1)
                    if i >= 1:
                        k = i - 1
                        pool.wait_ge(s_rc, k + 1)
                        pool.tensor_tensor(gq[:, k, :], gq[:, k, :], rt[:, k % 2, :], ALU.mult).then_inc(s_l2p, 1)

            @block.tensor
            def _(pe):
                def turn_keys(g, pg):
                    q = NPG * g + pg
                    if q >= 1:
                        pe.wait_ge(s_kta, q)
                        pe.wait_ge(s_ktd, q)
                    if g == 1 and pg == 0:
                        pe.wait_ge(s_ATe, 1)
                    for s in range(G):
                        u = U_C + 16 * g + 4 * (pg // PGL) + s
                        if pg % PGL == 0:
                            slot_wait(pe, u)
                        for p in range(HP):
                            ins = pe.transpose(bank[:, 1 + s, p * P:(p + 1) * P],
                                               slot(u)[:, pg % PGL * GW + p * P:pg % PGL * GW + (p + 1) * P], ident[:])
                    ins.then_inc(s_kt, 1)
                    if pg % PGL == PGL - 1:
                        pe.wait_ge(s_kt, q + 1)
                        pe.sem_inc(s_ringfree, G)

                def scores(g, pg):
                    q = NPG * g + pg
                    pe.wait_ge(s_kta, q + 1)
                    pe.wait_ge(s_ktd, q + 1)
                    if g == 1 and pg == 0:
                        pe.wait_ge(s_beta, 1)
                    c = (pg % 4) * PAGE
                    for p in range(HP):
                        for s in range(G):
                            ins = pe.matmul(bank[32 * s:32 * s + 32, 6 + pg // 4, c:c + PAGE], qbd[:, p, G * g + s, :],
                                            KT[q % 2][:, s, p, :], start=p == 0, stop=p == HP - 1)
                    ins.then_inc(s_sc, 1)

                pe.wait_ge(s_qbd, 1)
                for g in range(2):
                    if g == 1:
                        pe.wait_ge(s_oTe, 1)
                    for p in range(HP):
                        for s in range(G):
                            pe.matmul(bank[32 * s:32 * s + 32, 0, 0:ND], qbd[:, p, G * g + s, :], ksT[:, p, SEQ:T],
                                      start=p == 0, stop=False, skip_group_check=True)
                    pe.matmul(bank[:, 0, 0:ND], E[0:ND, g, :], dneg[0:ND, :], start=False, stop=True,
                              skip_group_check=True).then_inc(s_new, 1)
                    for pg in range(NPG):
                        turn_keys(g, pg)
                        if pg:
                            scores(g, pg - 1)
                        if g == 0:
                            pe.wait_ge(s_sq, pg + 1)
                            if pg:
                                pe.wait_ge(s_rt, pg)
                            pe.matmul(bank[:, 0, P:P + T], blk64, sq[:, pg % 2, :], start=True, stop=True).then_inc(s_ss, 1)
                    scores(g, NPG - 1)
                    pe.wait_ge(s_A, g + 1)
                    for pg in range(NPG):
                        pe.transpose(bank[:, 1 + pg // 4, (pg % 4) * P:(pg % 4 + 1) * P], beta[:, pg * PAGE:(pg + 1) * PAGE],
                                     ident[:])
                    pe.transpose(bank[0:ND, 3, 0:P], beta[:, PAST:NK], ident[:]).then_inc(s_AT, 1)
                    pe.wait_ge(s_ATe, g + 1)
                    if g == 1:
                        pe.wait_ge(s_om, 1)
                    for ph in range(2):
                        for s in range(G):
                            slot_wait(pe, U_C + 16 * g + 8 + 4 * ph + s)
                        for pg in range(PGL):
                            for s in range(G):
                                ins = pe.matmul(bank[32 * s:32 * s + 32, 5, :], AT[:, PGL * ph + pg, 32 * s:32 * s + 32],
                                                slot(U_C + 16 * g + 8 + 4 * ph + s)[:, pg * GW:(pg + 1) * GW],
                                                start=ph == 0 and pg == 0, stop=False)
                        if ph == 0:
                            ins.then_inc(s_av, 1)
                            pe.wait_ge(s_av, 2 * g + 1)
                            pe.sem_inc(s_ringfree, G)
                    for s in range(G):
                        ins = pe.matmul(bank[32 * s:32 * s + 32, 5, :], ATn[:, 32 * s:32 * s + 32], vs_tok[0:ND, 2, :],
                                        start=False, stop=True)
                    ins.then_inc(s_av, 1)
                    pe.wait_ge(s_av, 2 * g + 2)
                    pe.sem_inc(s_ringfree, G)
                    pe.wait_ge(s_om, g + 1)
                    for p in range(HP):
                        ins = pe.matmul(bank[:, 0, 64 + 16 * p:80 + 16 * p], om[:, p * P:(p + 1) * P], Sel[:, g, :],
                                        start=True, stop=True)
                    ins.then_inc(s_oT, 1)

            @block.scalar
            def _(act):
                c = Chain(act, s_act)
                c.n = act_n[0]
                act.activation(bet, ba[:, :, 0:NH], ACT.Sigmoid)
                act.activation(ea, alog, ACT.Exp)
                act.wait_ge(s_ax, 1)
                c(act.activation(ax, ax, ACT.Exp))
                act.activation(ax, ax, ACT.Ln, bias=ones[:, 0:1]).then_inc(s_ex, 1)
                act_n[0] = c.n
                for g in range(2):
                    for pg in range(NPG):
                        q = NPG * g + pg
                        act.wait_ge(s_kt, q + 1)
                        if q >= 2:
                            act.wait_ge(s_sc, q - 1)
                        if q == 9:
                            act.wait_ge(s_av, 2)
                        if q == 1:
                            act.wait_ge(s_cs, 16 * 9)
                        act.activation(KT[q % 2][:, 0:2, :, :].rearrange("p s h k -> p (s h k)"),
                                       bank[:, 1:3, :].rearrange("p b n -> p (b n)"), ACT.Copy).then_inc(s_kta, 1)
                        if g == 0:
                            act.wait_ge(s_ss, pg + 1)
                            if pg >= 2:
                                act.wait_ge(s_l2p, pg - 1)
                            act.activation(rt[:, pg % 2, :], bank[:, 0, P:P + T], ACT.Sqrt, scale=float(HD) if pg < HP else 1.0,
                                           bias=epst[:, 1:2] if pg < HP else epst[:, 0:1]).then_inc(s_rt, 1)
                    act.wait_ge(s_sc, NPG * (g + 1))
                    act.wait_ge(s_new, g + 1)
                    if g == 0:
                        act.wait_ge(s_kvout, 64)
                    else:
                        act.wait_ge(s_AT, 1)
                        act.wait_ge(s_oT, 1)
                    z = bank[:, 6:8, :].rearrange("p b n -> p (b n)")
                    act.activation(rem[:, 0:PAST], z, ACT.Sigmoid, scale=-SCALE, bias=nsbrow)
                    act.activation(rem[:, PAST:NK], bank[:, 0, 0:ND], ACT.Sigmoid, scale=-SCALE, bias=nsbrow)
                    act.activation(beta[:, 0:PAST], z, ACT.Sigmoid, scale=SCALE, bias=sbrow)
                    act.activation(beta[:, PAST:NK], bank[:, 0, 0:ND], ACT.Sigmoid, scale=SCALE, bias=sbrow)\
                       .then_inc(s_beta, 1)
                    act.wait_ge(s_oT, g + 1)
                    act.activation(oT[:, HP:KD, SEQ + 16 * g:SEQ + 16 * g + 16],
                                   bank[:, 0, 64:128].rearrange("p (h c) -> p h c", h=HP), ACT.Copy).then_inc(s_oTe, 1)

            @block.vector
            def _(dve):
                c = Chain(dve, s_dve)
                c.n = dve_n[0]
                c(dve.tensor_tensor(xa, ba[:, :, NH:2 * NH], dtb.unsqueeze(1).to_broadcast([P, 3, NH]), ALU.add))
                dve.scalar_tensor_tensor(out=ax, in0=xa, scalar=-1.0, in1=xa, op0=ALU.mult, op1=ALU.min).then_inc(s_ax, 1)
                c(dve.memset(qbd, 0.0))
                for p in range(HP):
                    for half in range(2):
                        r, col = slice(HD * half, HD * half + HD), NDEC * (2 * p + half)
                        ins = dve.tensor_copy(qbd[r, p, :, col:col + NDEC],
                                              qsT[r, p, SEQ:T].rearrange("p (s i) -> p s i", i=NDEC))
                ins.then_inc(s_qbd, 1)
                dve.wait_ge(s_ex, 1)
                c(dve.scalar_tensor_tensor(out=gg, in0=xa, scalar=0.0, in1=ax, op0=ALU.max, op1=ALU.add))
                c(dve.scalar_tensor_tensor(out=gg, in0=gg, scalar=-1.0, in1=ea.unsqueeze(1).to_broadcast([P, 3, NH]),
                                           op0=ALU.mult, op1=ALU.mult))

                def invert_root(i):
                    dve.wait_ge(s_rt, i + 1)
                    dve.reciprocal(rt[:, i % 2, :], rt[:, i % 2, :]).then_inc(s_rc, 1)

                for g in range(2):
                    for pg in range(NPG):
                        q = NPG * g + pg
                        if 2 <= q < NPG + 2:
                            invert_root(q - 2)
                        dve.wait_ge(s_kt, q + 1)
                        if q >= 2:
                            dve.wait_ge(s_sc, q - 1)
                        if q == 9:
                            dve.wait_ge(s_av, 2)
                        if q == 1:
                            dve.wait_ge(s_cs, 16 * 9)
                        dve.tensor_copy(KT[q % 2][:, 2:4, :, :].rearrange("p s h k -> p (s h k)"),
                                        bank[:, 3:5, :].rearrange("p b n -> p (b n)")).then_inc(s_ktd, 1)
                    dve.wait_ge(s_beta, g + 1)
                    if g == 0:
                        c(dve.memset(incl[:, NK:NK + 1], 1.0))
                    c(dve.tensor_tensor_scan(incl[:, 0:NK][:, ::-1], rem[:, ::-1], rem[:, ::-1], 1.0, ALU.mult, ALU.bypass))
                    dve.tensor_tensor(beta, beta, incl[:, 1:NK + 1], ALU.mult).then_inc(s_A, 1)
                    dve.wait_ge(s_AT, g + 1)
                    dve.wait_ge(s_sc, NPG * (g + 1))
                    dve.tensor_copy(AT.rearrange("p g r -> p (g r)"), bank[:, 1:3, :].rearrange("p b n -> p (b n)"))
                    dve.tensor_copy(ATn, bank[0:ND, 3, 0:P]).then_inc(s_ATe, 1)
                    dve.wait_ge(s_av, 2 * g + 2)
                    dve.tensor_tensor(om, bank[:, 5, :], headmask, ALU.mult).then_inc(s_om, 1)
                dve_n[0] = c.n

        W3 = 3 * P
        pbeta = [work[:, A2 + W3 * i:A2 + W3 * (i + 1)] for i in range(2)]
        prem = [work[:, A2 + W3 * (2 + i):A2 + W3 * (3 + i)] for i in range(2)]
        D3 = A2 + 4 * W3
        pincl = [work[:, D3 + 386 * i:D3 + 386 * (i + 1)] for i in range(2)]
        D4 = D3 + 772
        pAT = [work[:, D4 + W3 * i:D4 + W3 * (i + 1)] for i in range(2)]
        assert D4 + 2 * W3 <= CONST_END
        s_pz, s_pbeta, s_pA, s_pAT, s_pATe, s_po, s_poe = (sem(n) for n in (
            "prompt_scores", "prompt_betas", "prompt_A", "prompt_A_turned", "prompt_A_copied", "prompt_heads",
            "prompt_heads_copied"))
        with nc.Block() as block:
            @block.tensor
            def _(pe):
                def scores(h):
                    p, r = h // 2, slice(HD * (h % 2), HD * (h % 2) + HD)
                    if h >= 2:
                        pe.wait_ge(s_pbeta, h - 1)
                    z = bank[:, h % 2, :]
                    pe.matmul(z[:, 0:P], qsT[r, p, 0:P], ksT[r, p, 0:P], start=True, stop=False, skip_group_check=True)
                    pe.matmul(z[:, 0:P], ident[:], negS, start=False, stop=True, skip_group_check=True)
                    pe.matmul(z[:, P:W3], qsT[r, p, P:SEQ], ksT[r, p, 0:SEQ], start=True, stop=False, skip_group_check=True)
                    pe.matmul(z[:, 2 * P:W3], ident[:], negS, start=False, stop=True, skip_group_check=True)\
                      .then_inc(s_pz, 1)

                def turn(h):
                    pe.wait_ge(s_pA, h + 1)
                    if h >= 2:
                        pe.wait_ge(s_pATe, h - 1)
                    for b in range(3):
                        ins = pe.transpose(bank[:, 2 + h % 2, b * P:(b + 1) * P], pbeta[h % 2][:, b * P:(b + 1) * P], ident[:])
                    ins.then_inc(s_pAT, 1)

                def values(h):
                    pe.wait_ge(s_pATe, h + 1)
                    if h >= 4 and h % 2 == 0:
                        pe.wait_ge(s_poe, h // 2 - 1)
                    r = slice(HD * (h % 2), HD * (h % 2) + HD)
                    o = bank[r, 4 + (h // 2) % 2, :]
                    a = pAT[h % 2]
                    hc = slice(HD * h, HD * h + HD)
                    pe.matmul(o[:, 0:P], vs_tok[:, 0, hc], a[:, 0:P], start=True, stop=True)
                    pe.matmul(o[:, P:SEQ], vs_tok[:, 0, hc], a[:, P:2 * P], start=True, stop=False)
                    pe.matmul(o[:, P:SEQ], vs_tok[:, 1, hc], a[:, 2 * P:W3], start=False, stop=True).then_inc(s_po, 1)

                scores(0)
                for h in range(NH):
                    if h + 1 < NH:
                        scores(h + 1)
                    turn(h)
                    if h:
                        values(h - 1)
                values(NH - 1)

            @block.scalar
            def _(act):
                for h in range(NH):
                    act.wait_ge(s_pz, h + 1)
                    if h >= 2:
                        act.wait_ge(s_pAT, h - 1)
                    act.activation(prem[h % 2], bank[:, h % 2, 0:W3], ACT.Sigmoid, scale=-SCALE, bias=nsbb[:, h:h + 1])
                    act.activation(pbeta[h % 2], bank[:, h % 2, 0:W3], ACT.Sigmoid, scale=SCALE, bias=sbb[:, h:h + 1])\
                       .then_inc(s_pbeta, 1)
                    if h >= 1:
                        act.wait_ge(s_pAT, h)
                        if h >= 3:
                            act.wait_ge(s_po, h - 2)
                        act.activation(pAT[(h - 1) % 2], bank[:, 2 + (h - 1) % 2, 0:W3], ACT.Copy).then_inc(s_pATe, 1)
                act.wait_ge(s_pAT, NH)
                act.wait_ge(s_po, NH - 2)
                act.activation(pAT[(NH - 1) % 2], bank[:, 2 + (NH - 1) % 2, 0:W3], ACT.Copy).then_inc(s_pATe, 1)

            def copy_heads(dve, p):
                dve.wait_ge(s_po, 2 * p + 2)
                dve.tensor_copy(oT[:, HP + p, 0:SEQ], bank[:, 4 + p % 2, 0:SEQ]).then_inc(s_poe, 1)

            @block.vector
            def _(dve):
                c = Chain(dve, s_dve)
                c.n = dve_n[0]
                for i in range(2):
                    for col in (P, 385):
                        ins = dve.memset(pincl[i][:, col:col + 1], 1.0)
                c(ins)
                for h in range(NH):
                    dve.wait_ge(s_pbeta, h + 1)
                    b, m, i = pbeta[h % 2], prem[h % 2], pincl[h % 2]
                    dve.tensor_tensor_scan(i[:, 0:P][:, ::-1], m[:, 0:P][:, ::-1], m[:, 0:P][:, ::-1], 1.0, ALU.mult, ALU.bypass)
                    c(dve.tensor_tensor_scan(i[:, 129:385][:, ::-1], m[:, P:W3][:, ::-1], m[:, P:W3][:, ::-1], 1.0, ALU.mult,
                                             ALU.bypass))
                    dve.tensor_tensor(b[:, 0:P], b[:, 0:P], i[:, 1:P + 1], ALU.mult)
                    dve.tensor_tensor(b[:, P:W3], b[:, P:W3], i[:, 130:386], ALU.mult).then_inc(s_pA, 1)
                    if h % 2 == 1:
                        if h >= 3:
                            copy_heads(dve, h // 2 - 1)
                copy_heads(dve, HP - 1)
                dve_n[0] = c.n

        S1 = 3328

        wTb = work[:, 2560:3072]
        St = at(3072, (HP, HD))
        S0 = at(A2 + 2048, (NSEQ, HP, HD))
        eLs = work[:, S1 + 216:S1 + 220]
        s_ssm = sem("ssm_stored")
        s_s0 = sem("ssm_loaded")

        N = {k: sem(f"gdn_{k}") for k in (
            "gU", "G", "Gs", "R", "kv", "kvused", "kk", "qk", "dec", "exp", "L", "QK", "lm", "T0", "TTp",
            "TT", "Y", "Ye", "P", "Tn", "wu", "wTe", "vn", "qs", "o2", "S", "ss", "std", "oT", "sz", "ws", "vmr", "St")}

        class GdnChunk:

            def __init__(self, ci):
                self.ci, self.n, self.dec = ci, ROWS[ci], ci == 2
                n, dec = self.n, self.dec
                self.R = R = slice(0, n)
                self.w = NH * n
                stp = self.w if dec else 1024
                if ci == 1:
                    base, o1, o2 = ring, 0, 6 * 1024
                else:
                    base, o1, o2 = work, A2, 0
                self.Lb, self.Lm, self.Tb, self.TT, self.Y, self.QK = (
                    base[R, o1 + stp * i:o1 + stp * i + self.w] for i in range(6))
                self.kbg, self.vb, self.ktail, self.vn, self.ob = (
                    base[:, o2 + 512 * i:o2 + 512 * (i + 1)] for i in range(5))
                D0 = o1 + 6 * stp
                self.sz = base[R, o2 + 2560:o2 + 3072] if ci == 1 else work[R, D0:D0 + GW]
                sm = o2 + 3072 if ci == 1 else S1 + 104
                self.Gs, self.eG, self.eL, self.eT, self.bG, self.ss, self.rs = (
                    base[:, sm + 16 * i:sm + 16 * i + 16] for i in range(7))
                if dec:
                    self.vm = work[0:ND, D0 + 2560:D0 + 4608]
                    self.WQ = work[:, D0 + 4608:D0 + 4864].rearrange("p (h s c) -> p h s c", h=HP, s=NSEQ)
                    self.W1, self.Q1 = (work[:, D0 + 4864 + P * i:D0 + 4864 + P * (i + 1)] for i in range(2))
                    self.gm, self.eGb, self.eGls = (work[0:ND, 3840 - 264:3840 - 200], work[:, 3840 - 200:3840 - 136],
                                                    work[:, 3840 - 136:3840 - 104])
                else:
                    assert D0 + GW <= CONST_END or ci == 1
                self.mU, self.nU, self.nS, self.mAll = (dUinc[R], dnegU[R], dneg[R], SM[R]) if dec else \
                    (Uinc, negU, negS, ones[:])
                self.nlev = 2 if dec else 7
                self.bU, self.bWS, self.bQS, self.bO, self.bS = ((2, None, None, 5, 4), (1, 6, 2, 0, 4), (1, 5, 6, 2, 3))[ci]

            STEPS = {"Gs": (2, 2, 3), "dec": (2, 2, 2), "exp": (3, 3, 3), "L": (2, 2, 2), "qs": (0, 1, 1), "S": (1, 1, 2),
                     "std": (2, 2, 2), "ws": (0, 0, 2), "vmr": (0, 0, 2), "wTe": (0, 1, 1)}

            def at(self, k, i=1):
                return sum(self.STEPS.get(k, (1, 1, 1))[:self.ci]) + i

            def lev(self, l, a):
                return 24 + a + 1 if self.dec else 4 * (l - 1) + 2 * self.ci + a + 1

            def hv(self, v):
                return v.rearrange("p (h i) -> p h i", h=NH)

            def bc(self, m):
                return m.unsqueeze(1).to_broadcast([self.n, NH, self.n])

            def hb(self, v):
                return v.unsqueeze(2).to_broadcast([self.n, NH, HD])

            def pv(self, v):
                return v.rearrange("p (a h i) -> p a h i", a=2, h=HP)

            def pb(self, v):
                return v.rearrange("p (h a) -> p a h", a=2).unsqueeze(3).to_broadcast([self.n, 2, HP, self.n])

            def rg(self, b):
                return bank[self.R, b:b + 2, 0:HP * self.n]

            def one(self, b, h):
                return bank[self.R, b, (h // 2) * self.n:(h // 2 + 1) * self.n]

            def hs(self, h):
                o = ((h % 2) * HP + h // 2) * self.n
                return slice(o, o + self.n)

            def half(self, a):
                return slice(HP * self.n * a, HP * self.n * (a + 1))

            def pe_setup(self, pe):
                ci, R, n = self.ci, self.R, self.n
                if ci == 1:
                    pe.wait_ge(N["kvused"], 1)
                pe.matmul(bank[R, 6, 0:NH], self.mU, gg[R, ci, :], start=True, stop=True)
                ins = pe.matmul(bank[R, 6, NH:2 * NH], self.mAll[:, 0:n], gg[R, ci, :], start=True, stop=True)
                pe.wait_ge(N["gU"], self.at("gU"))
                if self.dec:
                    ins = pe.matmul(bank[:, 7, 0:64], ones[0:ND, :], self.gm, start=True, stop=True)
                ins.then_inc(N["G"], 1)
                for a in range(2):
                    ins = pe.matmul(bank[R, a, 0:HP * n], ones[R, 0:n], self.Lm[:, self.half(a)], start=True, stop=True)
                ins.then_inc(N["R"], 1)
                if ci == 1:
                    pe.wait_ge(N["L"], 1)
                for h in range(NH):
                    k = gq[pr(h), 4 + h // 2, toks(ci)]
                    ins = pe.matmul(self.one(2 + h % 2, h), k, k, start=True, stop=True)
                ins.then_inc(N["kk"], 1)
                if ci == 1:
                    pe.wait_ge(N["QK"], 1)
                for h in range(NH):
                    ins = pe.matmul(self.one(4 + h % 2, h), gq[pr(h), 4 + h // 2, toks(ci)], gq[pr(h), h // 2, toks(ci)],
                                    start=True, stop=True)
                ins.then_inc(N["qk"], 1)
                pe.wait_ge(N["Gs"], self.at("Gs", 2 if self.dec else 1))
                for p in range(HP):
                    pe.transpose(bank[R, 6, p * P:(p + 1) * P], gq[:, 4 + p, toks(ci)], ident[:])
                    ins = pe.transpose(bank[R, 7, p * P:(p + 1) * P], gq[:, 8 + p, toks(ci)], ident[:])
                ins.then_inc(N["kv"], 1)

            def pe_turn(self, pe):
                pe.wait_ge(N["T0"], self.at("T0"))
                if self.ci == 0:
                    pe.wait_ge(N["dec"], 3)
                for h in range(NH):
                    ins = pe.transpose(self.one(2 * (self.ci == 1) + h % 2, h), self.Tb[:, self.hs(h)], ident[self.R, 0:self.n])
                ins.then_inc(N["TTp"], 1)

            def bank_y(self, a):
                return (2 if self.dec else 2 * self.ci) + a

            def pe_level_y(self, pe, l):
                for a in range(2):
                    pe.wait_ge(N["lm"], self.lev(l, a))
                    if l > 1:
                        pe.wait_ge(N["Tn"], self.lev(l - 1, a))
                    for h in range(a, NH, 2):
                        ins = pe.matmul(self.one(self.bank_y(a), h), self.Lm[:, self.hs(h)], self.TT[:, self.hs(h)],
                                        start=True, stop=True)
                    ins.then_inc(N["Y"], 1)

            def pe_level_p(self, pe, l):
                for a in range(2):
                    pe.wait_ge(N["Ye"], self.lev(l, a))
                    if self.ci == 1:
                        pe.wait_ge(N["Tn"], self.lev(l, a) - 2)
                    elif not self.dec and l > 1:
                        pe.wait_ge(N["Tn"], self.lev(l, a) - 2)
                    for h in range(a, NH, 2):
                        if l < self.nlev - 1:
                            pe.matmul(self.one(4 + 2 * a, h), self.Y[:, self.hs(h)], self.Tb[:, self.hs(h)], start=True, stop=True)
                        ins = pe.matmul(self.one(5 + 2 * a, h), self.Tb[:, self.hs(h)], self.Y[:, self.hs(h)],
                                        start=True, stop=True)
                    ins.then_inc(N["P"], 1)

            def pe_wu(self, pe):
                if self.ci:
                    for h in range(NH):
                        pe.matmul(bank[pr(h), 0, (h // 2) * self.n:(h // 2 + 1) * self.n], self.kbg[self.R, hc(h)],
                                  self.TT[:, self.hs(h)], start=True, stop=True)
                for h in range(NH):
                    ins = pe.matmul(bank[self.R, self.bU, hc(h)], self.TT[:, self.hs(h)], self.vb[self.R, hc(h)],
                                    start=True, stop=True)
                ins.then_inc(N["wu"], 1)

            def pe_old_state(self, pe):
                pe.wait_ge(N["St"], 1)
                pe.wait_ge(N["wTe"], self.at("wTe"))
                for h in range(NH):
                    pe.matmul(bank[self.R, self.bWS + h % 2, hc(h // 2)], wTb[pr(h), (h // 2) * P:(h // 2 + 1) * P],
                              St[pr(h), h // 2, :], start=True, stop=True)
                for h in range(NH):
                    ins = pe.matmul(bank[self.R, self.bQS + h % 2, hc(h // 2)], gq[pr(h), h // 2, toks(1)], St[pr(h), h // 2, :],
                                    start=True, stop=True)
                ins.then_inc(N["qs"], 1)

            def pe_new_state(self, pe):
                pe.wait_ge(N["vn"], self.at("vn"))
                for h in range(NH):
                    ins = pe.matmul(bank[pr(h), self.bS, hc(h // 2)], self.ktail[self.R, hc(h)], self.vn[self.R, hc(h)],
                                    start=True, stop=True)
                ins.then_inc(N["S"], 1)

            def pe_out(self, pe):
                pe.wait_ge(N["vn"], self.at("vn"))
                for h in range(NH):
                    ins = pe.matmul(bank[self.R, self.bO, hc(h)], self.QK[:, self.hs(h)], self.vn[self.R, hc(h)],
                                    start=True, stop=True)
                ins.then_inc(N["o2"], 1)

            def pe_turn_out(self, pe):
                b = 0 if self.dec else self.bO
                pe.wait_ge(N["std"], self.at("std", 2))
                for p in range(HP):
                    ins = pe.transpose(bank[:, b, p * self.n:(p + 1) * self.n], self.ob[self.R, p * P:(p + 1) * P],
                                       ident[self.R, 0:self.n])
                ins.then_inc(N["oT"], 1)

            def act_setup(self, act):
                R = self.R
                act.wait_ge(N["Gs"], self.at("Gs", 3 if self.dec else 2))
                act.activation(self.eG[R, 0:NH], self.Gs[R, 0:NH], ACT.Exp)
                act.activation(self.eL[R, 0:NH], self.Gs[R, NH:2 * NH], ACT.Exp)
                if self.dec:
                    act.activation(self.eGb, self.eGb, ACT.Exp)
                act.activation(self.eT[R, 0:NH], self.eT[R, 0:NH], ACT.Exp).then_inc(N["exp"], 1)
                act.wait_ge(N["dec"], self.at("dec", 1))
                act.activation(self.Y, self.Y, ACT.Exp).then_inc(N["exp"], 1)
                act.wait_ge(N["dec"], self.at("dec", 2))
                act.activation(self.QK, self.QK, ACT.Exp).then_inc(N["exp"], 1)

            def act_turn(self, act):
                act.wait_ge(N["TTp"], self.at("TTp"))
                act.activation(self.TT.rearrange("p (a c) -> p a c", a=2), self.rg(2 * (self.ci == 1)), ACT.Copy)\
                   .then_inc(N["TT"], 1)

            def act_level(self, act, l):
                for a in range(2):
                    act.wait_ge(N["Y"], self.lev(l, a))
                    if l == 1 and a == 0:
                        act.wait_ge(N["L"], self.at("L", 2))
                    if l > 1:
                        act.wait_ge(N["P"], self.lev(l - 1, a))
                    act.activation(self.Y[:, self.half(a)], bank[self.R, self.bank_y(a), 0:HP * self.n], ACT.Copy)\
                       .then_inc(N["Ye"], 1)

            def act_root(self, act):
                act.wait_ge(N["ss"], self.at("ss"))
                act.activation(self.rs[self.R, 0:NH], self.ss[self.R, 0:NH], ACT.Sqrt, scale=1.0 / HD, bias=epst[self.R, 0:1])\
                   .then_inc(N["std"], 1)

            def act_out(self, act):
                b = 0 if self.dec else self.bO
                act.wait_ge(N["oT"], self.at("oT"))
                act.activation(oT[:, 0:HP, toks(self.ci)], bank[:, b, 0:HP * self.n].rearrange("p (h i) -> p h i", h=HP),
                               ACT.Copy)

            def pool_level(self, pool, l):
                if l == 1:
                    pool.wait_ge(N["T0"], self.at("T0"))
                for a in range(2):
                    if l > 1:
                        pool.wait_ge(N["Y"], self.lev(l - 1, a))
                    hh = slice(HP * a, HP * a + HP)
                    pool.tensor_tensor(self.hv(self.Lm)[:, hh, :], self.hv(self.Lb)[:, hh, :],
                                       LVL[self.R, l, 0:self.n].unsqueeze(1).to_broadcast([self.n, HP, self.n]), ALU.mult)\
                        .then_inc(N["lm"], 1)

            def dve_setup(self, dve, c):
                ci, R, n, dec = self.ci, self.R, self.n, self.dec
                Gs, eG, eT, bG, Lb, Lm, Tb, Y, QK = (self.Gs, self.eG, self.eT, self.bG, self.Lb, self.Lm, self.Tb, self.Y,
                                                     self.QK)
                g = gg[R, ci, :]
                if dec:
                    dve.tensor_tensor(self.gm.rearrange("p (s h) -> p s h", s=NSEQ), g.unsqueeze(1).to_broadcast([ND, NSEQ, NH]),
                                      sm8.unsqueeze(2).to_broadcast([ND, NSEQ, NH]), ALU.mult)
                dve.tensor_tensor(self.pv(Lm), self.mU.unsqueeze(1).unsqueeze(1).to_broadcast([n, 2, HP, n]), self.pb(g),
                                  ALU.mult).then_inc(N["gU"], 1)
                dve.wait_ge(N["G"], self.at("G"))
                ins = dve.tensor_copy(Gs[R, :], bank[R, 6, 0:2 * NH])
                if dec:
                    ins.then_inc(N["Gs"], 1)
                    ins = dve.tensor_copy(self.eGb, bank[:, 7, 0:64])
                ins.then_inc(N["Gs"], 1)
                dve.wait_ge(N["Gs"], self.at("Gs", 2 if dec else 1))
                dve.tensor_tensor(eT[R, 0:NH], Gs[R, NH:2 * NH], Gs[R, 0:NH], ALU.subtract).then_inc(N["Gs"], 1)
                dve.wait_ge(N["R"], self.at("R"))
                c(dve.tensor_tensor(self.pv(Tb), self.rg(0).rearrange("p a (h i) -> p a h i", h=HP), self.pb(Gs[R, 0:NH]),
                                    ALU.subtract))
                dve.scalar_tensor_tensor(out=self.hv(Y), in0=self.hv(Tb), scalar=-1.0, in1=self.bc(self.nS), op0=ALU.mult,
                                         op1=ALU.add).then_inc(N["dec"], 1)
                dve.tensor_tensor(self.hv(QK), self.hv(Tb), self.bc(self.nU), ALU.add).then_inc(N["dec"], 1)
                dve.wait_ge(N["exp"], self.at("exp", 1))
                c(dve.tensor_tensor(bG[R, 0:NH], bet[R, ci, :], eG[R, 0:NH], ALU.mult))
                dve.wait_ge(N["kk"], self.at("kk"))
                dve.tensor_tensor(self.pv(Lb), self.rg(2).rearrange("p a (h i) -> p a h i", h=HP), self.pb(bet[R, ci, :]),
                                  ALU.mult).then_inc(N["L"], 1)
                dve.wait_ge(N["L"], self.at("L", 1))
                dve.wait_ge(N["exp"], self.at("exp", 2))
                dve.tensor_tensor(Lb, Lb, Y, ALU.mult).then_inc(N["L"], 1)
                dve.wait_ge(N["L"], self.at("L", 2))
                dve.wait_ge(N["R"], self.at("R"))
                c(dve.tensor_tensor(self.hv(Lm), self.hv(Lb), self.bc(LVL[R, 0, 0:n]), ALU.mult))
                dve.tensor_tensor(self.hv(Tb), self.bc(ident[R, 0:n]), self.hv(Lm), ALU.subtract).then_inc(N["T0"], 1)
                dve.wait_ge(N["qk"], self.at("qk"))
                dve.wait_ge(N["exp"], self.at("exp", 3))
                q2 = QK.rearrange("p (a c) -> p a c", a=2)
                dve.tensor_tensor(q2, self.rg(4), q2, ALU.mult).then_inc(N["QK"], 1)
                dve.wait_ge(N["kv"], self.at("kv"))
                dve.tensor_tensor(hd(self.kbg[R]), hd(bank[R, 6, :]), self.hb(bG[R, 0:NH]), ALU.mult)
                dve.tensor_tensor(hd(self.ktail[R]), hd(bank[R, 6, :]), self.hb(eT[R, 0:NH]), ALU.mult)
                dve.tensor_tensor(hd(self.vb[R]), hd(bank[R, 7, :]), self.hb(bet[R, ci, :]), ALU.mult).then_inc(N["kvused"], 1)

            def dve_level(self, dve, l):
                for a in range(2):
                    dve.wait_ge(N["P"], self.lev(l, a))
                    if l == 1 and a == 0:
                        dve.wait_ge(N["TT"], self.at("TT"))
                    w = self.half(a)
                    if l < self.nlev - 1:
                        dve.tensor_tensor(self.Tb[:, w], self.Tb[:, w], bank[self.R, 4 + 2 * a, 0:HP * self.n], ALU.subtract)
                    dve.tensor_tensor(self.TT[:, w], self.TT[:, w], bank[self.R, 5 + 2 * a, 0:HP * self.n], ALU.subtract)\
                       .then_inc(N["Tn"], 1)

            def dve_norm(self, dve, c, osq):
                ci, R, n = self.ci, self.R, self.n
                c(dve.tensor_tensor(osq, self.ob[R], self.ob[R], ALU.mult))
                dve.tensor_reduce(self.ss[R, 0:NH], hd(osq), AX.X, ALU.add).then_inc(N["ss"], 1)
                dve.wait_ge(N["sz"], self.at("sz"))
                c(dve.tensor_tensor(self.sz, z_tok[R, ci, :], self.sz, ALU.mult))
                c(dve.tensor_tensor(hd(self.sz), hd(self.sz), gnorm[R].unsqueeze(1).to_broadcast([n, NH, HD]), ALU.mult))
                dve.wait_ge(N["std"], self.at("std", 1))
                c(dve.reciprocal(self.rs[R, 0:NH], self.rs[R, 0:NH]))
                c(dve.tensor_tensor(hd(self.ob[R]), hd(self.ob[R]), self.hb(self.rs[R, 0:NH]), ALU.mult))
                dve.tensor_tensor(self.ob[R], self.ob[R], self.sz, ALU.mult).then_inc(N["std"], 1)

        hc = lambda h: slice(HD * h, HD * h + HD)
        pr = lambda h: slice(HD * (h % 2), HD * (h % 2) + HD)
        hd = lambda v: v.rearrange("p (h d) -> p h d", h=NH)
        sm8 = SM[0:ND].rearrange("p (s j) -> p s j", j=NDEC)[:, :, 0]
        first, second, decode = (GdnChunk(ci) for ci in range(3))
        prompt = (first, second)

        with nc.Block() as block:
            @block.tensor
            def _(pe):
                for k in prompt:
                    k.pe_setup(pe)
                for k in prompt:
                    k.pe_turn(pe)
                pe.wait_ge(N["TT"], 2)
                pe.wait_ge(N["QK"], 2)
                pe.wait_ge(N["kvused"], 2)
                for l in range(1, 7):
                    for k in prompt:
                        k.pe_level_y(pe, l)
                    for k in prompt:
                        k.pe_level_p(pe, l)
                pe.wait_ge(N["Tn"], 24)
                for k in prompt:
                    k.pe_wu(pe)
                first.pe_new_state(pe)
                first.pe_out(pe)
                second.pe_old_state(pe)
                second.pe_new_state(pe)
                second.pe_out(pe)
                for k in prompt:
                    k.pe_turn_out(pe)

            @block.scalar
            def _(act):
                for k in prompt:
                    act.activation(k.sz, z_tok[:, k.ci, :], ACT.Sigmoid).then_inc(N["sz"], 1)
                for k in prompt:
                    k.act_setup(act)
                for k in prompt:
                    k.act_turn(act)
                for l in range(1, 7):
                    for k in prompt:
                        k.act_level(act, l)
                act.wait_ge(N["wu"], 2)
                act.activation(wTb, bank[:, 0, :], ACT.Copy).then_inc(N["wTe"], 1)
                for k in prompt:
                    k.act_root(act)
                for k in prompt:
                    k.act_out(act)

            @block.gpsimd
            def _(pool):
                for l in range(1, 7):
                    for k in prompt:
                        k.pool_level(pool, l)

            @block.vector
            def _(dve):
                c = Chain(dve, s_dve)
                c.n = dve_n[0]
                for k in prompt:
                    k.dve_setup(dve, c)
                for l in range(1, 7):
                    for k in prompt:
                        k.dve_level(dve, l)
                dve.wait_ge(N["wu"], 1)
                dve.tensor_copy(first.vn, bank[:, first.bU, :]).then_inc(N["vn"], 1)
                dve.wait_ge(N["wu"], 2)
                c(dve.tensor_copy(second.vn, bank[:, second.bU, :]))
                dve.wait_ge(N["S"], 1)
                dve.tensor_copy(St, bank[:, first.bS, 0:256].rearrange("p (h d) -> p h d", h=HP)).then_inc(N["St"], 1)
                dve.tensor_copy(eLs[0:HD, :], second.eL[0:HD, 0:NH:2])
                c(dve.tensor_copy(eLs[HD:P, :], second.eL[HD:P, 1:NH:2]))
                dve.wait_ge(N["o2"], 1)
                c(dve.tensor_copy(first.ob, bank[:, first.bO, :]))
                dve.wait_ge(N["qs"], 1)
                par = lambda v, a: v.rearrange("p (h a d) -> p a h d", a=2, d=HD)[:, a]
                ph = lambda b: bank[:, b, 0:HP * HD].rearrange("p (h d) -> p h d", h=HP)
                for a in range(2):
                    ins = dve.tensor_tensor(par(second.vn, a), par(second.vn, a), ph(second.bWS + a), ALU.subtract)
                ins.then_inc(N["vn"], 1)
                for a in range(2):
                    ins = dve.tensor_tensor(par(second.ob, a), ph(second.bQS + a), second.eG[:, a:NH:2].unsqueeze(2)
                                            .to_broadcast([P, HP, HD]), ALU.mult)
                c(ins)
                c(dve.tensor_tensor(St, St, eLs.unsqueeze(2).to_broadcast([P, HP, HD]), ALU.mult))
                first.dve_norm(dve, c, first.Lb[:, 0:GW])
                dve.wait_ge(N["o2"], 2)
                c(dve.tensor_tensor(second.ob, second.ob, bank[:, second.bO, :], ALU.add))
                second.dve_norm(dve, c, second.Lb[:, 0:GW])
                dve.wait_ge(N["S"], 2)
                dve.tensor_tensor(St, St, bank[:, second.bS, 0:256].rearrange("p (h d) -> p h d", h=HP), ALU.add)\
                   .then_inc(N["St"], 1)
                dve_n[0] = c.n

        with nc.Block() as block:
            @block.sync
            def _(sp):
                for par in range(2):
                    for s in range(NSEQ):
                        sp.dma_start(S0[HD * par:HD * par + HD, s],
                                     state_ssm[0, s].rearrange("(p two) k v -> two k p v", two=2)[par]).then_inc(s_s0, 16)

            @block.tensor
            def _(pe):
                k = decode
                k.pe_setup(pe)
                k.pe_turn(pe)
                pe.wait_ge(N["TT"], 3)
                pe.wait_ge(N["QK"], 3)
                pe.wait_ge(N["kvused"], 3)
                k.pe_level_y(pe, 1)
                k.pe_level_p(pe, 1)
                pe.wait_ge(N["Tn"], k.lev(1, 1))
                k.pe_wu(pe)
                pe.wait_ge(N["wTe"], k.at("wTe"))
                pe.wait_ge(s_s0, 256)
                for s in range(NSEQ):
                    for h in range(NH):
                        o = 64 * (h // 2) + 8 * s
                        ins = pe.matmul(bank[pr(h), 4, o:o + 8], S0[pr(h), s, h // 2, :], k.WQ[pr(h), h // 2, s, :],
                                        start=True, stop=True)
                ins.then_inc(N["ws"], 1)
                pe.wait_ge(N["ws"], 2)
                for p in range(HP):
                    pe.transpose(bank[0:ND, k.bWS, p * P:(p + 1) * P], k.W1[:, 32 * p:32 * p + 32], ident[:])
                    ins = pe.transpose(bank[0:ND, k.bQS, p * P:(p + 1) * P], k.Q1[:, 32 * p:32 * p + 32], ident[:])
                ins.then_inc(N["qs"], 1)
                k.pe_out(pe)
                for a in range(2):
                    pe.wait_ge(N["vmr"], a + 1)
                    for h in range(4 * a, 4 * a + 4):
                        ins = pe.matmul(bank[pr(h), (3, 4, 5, 7)[h // 2], :], k.ktail[0:ND, hc(h)],
                                        k.vm[:, 512 * (h % 4):512 * (h % 4 + 1)], start=True, stop=True)
                    ins.then_inc(N["S"], 1)
                k.pe_turn_out(pe)

            @block.scalar
            def _(act):
                k = decode
                act.activation(k.sz, z_tok[0:ND, 2, :], ACT.Sigmoid).then_inc(N["sz"], 1)
                k.act_setup(act)
                k.act_turn(act)
                k.act_level(act, 1)
                act.wait_ge(N["wu"], k.at("wu"))
                act.activation(k.WQ[:, :, :, 0:4], bank[:, 0, 0:HP * ND].rearrange("p (h s i) -> p h s i", h=HP, s=NSEQ), ACT.Copy)
                act.activation(k.WQ[:, :, :, 4:8], gq[:, 0:HP, SEQ:T].rearrange("p h (s i) -> p h s i", s=NSEQ),
                               ACT.Copy).then_inc(N["wTe"], 1)
                act.wait_ge(N["ws"], 1)
                v = bank[:, 4, 0:256].rearrange("p (h s c) -> p h s c", h=HP, s=NSEQ)
                act.activation(k.W1.rearrange("p (h s i) -> p h s i", h=HP, s=NSEQ), v[:, :, :, 0:4], ACT.Copy)
                act.activation(k.Q1.rearrange("p (h s i) -> p h s i", h=HP, s=NSEQ), v[:, :, :, 4:8], ACT.Copy)\
                   .then_inc(N["ws"], 1)
                k.act_root(act)
                k.act_out(act)

            @block.gpsimd
            def _(pool):
                decode.pool_level(pool, 1)

            @block.vector
            def _(dve):
                k = decode
                c = Chain(dve, s_dve)
                c.n = dve_n[0]
                k.dve_setup(dve, c)
                k.dve_level(dve, 1)
                R = slice(0, ND)
                dve.wait_ge(N["wu"], k.at("wu"))
                c(dve.tensor_copy(k.vn[R], bank[R, k.bU, :]))
                dve.wait_ge(N["qs"], k.at("qs"))
                dve.tensor_tensor(k.vn[R], k.vn[R], bank[R, k.bWS, :], ALU.subtract).then_inc(N["vn"], 1)
                c(dve.tensor_tensor(hd(k.ob[R]), hd(bank[R, k.bQS, :]), k.hb(k.eG[R, 0:NH]), ALU.mult))
                dve.wait_ge(N["vn"], k.at("vn"))
                for a in range(2):
                    if a:
                        dve.wait_ge(N["S"], k.at("S", 1))
                    dve.tensor_tensor(k.vm.rearrange("p (h s d) -> p h s d", h=4, s=NSEQ),
                                      k.vn[R, 256 * a:256 * a + 256].rearrange("p (h d) -> p h d", h=4).unsqueeze(2)
                                      .to_broadcast([ND, 4, NSEQ, HD]),
                                      sm8.unsqueeze(1).unsqueeze(3).to_broadcast([ND, 4, NSEQ, HD]), ALU.mult)\
                       .then_inc(N["vmr"], 1)
                dve.wait_ge(N["o2"], k.at("o2"))
                c(dve.tensor_tensor(k.ob[R], k.ob[R], bank[R, k.bO, :], ALU.add))
                dve.wait_ge(N["S"], k.at("S", 2))
                k.dve_norm(dve, c, k.vm[:, 0:GW])
                v = k.eGb.rearrange("p (s h) -> p s h", s=NSEQ)
                e = k.eGls.rearrange("p (s h) -> p s h", s=NSEQ)
                dve.tensor_copy(e[0:HD], v[0:HD, :, 0:NH:2])
                c(dve.tensor_copy(e[HD:P], v[HD:P, :, 1:NH:2]))
                c(dve.tensor_tensor(S0.rearrange("p s h d -> p (s h) d"), S0.rearrange("p s h d -> p (s h) d"),
                                    k.eGls.unsqueeze(2).to_broadcast([P, NSEQ * HP, HD]), ALU.mult))
                for p in range(HP):
                    ins = dve.tensor_tensor(S0[:, :, p, :], S0[:, :, p, :],
                                            bank[:, (3, 4, 5, 7)[p], :].rearrange("p (s d) -> p s d", s=NSEQ), ALU.add)
                ins.then_inc(N["St"], 1)
                dve_n[0] = c.n

        h2 = gq[:].rearrange("p a t -> p (a t)")[:, 0:3 * D].rearrange("p (t d) -> p t d", t=3)
        tab = gq[:].rearrange("p a t -> p (a t)")[:, 3 * D:]
        rk, gt = (tab[:, 102 * i:102 * (i + 1)].rearrange("p (t e) -> p t e", t=3) for i in range(2))
        iota = tab[:, 204:268]
        curP, curR, curG = (tab[:, 268 + 6 * i:274 + 6 * i].rearrange("p (t e) -> p t e", t=3) for i in range(3))
        npass = sb("npass", [1, 1], I32)
        rw, rbias = at(0, (KD, NE)), work[:, 256:288]
        s_rw = sem("router_loaded")
        s_wo, s_wor = sem("mixer_out"), sem("residual_added")
        with nc.Block() as block:
            @block.sync
            def _(sp):
                sp.dma_start(wb[:], norm_ffn[0].partition_broadcast(P)).then_inc(s_wb, 16)
                sp.dma_start(rw, router_w[0].rearrange("(k p) e -> p k e", p=P)).then_inc(s_rw, 16)
                sp.dma_start(rbias, router_b[0].partition_broadcast(P)).then_inc(s_rw, 16)
                for ch in range(5):
                    load_chunk(sp, 0, ch)
                for par in range(2):
                    sp.dma_start(ssm_prompt[0, 0].rearrange("(p two) k v -> two k p v", two=2)[par],
                                 St[HD * par:HD * par + HD]).then_inc(s_ssm, 16)
                    for s in range(NSEQ):
                        sp.dma_start(ssm_sample[0, s].rearrange("(p two) k v -> two k p v", two=2)[par],
                                     S0[HD * par:HD * par + HD, s]).then_inc(s_ssm, 16)
                sp.wait_ge(s_ringfree, U_END)
                for ch in range(8, NSLOT):
                    load_chunk(sp, 0, ch)

            @block.gpsimd
            def _(pool):
                pool.memset(h2[:, 2, :], 0.0)
                pool.memset(gt, 0.0)
                pool.memset(rk, -1.0e6)
                pool.iota(work[:, 300:364].bitcast(I32), pattern=[[1, CAP]], base=0, channel_multiplier=0)

            @block.tensor
            def _(pe):
                slot_wait(pe, U_WO)
                slot_wait(pe, U_WO + 2)
                for m in range(2):
                    w = slot(U_WO + 2 * m, 2).rearrange("p (k n) -> p k n", k=KD)
                    for k in range(KD):
                        q = slice(ND * (k % 4), ND * (k % 4) + ND)
                        ins = pe.matmul(bank[q, 3 * m + 2, :], oT[:, k, toks(2)], w[:, k, :], start=k < 4, stop=k >= 4)
                    ins.then_inc(s_wo, 1)
                    for t in range(2):
                        for k in range(KD):
                            ins = pe.matmul(bank[:, 3 * m + t, :], oT[:, k, toks(t)], w[:, k, :], start=k == 0,
                                            stop=k == KD - 1)
                        ins.then_inc(s_wo, 1)
                pe.wait_ge(s_wo, 6)
                pe.sem_inc(s_ringfree, U_END - U_WO)

            @block.vector
            def _(dve):
                c = Chain(dve, s_dve)
                c.n = dve_n[0]
                for m in range(2):
                    cols = slice(512 * m, 512 * (m + 1))
                    dve.wait_ge(s_wo, 3 * m + 1)
                    for q in range(4):
                        x = X[0:ND, 2, cols]
                        c(dve.tensor_tensor(x, x, bank[ND * q:ND * q + ND, 3 * m + 2, :], ALU.add))
                    for t in range(2):
                        dve.wait_ge(s_wo, 3 * m + t + 2)
                        dve.tensor_tensor(X[:, t, cols], X[:, t, cols], bank[:, 3 * m + t, :], ALU.add).then_inc(s_wor, 1)
                dve_n[0] = c.n

        ffnnorm = Norm(1, lambda t: h2[rows(t), t, :], lambda e: e.wait_ge(s_wb, 32), True)
        with nc.Block() as block:
            @block.scalar
            def _(act):
                ffnnorm.scalar(act)

            @block.vector
            def _(dve):
                ffnnorm.vector(dve)

            @block.tensor
            def _(pe):
                ffnnorm.tensor(pe)

        lg, mk, ex, gtr, eq, ce = (at(400 + 96 * i, (3, NE)) for i in range(6))
        m8 = at(980, (3, 8))
        ng, nd, nm, gs, mc = (work[:, 1010 + 4 * i:1014 + 4 * i] for i in range(5))
        s_lg, s_nm, s_exp, s_mk, s_rank = (sem(n) for n in ("logits", "neg_top", "exps", "chosen", "ranks"))
        with nc.Block() as block:
            @block.sync
            def _(sp):
                sp.wait_ge(s_ssm, 32 + 256)

            @block.tensor
            def _(pe):
                pe.wait_ge(s_rw, 32)
                for t in range(3):
                    for k in range(KD):
                        ins = pe.matmul(bank[rows(t), t, 0:NE], hT[:, k, toks(t)], rw[:, k, :], start=k == 0, stop=k == KD - 1)
                ins.then_inc(s_lg, 1)
                pe.wait_ge(s_mk, 1)
                for t in range(3):
                    for u in range(t):
                        pe.matmul(bank[rows(t), 3 + t, 0:NE], ones[:, rows(t)], mk[:, u, :], start=u == 0, stop=False)
                    pe.matmul(bank[rows(t), 3 + t, 0:NE], Uinc[rows(t), rows(t)], mk[rows(t), t, :], start=t == 0, stop=True)
                for t in range(3):
                    ins = pe.matmul(bank[:, 6, 0:NE], ones[rows(t), :], mk[rows(t), t, :], start=t == 0, stop=t == 2)
                ins.then_inc(s_rank, 1)

            @block.scalar
            def _(act):
                act.wait_ge(s_nm, 1)
                for t in range(3):
                    ins = act.activation(ex[rows(t), t, :], lg[rows(t), t, :], ACT.Exp, bias=nm[rows(t), t:t + 1])
                ins.then_inc(s_exp, 1)

            @block.vector
            def _(dve):
                c = Chain(dve, s_dve)
                c.n = dve_n[0]
                dve.tensor_copy(iota, work[:, 300:364].bitcast(I32))
                dve.wait_ge(s_rw, 32)
                dve.wait_ge(s_lg, 1)
                for t in range(3):
                    r = rows(t)
                    c(dve.tensor_tensor(lg[r, t, :], bank[r, t, 0:NE], rbias[r], ALU.add))
                    c(dve.max(m8[r, t, :], lg[r, t, :]))
                    ins = dve.tensor_scalar(nm[r, t:t + 1], m8[r, t, 0:1], -1.0, None, ALU.mult)
                ins.then_inc(s_nm, 1)
                for t in range(3):
                    r = rows(t)
                    v4 = m8[r, t, TOPK - 1:TOPK]
                    dve.tensor_scalar(eq[r, t, :], lg[r, t, :], v4, None, ALU.is_equal)
                    c(dve.tensor_scalar(gtr[r, t, :], lg[r, t, :], v4, None, ALU.is_gt))
                    dve.tensor_reduce(ng[r, t:t + 1], gtr[r, t, :], AX.X, ALU.add)
                    c(dve.tensor_tensor_scan(ce[r, t, :], eq[r, t, :], eq[r, t, :], 0.0, ALU.add, ALU.bypass))
                    c(dve.tensor_scalar(nd[r, t:t + 1], ng[r, t:t + 1], -1.0, float(TOPK), ALU.mult, ALU.add))
                    c(dve.scalar_tensor_tensor(out=mk[r, t, :], in0=ce[r, t, :], scalar=nd[r, t:t + 1], in1=eq[r, t, :],
                                               op0=ALU.is_le, op1=ALU.mult))
                    ins = dve.tensor_tensor(mk[r, t, :], mk[r, t, :], gtr[r, t, :], ALU.add)
                ins.then_inc(s_mk, 1)
                dve.wait_ge(s_mk, 1)
                dve.wait_ge(s_exp, 1)
                for t in range(3):
                    r = rows(t)
                    c(dve.tensor_tensor(ex[r, t, :], ex[r, t, :], mk[r, t, :], ALU.mult))
                    c(dve.tensor_reduce(gs[r, t:t + 1], ex[r, t, :], AX.X, ALU.add))
                    c(dve.reciprocal(gs[r, t:t + 1], gs[r, t:t + 1]))
                    c(dve.tensor_scalar(gt[r, t, 0:NE], ex[r, t, :], gs[r, t:t + 1], None, ALU.mult))
                dve.tensor_copy(gt[:, :, NE:NE + 2], gt[:, :, 0:2])
                dve.wait_ge(s_rank, 1)
                for t in range(3):
                    r = rows(t)
                    c(dve.scalar_tensor_tensor(out=rk[r, t, 0:NE], in0=bank[r, 3 + t, 0:NE], scalar=1.0e6, in1=mk[r, t, :],
                                               op0=ALU.add, op1=ALU.mult))
                    c(dve.tensor_scalar(rk[r, t, 0:NE], rk[r, t, 0:NE], -1000001.0, None, ALU.add))
                dve.tensor_scalar(rk[:, :, NE:NE + 2], rk[:, :, 0:2], -float(CAP), None, ALU.add)
                c(dve.tensor_reduce(mc[:, 0:1], bank[:, 6, 0:NE], AX.X, ALU.max))
                c(dve.memset(mc[:, 1:2], 1.0))
                for k in range(1, -(-T // CAP)):
                    c(dve.scalar_tensor_tensor(out=mc[:, 1:2], in0=mc[:, 0:1], scalar=float(k * CAP), in1=mc[:, 1:2],
                                               op0=ALU.is_gt, op1=ALU.add))
                dve.tensor_copy(npass[:], mc[0:1, 1:2])
                dve_n[0] = c.n

        o_ = 0
        def take(n, parts=P):
            nonlocal o_
            o_ += n
            return work[0:parts, o_ - n:o_]
        xs, gb, ub, sg, ab, oo = take(D), take(512), take(512), take(512), take(D), take(D)
        xT = take(D).rearrange("p (k s) -> p k s", k=KD)
        aT = take(D).rearrange("p (k s) -> p k s", k=KD)
        PGT, Pm, PG = take(3 * P), take(3 * P), take(3 * P)
        bu, bd = take(D, 4), take(D, 2)
        bsel = take(4 * CAP, 4).rearrange("p (r s) -> p r s", r=4)
        assert o_ <= CONST_END
        names = ("P", "PG", "gathered", "x_copied", "xT_turned", "xT_copied", "up", "gate_clamped", "sigmoid", "act",
                 "aT_turned", "aT_copied", "out", "out_copied_act", "out_copied_dve", "PG_turned", "PGT_copied", "y",
                 "y_added", "dve_links", "bu_loaded", "bd_loaded", "bu_used", "bd_used", "ready")
        M = {k: sem("moe_" + k) for k in names}
        before = [slot_count(max(u for u in range(U_END) if (u + 10) % NSLOT == i)) for i in range(NSLOT)]
        K_DVE = 6

        def expert_loops(eng, body, after_pass=None):
            n = eng.value_load(npass[0:1, 0:1], min_val=1, max_val=-(-T // CAP))
            with eng.Fori(0, n) as p:
                with eng.Fori(0, NPAIR) as j:
                    body(p * NPAIR + j, j)
                if after_pass:
                    after_pass(p)
            return n

        with nc.Block() as block:
            @block.sync
            def _(sp):
                sp.dma_start(wb[:], norm_final.partition_broadcast(P)).then_inc(s_wb, 16)
                with sp.Fori(0, NPAIR - 1) as j:
                    for ch in range(12, CH):
                        sp.wait_ge(s_wused, CH * j + ch - 11)
                        load_chunk(sp, j, ch)
                    for ch in range(12):
                        sp.wait_ge(s_wused, CH * j + 12 + ch + 1)
                        load_chunk(sp, j + 1, ch)
                for ch in range(12, CH):
                    sp.wait_ge(s_wused, CH * (NPAIR - 1) + ch - 11)
                    load_chunk(sp, NPAIR - 1, ch)
                n = sp.value_load(npass[0:1, 0:1], min_val=1, max_val=-(-T // CAP))
                with sp.If(n > 1):
                    with sp.Fori(1, n) as p:
                        with sp.Fori(0, NPAIR) as j:
                            for ch in range(CH):
                                sp.wait_ge(s_wused, CH * (p * NPAIR + j) + ch - 11)
                                load_chunk(sp, j, ch)

            @block.gpsimd
            def _(pool):
                c = Chain(pool, s_pool)
                c.n = pool_n[0]
                c(pool.memset(bsel, 0.0))
                c(pool.affine_select(out=bsel, in_=bsel, pattern=[[1, 4], [0, CAP]], compare_op=ALU.not_equal, fill=1.0,
                                     base=0, channel_multiplier=-1))
                c(pool.memset(PGT, 0.0))
                pool.memset(oo, 0.0).then_inc(M["ready"], 1)
                pool_n[0] = c.n

                def body(i, j):
                    pool.wait_ge(M["bu_used"], i + 1)
                    pool.dma_start(bu, b_up[0, bass.ds(2 * j, 2), :].rearrange("e (h c) -> (e h) c", h=2))\
                        .then_inc(M["bu_loaded"], 16)
                    pool.wait_ge(M["bd_used"], i + 1)
                    pool.dma_start(bd, b_down[0, bass.ds(2 * j, 2), :]).then_inc(M["bd_loaded"], 16)
                expert_loops(pool, body)

            @block.tensor
            def _(pe):
                def gather(n):
                    pe.wait_ge(M["P"], n)
                    for t in range(3):
                        for m in range(2):
                            ins = pe.matmul(bank[:, 4 + m, :], Pm[:, t * P:(t + 1) * P], h2[:, t, 512 * m:512 * (m + 1)],
                                            start=t == 0, stop=t == 2)
                    ins.then_inc(M["gathered"], 1)

                def turn_x(n):
                    pe.wait_ge(M["x_copied"], n)
                    for k in range(KD):
                        ins = pe.transpose(bank[:, 7 - k // 4, (k % 4) * P:(k % 4 + 1) * P], xs[:, k * P:(k + 1) * P], ident[:])
                        if k % 4 == 3:
                            ins.then_inc(M["xT_turned"], 1)

                def combine(i):
                    pe.wait_ge(M["out_copied_act"], i + 1)
                    pe.wait_ge(M["out_copied_dve"], i + 1)
                    pe.wait_ge(M["PGT_copied"], i + 1)
                    for n in range(6):
                        t, m = n // 2, n % 2
                        if n >= 4:
                            pe.wait_ge(M["y_added"], 6 * i + n - 3)
                        pe.matmul(bank[rows(t), 4 + n % 4, :], PGT[:, t * P:t * P + ROWS[t]], oo[:, 512 * m:512 * (m + 1)],
                                  start=True, stop=True).then_inc(M["y"], 1)

                def products(i, b0, ch0, lhs, k0=0):
                    for kp in range(4):
                        for e in range(2):
                            ch = ch0 + 2 * kp + e
                            pe.wait_ge(s_slot[ch % NSLOT], 32 * i + (16 * (ch // NSLOT + 1) + before[ch % NSLOT]))
                        for kk in range(2):
                            k = 2 * kp + kk
                            for m in range(2):
                                for e in range(2):
                                    ch = ch0 + 2 * kp + e
                                    w = ring[:, (ch % NSLOT) * RSLOT + kk * D + 512 * m:(ch % NSLOT) * RSLOT + kk * D + 512 * (m + 1)]
                                    ins = pe.matmul(bank[CAP * e:CAP * e + CAP, b0 + m, :], lhs[:, k, CAP * e:CAP * e + CAP], w,
                                                    start=False, stop=k == KD - 1)
                                    if kk == 1 and m == 1:
                                        ins.then_inc(s_wused, 1)
                    return ins

                def up(i, half):
                    for m in range(2):
                        for e in range(2):
                            ins = pe.matmul(bank[CAP * e:CAP * e + CAP, 2 * half + m, :], bsel[0:4, 2 * e + half, :],
                                            bu[0:4, 512 * m:512 * (m + 1)], start=True, stop=False)
                    if half:
                        ins.then_inc(M["bu_used"], 1)
                    products(i, 2 * half, 8 * half, xT)

                def turn_act(i, half):
                    pe.wait_ge(M["act"], 2 * i + half + 1)
                    for k in range(4):
                        ins = pe.transpose(bank[:, 6, k * P:(k + 1) * P], ab[:, 512 * half + k * P:512 * half + (k + 1) * P], ident[:])
                    ins.then_inc(M["aT_turned"], 1)

                pe.sem_inc(M["bu_used"], 1)
                pe.sem_inc(M["bd_used"], 1)
                gather(1)
                turn_x(1)
                pe.wait_ge(M["ready"], 1)

                def body(i, j):
                    pe.wait_ge(M["bu_loaded"], 16 * i + 16)
                    pe.wait_ge(M["xT_copied"], 2 * i + 2)
                    up(i, 0)
                    combine(i)
                    up(i, 1)
                    pe.wait_ge(M["y_added"], 6 * i + 6)
                    turn_act(i, 0)
                    gather(i + 2)
                    pe.wait_ge(M["PG"], i + 1)
                    for t in range(3):
                        ins = pe.transpose(bank[:, 7, t * P:(t + 1) * P], PG[:, t * P:(t + 1) * P], ident[:])
                    ins.then_inc(M["PG_turned"], 1)
                    pe.wait_ge(M["aT_copied"], 2 * i + 1)
                    turn_act(i, 1)
                    pe.wait_ge(M["PGT_copied"], i + 2)
                    pe.wait_ge(M["aT_copied"], 2 * i + 2)
                    turn_x(i + 2)
                    pe.wait_ge(M["bd_loaded"], 16 * i + 16)
                    for m in range(2):
                        for e in range(2):
                            ins = pe.matmul(bank[CAP * e:CAP * e + CAP, 4 + m, :], bsel[0:2, e, :],
                                            bd[0:2, 512 * m:512 * (m + 1)], start=True, stop=False)
                    ins.then_inc(M["bd_used"], 1)
                    products(i, 4, 16, aT)
                n = expert_loops(pe, body)
                pe.wait_ge(M["xT_copied"], 2 * (n * NPAIR) + 2)
                combine(n * NPAIR)

            @block.scalar
            def _(act):
                def copy_x(n):
                    act.wait_ge(M["gathered"], n)
                    act.activation(xs, bank[:, 4:6, :].rearrange("p b n -> p (b n)"), ACT.Copy).then_inc(M["x_copied"], 1)

                def copy_xT(n):
                    for q in range(2):
                        act.wait_ge(M["xT_turned"], 2 * n - 1 + q)
                        act.activation(xT[:, 4 * q:4 * q + 4, :].rearrange("p k s -> p (k s)"), bank[:, 7 - q, :], ACT.Copy)\
                           .then_inc(M["xT_copied"], 1)

                act.sem_inc(M["out_copied_act"], 1)
                copy_x(1)
                copy_xT(1)

                def body(i, j):
                    def sigmoid(half):
                        act.wait_ge(M["gate_clamped"], 2 * i + half + 1)
                        act.activation(sg, gb, ACT.Sigmoid, scale=1.702).then_inc(M["sigmoid"], 1)

                    def copy_aT(half):
                        act.wait_ge(M["aT_turned"], 2 * i + half + 1)
                        act.activation(aT[:, 4 * half:4 * half + 4, :].rearrange("p k s -> p (k s)"), bank[:, 6, :], ACT.Copy)\
                           .then_inc(M["aT_copied"], 1)
                    sigmoid(0)
                    copy_aT(0)
                    sigmoid(1)
                    copy_x(i + 2)
                    copy_aT(1)
                    copy_xT(i + 2)
                    act.wait_ge(s_wused, CH * i + CH)
                    act.activation(oo[:, 0:512], bank[:, 4, :], ACT.Copy).then_inc(M["out_copied_act"], 1)
                expert_loops(act, body)

            @block.vector
            def _(dve):
                c = Chain(dve, M["dve_links"])

                def place(dst, cur, gate, col):
                    ins = dve.tensor_copy(cur, rk[:, :, bass.ds(col, 2)])
                    if gate is not None:
                        ins = dve.tensor_copy(gate, gt[:, :, bass.ds(col, 2)])
                    c(ins)
                    for t in range(3):
                        for e in range(2):
                            d = dst[:, t * P + CAP * e:t * P + CAP * e + CAP]
                            if gate is None:
                                ins = dve.tensor_scalar(d, iota, cur[:, t, e:e + 1], None, ALU.is_equal)
                            else:
                                ins = dve.tensor_scalar(d, iota, cur[:, t, e:e + 1], gate[:, t, e:e + 1], ALU.is_equal, ALU.mult)
                    return ins

                def add_y(i):
                    for n in range(6):
                        t, m = n // 2, n % 2
                        dve.wait_ge(M["y"], 6 * i + n + 1)
                        x = X[rows(t), t, 512 * m:512 * (m + 1)]
                        dve.tensor_tensor(x, x, bank[rows(t), 4 + n % 4, :], ALU.add).then_inc(M["y_added"], 1)

                place(Pm, curP, None, 0).then_inc(M["P"], 1)
                dve.sem_inc(M["out_copied_dve"], 1)
                dve.sem_inc(M["PGT_copied"], 1)
                n0 = c.n

                def body(i, j, p):
                    c.base, c.n = K_DVE * i + p + n0, 0
                    place(PG, curR, curG, 2 * j).then_inc(M["PG"], 1)
                    dve.wait_ge(M["gathered"], i + 1)
                    place(Pm, curP, None, 2 * j + 2).then_inc(M["P"], 1)

                    def activation(half):
                        dve.wait_ge(s_wused, CH * i + 8 * half + 8)
                        hu = bank[:, 2 * half:2 * half + 2, :].rearrange("p b (f two) -> p (b f) two", two=2)
                        dve.tensor_scalar(gb, hu[:, :, 0], 7.0, None, ALU.min).then_inc(M["gate_clamped"], 1)
                        c(dve.tensor_scalar(ub, hu[:, :, 1], 7.0, -7.0, ALU.min, ALU.max))
                        c(dve.scalar_tensor_tensor(out=ub, in0=ub, scalar=1.0, in1=gb, op0=ALU.add, op1=ALU.mult))
                        dve.wait_ge(M["sigmoid"], 2 * i + half + 1)
                        dve.tensor_tensor(ab[:, 512 * half:512 * (half + 1)], ub, sg, ALU.mult).then_inc(M["act"], 1)
                    activation(0)
                    add_y(i)
                    activation(1)
                    dve.wait_ge(M["PG_turned"], i + 1)
                    dve.tensor_copy(PGT, bank[:, 7, 0:3 * P]).then_inc(M["PGT_copied"], 1)
                    dve.wait_ge(s_wused, CH * i + CH)
                    dve.tensor_copy(oo[:, 512:D], bank[:, 5, :]).then_inc(M["out_copied_dve"], 1)
                    assert c.n == K_DVE, c.n

                nn = dve.value_load(npass[0:1, 0:1], min_val=1, max_val=-(-T // CAP))
                with dve.Fori(0, nn) as p:
                    with dve.Fori(0, NPAIR) as j:
                        body(p * NPAIR + j, j, p)
                    c.base, c.n = (K_DVE * NPAIR + 1) * p + K_DVE * NPAIR + n0, 0
                    c(dve.tensor_scalar(rk, rk, -float(CAP), None, ALU.add))
                add_y(nn * NPAIR)

        yrow = lambda t: work[rows(t), D * t:D * (t + 1)]
        s_yout = sem("y_stored")
        final = Norm(2, yrow, lambda e: e.wait_ge(s_wb, 48), False)
        with nc.Block() as block:
            @block.scalar
            def _(act):
                final.scalar(act)

            @block.vector
            def _(dve):
                final.vector(dve)

            @block.sync
            def _(sp):
                for t in range(2):
                    sp.wait_ge(s_nrow, final.base + t + 1)
                    sp.dma_start(y_prompt[0, toks(t), :], yrow(t)).then_inc(s_yout, 16)
                sp.wait_ge(s_nrow, final.base + 3)
                sp.dma_start(y_sample.rearrange("s i d -> (s i) d"), yrow(2)).then_inc(s_yout, 16)
                sp.wait_ge(s_yout, 48)


_INS = ['x_prompt', 'x_sample', 'cache_k', 'cache_v', 'page_table', 'state_conv', 'state_ssm', 'norm_mix', 'w_in', 'conv_w',
        'a_log', 'dt_bias', 'gdn_norm', 'sb_bias', 'w_out', 'norm_ffn', 'router_w', 'router_b', 'w_up', 'b_up', 'w_down',
        'b_down', 'norm_final']
_OUTS = [(1, SEQ, D), (NSEQ, NDEC, D), (1, 1, SEQ, NH, HD), (1, 1, SEQ, NH, HD), (1, 1, CONV - 1, CONVD),
         (1, 1, NH, HD, HD), (1, NSEQ, NDEC, NH, HD), (1, NSEQ, NDEC, NH, HD), (1, NSEQ, CONV - 1, CONVD),
         (1, NSEQ, NH, HD, HD)]


def kernel(**inputs):
    import concourse.bacc as bacc
    from concourse.bass_utils import run_bass_kernel_spmd

    nc = bacc.Bacc("TRN2", target_bir_lowering=False, num_devices=1)
    arrays, args = {}, []
    for name in _INS:
        a = np.ascontiguousarray(inputs[name])
        arrays[f"in_{name}"] = a
        args.append(nc.dram_tensor(f"in_{name}", a.shape, mybir.dt.from_np(a.dtype), kind="ExternalInput").ap())
    for i, shape in enumerate(_OUTS):
        args.append(nc.dram_tensor(f"out_{i}", shape, F32, kind="ExternalOutput").ap())
    build(nc, *args)
    r = run_bass_kernel_spmd(nc, [arrays], core_ids=[0])
    return tuple(r.results[0][f"out_{i}"] for i in range(len(_OUTS)))
```
